# Optimizing a Trainium2 kernel written in Bass

```python
import math
import jax, jax.numpy as jnp
from jax import lax
import numpy as np

D_MODEL = 1024
BATCH = 1
SEQ = 256
DEPTH = 1
DEC_BATCH = 8
DEC_SEQ = 4
PAST_LEN = 2048
PAGE_SIZE = 128

ML_H = 4
ML_DK = 128
ML_DV = 128
ML_W = ML_H * ML_DV
MLSTM_CHUNK = 64
GD_H = 4
GD_DK = 128
GD_DV = 128
GD_W = GD_H * GD_DV
GD_CONV_CH = 2 * GD_H * GD_DK + GD_W
CONV_W = 4
GDN_CHUNK = 64
XA_H = 4
XA_DH = 128
XA_W = XA_H * XA_DH
MEM_LEN = 256
N_GROUPS = 4
EXPERTS_PER_GROUP = 4
N_EXPERTS = N_GROUPS * EXPERTS_PER_GROUP
TOP_K_IN_GROUP = 2
D_EXPERT = 512
EPS = 1e-6

IN_SIZES = (ML_H * ML_DK, ML_H * ML_DK, ML_W, ML_H, ML_H, ML_W,
            GD_CONV_CH, GD_H, GD_H, GD_W,
            XA_W,
            D_MODEL, D_MODEL, D_MODEL)
N_IN = sum(IN_SIZES)

kernel_name = 'hybrid_mlstm_gdn_memxattn_hmoe_step'

def rmsnorm(x, g):
    xf = x.astype(jnp.float32)
    y = xf * lax.rsqrt(jnp.mean(xf * xf, axis=-1, keepdims=True) + EPS)
    return (y * g.astype(jnp.float32)).astype(x.dtype)

def head_rmsnorm(h, g):
    return h * lax.rsqrt(jnp.mean(h * h, axis=-1, keepdims=True) + EPS) * g

def l2norm(x):
    return x * lax.rsqrt(jnp.sum(x * x, axis=-1, keepdims=True) + EPS)

def mlstm_chunked(q, k, v, i_pre, log_f, C0, n0, m0):
    B, S, H, DK = q.shape
    L = math.gcd(S, MLSTM_CHUNK)
    nc = S // L

    def to_chunks(t):
        return jnp.moveaxis(t.reshape((B, nc, L) + t.shape[2:]), 1, 0)

    causal = jnp.tril(jnp.ones((L, L), dtype=bool))

    def step(carry, inp):
        C, n, m = carry
        qc, kc, vc, ic, fc = inp
        bt = jnp.swapaxes(jnp.cumsum(fc, axis=1), 1, 2)
        it = jnp.swapaxes(ic, 1, 2)
        log_d = bt[..., :, None] - bt[..., None, :] + it[..., None, :]
        log_d = jnp.where(causal, log_d, -jnp.inf)
        inter = bt + m[..., None]
        m_t = jnp.maximum(inter, jnp.max(log_d, axis=-1))
        d = jnp.exp(log_d - m_t[..., None])
        inter_w = jnp.exp(inter - m_t)
        s = jnp.einsum('blhd,bshd->bhls', qc, kc) * d
        num = (jnp.einsum('bhls,bshv->blhv', s, vc)
               + jnp.einsum('blhd,bhdv->blhv', qc, C) * jnp.swapaxes(inter_w, 1, 2)[..., None])
        den = jnp.sum(s, axis=-1) + inter_w * jnp.einsum('blhd,bhd->bhl', qc, n)
        denom = jnp.maximum(jnp.abs(den), jnp.exp(-m_t))
        h = num / jnp.swapaxes(denom, 1, 2)[..., None]
        m_new = m_t[..., -1]
        w = jnp.exp(bt[..., -1:] - bt + it - m_new[..., None])
        decay = jnp.exp(bt[..., -1] + m - m_new)
        kw = kc * jnp.swapaxes(w, 1, 2)[..., None]
        C_new = decay[..., None, None] * C + jnp.einsum('bshd,bshv->bhdv', kw, vc)
        n_new = decay[..., None] * n + jnp.sum(kw, axis=1)
        return (C_new, n_new, m_new), h

    xs = (to_chunks(q), to_chunks(k), to_chunks(v), to_chunks(i_pre), to_chunks(log_f))
    (C1, n1, m1), hs = lax.scan(step, (C0, n0, m0), xs)
    h = jnp.moveaxis(hs, 0, 1).reshape(B, S, H, v.shape[-1])
    return h, C1, n1, m1

def gated_delta_chunked(q, k, v, g, beta, S0):
    B, S, H, DK = q.shape
    DV = v.shape[-1]
    L = math.gcd(S, GDN_CHUNK)
    nc = S // L

    def heads_chunks(t):
        t = t.reshape((B, nc, L) + t.shape[2:])
        return jnp.moveaxis(jnp.moveaxis(t, 3, 2), 1, 0)

    qc, kc, vc, gc, bc = map(heads_chunks, (q, k, v, g, beta))
    gam = jnp.cumsum(gc, axis=-1)
    incl = jnp.tril(jnp.ones((L, L), dtype=bool))
    strict = jnp.tril(jnp.ones((L, L), dtype=bool), -1)
    diff = gam[..., :, None] - gam[..., None, :]
    decay_mat = jnp.where(incl, jnp.exp(jnp.where(incl, diff, 0.0)), 0.0)
    kk = jnp.einsum('...ld,...sd->...ls', kc, kc)
    a_mat = jnp.where(strict, bc[..., :, None] * kk * decay_mat, 0.0)
    rhs = jnp.concatenate([bc[..., None] * vc, bc[..., None] * kc * jnp.exp(gam)[..., None]], axis=-1)
    sol = lax.linalg.triangular_solve(a_mat + jnp.eye(L, dtype=a_mat.dtype), rhs,
                                      left_side=True, lower=True, unit_diagonal=True)
    u, w = sol[..., :DV], sol[..., DV:]
    qk = jnp.einsum('...ld,...sd->...ls', qc, kc) * decay_mat
    q_dec = qc * jnp.exp(gam)[..., None]
    k_dec = kc * jnp.exp(gam[..., -1:] - gam)[..., None]
    g_last = jnp.exp(gam[..., -1])

    def step(Sm, inp):
        u_c, w_c, qk_c, qd_c, kd_c, gl_c = inp
        v_new = u_c - jnp.einsum('bhld,bhdv->bhlv', w_c, Sm)
        o = jnp.einsum('bhld,bhdv->bhlv', qd_c, Sm) + jnp.einsum('bhls,bhsv->bhlv', qk_c, v_new)
        Sm = gl_c[..., None, None] * Sm + jnp.einsum('bhld,bhlv->bhdv', kd_c, v_new)
        return Sm, o

    S1, o = lax.scan(step, S0, (u, w, qk, q_dec, k_dec, g_last))
    o = jnp.moveaxis(jnp.moveaxis(o, 0, 1), 2, 3).reshape(B, S, H, DV)
    return o, S1

def memory_kv(mem, mem_norm, w_mem_kv):
    B, M, _ = mem.shape
    kv = rmsnorm(mem, mem_norm) @ w_mem_kv
    k, v = jnp.split(kv, 2, axis=-1)
    return k.reshape(B, M, XA_H, XA_DH), v.reshape(B, M, XA_H, XA_DH)

def memory_attention(q, mk, mv):
    s = jnp.einsum('bshd,bmhd->bhsm', q.astype(jnp.float32), mk.astype(jnp.float32)) * (XA_DH ** -0.5)
    p = jax.nn.softmax(s, axis=-1)
    return jnp.einsum('bhsm,bmhd->bshd', p, mv.astype(jnp.float32))

def hier_moe(h, w_router_group, b_router_group, w_router_expert, b_router_expert,
             w_exp_gate, w_exp_up, w_exp_down):
    f32 = jnp.float32
    B, S, D = h.shape
    t = h.reshape(-1, D)
    lg = (t @ w_router_group).astype(f32) + b_router_group.astype(f32)
    pg = jax.nn.softmax(lg, axis=-1)
    _, gi = lax.top_k(lg, 1)
    grp_1h = jax.nn.one_hot(gi[:, 0], N_GROUPS, dtype=f32)
    p_grp = jnp.sum(pg * grp_1h, axis=-1)
    le = ((t @ w_router_expert).astype(f32) + b_router_expert.astype(f32)).reshape(-1, N_GROUPS, EXPERTS_PER_GROUP)
    le_sel = jnp.sum(le * grp_1h[:, :, None], axis=1)
    top_v, top_i = lax.top_k(le_sel, TOP_K_IN_GROUP)
    w_top = jax.nn.softmax(top_v, axis=-1)
    within = jnp.sum(w_top[..., None] * jax.nn.one_hot(top_i, EXPERTS_PER_GROUP, dtype=f32), axis=1)
    comb = (p_grp[:, None, None] * grp_1h[:, :, None] * within[:, None, :]).astype(t.dtype)
    out = jnp.zeros_like(t)
    for gidx in range(N_GROUPS):
        e0 = gidx * EXPERTS_PER_GROUP
        e1 = e0 + EXPERTS_PER_GROUP
        a = jnp.einsum('td,edf->tef', t, w_exp_gate[e0:e1])
        u = jnp.einsum('td,edf->tef', t, w_exp_up[e0:e1])
        act = jax.nn.silu(a) * u * comb[:, gidx, :, None]
        out = out + jnp.einsum('tef,efd->td', act, w_exp_down[e0:e1])
    return out.reshape(B, S, D)

def decoder_layer(x, mem_k, mem_v, C0, n0, m0, S0, conv0,
                  norm_mix, w_in, b_igate, b_fgate, mlstm_norm, conv_w, a_log, dt_bias, gdn_norm,
                  w_br_mlstm, w_br_gdn, w_br_xattn, w_out, norm_ffn,
                  w_router_group, b_router_group, w_router_expert, b_router_expert,
                  w_exp_gate, w_exp_up, w_exp_down):
    f32 = jnp.float32
    B, S, _ = x.shape
    h = rmsnorm(x, norm_mix)
    points = np.cumsum(IN_SIZES)[:-1].tolist()
    (m_q, m_k, m_v, m_i, m_f, m_o, g_qkv, g_a, g_b, g_out, x_q,
     gate_a, gate_b, gate_c) = jnp.split(h @ w_in, points, axis=-1)

    q = m_q.reshape(B, S, ML_H, ML_DK).astype(f32)
    k = m_k.reshape(B, S, ML_H, ML_DK).astype(f32) * (ML_DK ** -0.5)
    v = m_v.reshape(B, S, ML_H, ML_DV).astype(f32)
    i_pre = m_i.astype(f32) + b_igate.astype(f32)
    log_f = jax.nn.log_sigmoid(m_f.astype(f32) + b_fgate.astype(f32))
    h_a, C1, n1, m1 = mlstm_chunked(q, k, v, i_pre, log_f, C0.astype(f32), n0.astype(f32), m0.astype(f32))
    h_a = head_rmsnorm(h_a, mlstm_norm.reshape(ML_H, ML_DV).astype(f32)) * jax.nn.sigmoid(m_o.reshape(B, S, ML_H, ML_DV).astype(f32))
    h_a = h_a.reshape(B, S, ML_W).astype(x.dtype)

    conv_in = jnp.concatenate([conv0.astype(x.dtype), g_qkv], axis=1)
    acc = conv_in[:, 0:S] * conv_w[0]
    for j in range(1, CONV_W):
        acc = acc + conv_in[:, j:j + S] * conv_w[j]
    conv_out = jax.nn.silu(acc.astype(f32))
    conv1 = conv_in[:, S:]
    gq, gk, gv = jnp.split(conv_out, [GD_H * GD_DK, 2 * GD_H * GD_DK], axis=-1)
    gq = l2norm(gq.reshape(B, S, GD_H, GD_DK)) * (GD_DK ** -0.5)
    gk = l2norm(gk.reshape(B, S, GD_H, GD_DK))
    gv = gv.reshape(B, S, GD_H, GD_DV)
    g = -jnp.exp(a_log.astype(f32)) * jax.nn.softplus(g_a.astype(f32) + dt_bias.astype(f32))
    beta = jax.nn.sigmoid(g_b.astype(f32))
    h_b, S1 = gated_delta_chunked(gq, gk, gv, g, beta, S0.astype(f32))
    h_b = head_rmsnorm(h_b, gdn_norm.astype(f32)) * jax.nn.silu(g_out.reshape(B, S, GD_H, GD_DV).astype(f32))
    h_b = h_b.reshape(B, S, GD_W).astype(x.dtype)

    h_c = memory_attention(x_q.reshape(B, S, XA_H, XA_DH), mem_k, mem_v).reshape(B, S, XA_W).astype(x.dtype)

    mixed = (jax.nn.sigmoid(gate_a) * (h_a @ w_br_mlstm)
             + jax.nn.sigmoid(gate_b) * (h_b @ w_br_gdn)
             + jax.nn.sigmoid(gate_c) * (h_c @ w_br_xattn))
    x = x + mixed @ w_out

    x = x + hier_moe(rmsnorm(x, norm_ffn), w_router_group, b_router_group, w_router_expert,
                     b_router_expert, w_exp_gate, w_exp_up, w_exp_down)
    dt = x.dtype
    return x, C1.astype(dt), n1.astype(dt), m1.astype(dt), S1.astype(dt), conv1.astype(dt)

def setup_inputs(seed: int = 0) -> dict:
    key = jax.random.key(seed)
    ks = iter(jax.random.split(key, 48))
    f32 = jnp.float32
    D = D_MODEL

    def nrm(shape, scale=1.0):
        return jax.random.normal(next(ks), shape, f32) * scale

    def gain(shape):
        return 1.0 + nrm(shape, 0.02)

    x_prompt = nrm((BATCH, SEQ, D))
    x_sample = nrm((DEC_BATCH, DEC_SEQ, D))
    mem_prompt = nrm((BATCH, MEM_LEN, D))
    cache_mem_k = nrm((DEPTH, DEC_BATCH, MEM_LEN, XA_H, XA_DH))
    cache_mem_v = nrm((DEPTH, DEC_BATCH, MEM_LEN, XA_H, XA_DH))
    state_mlstm_C = nrm((DEPTH, DEC_BATCH, ML_H, ML_DK, ML_DV), 0.5)
    state_mlstm_n = nrm((DEPTH, DEC_BATCH, ML_H, ML_DK))
    state_mlstm_m = nrm((DEPTH, DEC_BATCH, ML_H))
    state_gdn_S = nrm((DEPTH, DEC_BATCH, GD_H, GD_DK, GD_DV), 0.1)
    state_gdn_conv = nrm((DEPTH, DEC_BATCH, CONV_W - 1, GD_CONV_CH))

    norm_mix = gain((DEPTH, D))
    w_in = nrm((DEPTH, D, N_IN), D ** -0.5)
    b_igate = nrm((DEPTH, ML_H), 0.5)
    b_fgate = 3.0 + jnp.linspace(0.0, 3.0, ML_H, dtype=f32)[None, :] + nrm((DEPTH, ML_H), 0.1)
    mlstm_norm = gain((DEPTH, ML_W))
    conv_w = nrm((DEPTH, CONV_W, GD_CONV_CH), CONV_W ** -0.5)
    a_log = jnp.log(jax.random.uniform(next(ks), (DEPTH, GD_H), f32, 1.0, 16.0))
    dt0 = jnp.exp(jax.random.uniform(next(ks), (DEPTH, GD_H), f32, math.log(1e-3), math.log(1e-1)))
    dt_bias = jnp.log(jnp.expm1(dt0))
    gdn_norm = gain((DEPTH, GD_DV))
    mem_norm = gain((DEPTH, D))
    w_mem_kv = nrm((DEPTH, D, 2 * XA_W), D ** -0.5)
    w_br_mlstm = nrm((DEPTH, ML_W, D), ML_W ** -0.5)
    w_br_gdn = nrm((DEPTH, GD_W, D), GD_W ** -0.5)
    w_br_xattn = nrm((DEPTH, XA_W, D), XA_W ** -0.5)
    w_out = nrm((DEPTH, D, D), D ** -0.5)
    norm_ffn = gain((DEPTH, D))
    w_router_group = nrm((DEPTH, D, N_GROUPS), D ** -0.5)
    b_router_group = nrm((DEPTH, N_GROUPS), 0.01)
    w_router_expert = nrm((DEPTH, D, N_EXPERTS), D ** -0.5)
    b_router_expert = nrm((DEPTH, N_EXPERTS), 0.01)
    w_exp_gate = nrm((DEPTH, N_EXPERTS, D, D_EXPERT), D ** -0.5)
    w_exp_up = nrm((DEPTH, N_EXPERTS, D, D_EXPERT), D ** -0.5)
    w_exp_down = nrm((DEPTH, N_EXPERTS, D_EXPERT, D), D_EXPERT ** -0.5)
    final_norm = gain((D,))
    return {
        'x_prompt': x_prompt, 'x_sample': x_sample, 'mem_prompt': mem_prompt,
        'cache_mem_k': cache_mem_k, 'cache_mem_v': cache_mem_v,
        'state_mlstm_C': state_mlstm_C, 'state_mlstm_n': state_mlstm_n, 'state_mlstm_m': state_mlstm_m,
        'state_gdn_S': state_gdn_S, 'state_gdn_conv': state_gdn_conv,
        'norm_mix': norm_mix, 'w_in': w_in, 'b_igate': b_igate, 'b_fgate': b_fgate,
        'mlstm_norm': mlstm_norm, 'conv_w': conv_w, 'a_log': a_log, 'dt_bias': dt_bias,
        'gdn_norm': gdn_norm, 'mem_norm': mem_norm, 'w_mem_kv': w_mem_kv,
        'w_br_mlstm': w_br_mlstm, 'w_br_gdn': w_br_gdn, 'w_br_xattn': w_br_xattn,
        'w_out': w_out, 'norm_ffn': norm_ffn,
        'w_router_group': w_router_group, 'b_router_group': b_router_group,
        'w_router_expert': w_router_expert, 'b_router_expert': b_router_expert,
        'w_exp_gate': w_exp_gate, 'w_exp_up': w_exp_up, 'w_exp_down': w_exp_down,
        'final_norm': final_norm,
    }

def reference(x_prompt, x_sample, mem_prompt, cache_mem_k, cache_mem_v,
              state_mlstm_C, state_mlstm_n, state_mlstm_m, state_gdn_S, state_gdn_conv,
              norm_mix, w_in, b_igate, b_fgate, mlstm_norm, conv_w, a_log, dt_bias, gdn_norm,
              mem_norm, w_mem_kv, w_br_mlstm, w_br_gdn, w_br_xattn, w_out, norm_ffn,
              w_router_group, b_router_group, w_router_expert, b_router_expert,
              w_exp_gate, w_exp_up, w_exp_down, final_norm):
    f32 = jnp.float32
    dt = x_prompt.dtype
    bp = x_prompt.shape[0]
    xp, xs = x_prompt, x_sample
    mk_l, mv_l = [], []
    cp_l, np_l, mp_l, sp_l, vp_l = [], [], [], [], []
    cs_l, ns_l, ms_l, ss_l, vs_l = [], [], [], [], []
    for l in range(DEPTH):
        lw = (norm_mix[l], w_in[l], b_igate[l], b_fgate[l], mlstm_norm[l], conv_w[l], a_log[l],
              dt_bias[l], gdn_norm[l], w_br_mlstm[l], w_br_gdn[l], w_br_xattn[l], w_out[l],
              norm_ffn[l], w_router_group[l], b_router_group[l], w_router_expert[l],
              b_router_expert[l], w_exp_gate[l], w_exp_up[l], w_exp_down[l])
        mk_p, mv_p = memory_kv(mem_prompt, mem_norm[l], w_mem_kv[l])
        xp, c_p, n_p, m_p, s_p, v_p = decoder_layer(
            xp, mk_p, mv_p,
            jnp.zeros((bp, ML_H, ML_DK, ML_DV), f32), jnp.zeros((bp, ML_H, ML_DK), f32),
            jnp.zeros((bp, ML_H), f32), jnp.zeros((bp, GD_H, GD_DK, GD_DV), f32),
            jnp.zeros((bp, CONV_W - 1, GD_CONV_CH), dt), *lw)
        xs, c_s, n_s, m_s, s_s, v_s = decoder_layer(
            xs, cache_mem_k[l], cache_mem_v[l], state_mlstm_C[l], state_mlstm_n[l],
            state_mlstm_m[l], state_gdn_S[l], state_gdn_conv[l], *lw)
        mk_l.append(mk_p.astype(dt)); mv_l.append(mv_p.astype(dt))
        cp_l.append(c_p); np_l.append(n_p); mp_l.append(m_p); sp_l.append(s_p); vp_l.append(v_p)
        cs_l.append(c_s); ns_l.append(n_s); ms_l.append(m_s); ss_l.append(s_s); vs_l.append(v_s)
    y_prompt = rmsnorm(xp, final_norm)
    y_sample = rmsnorm(xs, final_norm)
    return (y_prompt, y_sample,
            jnp.stack(mk_l), jnp.stack(mv_l),
            jnp.stack(cp_l), jnp.stack(np_l), jnp.stack(mp_l), jnp.stack(sp_l), jnp.stack(vp_l),
            jnp.stack(cs_l), jnp.stack(ns_l), jnp.stack(ms_l), jnp.stack(ss_l), jnp.stack(vs_l))


_drawn_inputs = setup_inputs


def setup_inputs(seed=0):
    import zlib

    import numpy as np

    out = dict(_drawn_inputs(seed))
    spreads = {}
    factors = {'mlstm_norm': 55.705,
     'mem_norm': 8.008,
     'b_router_group': 65.633,
     'b_router_expert': 158.443,
     'final_norm': 22.861,
     'gdn_norm': 52.884,
     'cache_mem_k': 7.316,
     'cache_mem_v': 5.693,
     'norm_ffn': 8.0}
    for name, (base, spread) in spreads.items():
        noise = np.random.default_rng([zlib.crc32(name.encode()), seed]).standard_normal(out[name].shape)
        drawn = base * np.exp(spread * noise) if base else spread * noise
        out[name] = __import__('jax').numpy.asarray(drawn.astype(out[name].dtype))
    for name, factor in factors.items():
        out[name] = (out[name] * factor).astype(out[name].dtype)
    return out
```

```python
from contextlib import ExitStack

import numpy as np
import concourse.bass as bass
from concourse import mybir

F32 = mybir.dt.float32
I32 = mybir.dt.int32
ALU = mybir.AluOpType
ACT = mybir.ActivationFunctionType
AX = mybir.AxisListType

D = 1024
KD = D // 128
SEQ, NB, DS = 256, 8, 4
NS = NB * DS
T = SEQ + NS
TILES = [(0, 128), (128, 128), (SEQ, NS)]
H, DH = 4, 128
W = H * DH
DA = DH + 1
L = 64
NCH = SEQ // L + NB
CW = 4
CCH = 3 * W
NCT = CCH // 128
HIST = CW - 1
MEM = 256
G, EG = 4, 4
E = G * EG
FE = 512
SLOTS = 64
EPS = 1e-6
NEG = -1e30
RING, UNIT = 6, 4096
NSCRAP = 40
ARENA, SMALL = 19040, 1600
QSCALE = DH ** -0.5
PASSES = -(-T // SLOTS)
LEVELS = 6

O_Q, O_K, O_V = 0, W, 2 * W
O_IF = 3 * W
O_MO = O_IF + 2 * H
O_GQKV = O_MO + W
O_GAB = O_GQKV + CCH
O_GOUT = O_GAB + 2 * H
O_XQ = O_GOUT + W
O_GATE = O_XQ + W

C_ID, C_NEGP, C_NEGS, C_LVL = 0, 128, 256, 288
C_SEL = C_LVL + LEVELS * 128
C_BROW = C_SEL + H * 128
C_BCOL = C_BROW + NB * NS
C_IOTA = C_BCOL + NB
C_TRI = C_IOTA + SLOTS
C_FIRST = C_TRI + 128
C_N = C_FIRST + 3 * EG
C_RST = C_N
C_ALL = C_RST + T


def constants():
    t = np.zeros((128, C_ALL), np.float32)
    s, l = np.arange(128)[:, None], np.arange(128)[None, :]
    t[:, C_ID:C_ID + 128] = s == l
    t[:, C_NEGP:C_NEGP + 128] = np.where((s // L == l // L) & (s <= l), 0, NEG)
    t[:NS, C_NEGS:C_NEGS + NS] = np.where((s // DS == l // DS) & (s <= l), 0, NEG)[:NS, :NS]
    for k in range(LEVELS):
        n = 1 << k
        t[:, C_LVL + 128 * k:C_LVL + 128 * (k + 1)] = (s // n + 1 == l // n) & (l // n % 2 == 1)
    for h in range(H):
        t[h, C_SEL + 128 * h:C_SEL + 128 * (h + 1)] = 1
    for b in range(NB):
        t[:, C_BROW + NS * b:C_BROW + NS * (b + 1)] = np.arange(NS) // DS == b
        t[:NS, C_BCOL + b] = np.arange(NS) // DS == b
    t[:, C_IOTA:C_IOTA + SLOTS] = np.arange(SLOTS)
    t[:, C_TRI:C_TRI + 128] = s < l
    n = np.arange(T)
    t[:, C_RST:C_RST + T] = np.where(n < SEQ, n % L != 0, n % DS != 0)
    t[:, C_FIRST:C_FIRST + 3 * EG] = np.arange(3 * EG) % EG != 0
    return t


def bc(ap, *shape):
    return ap.to_broadcast(list(shape))


def build(nc, a, out):
    ctx = ExitStack()

    def sb(name, *shape):
        return ctx.enter_context(nc.sbuf_tensor(name, list(shape), F32))

    def sem(name):
        return ctx.enter_context(nc.semaphore(name))

    ring = sb("ring", 128, RING, UNIT)
    cst = sb("cst", 128, C_N)
    ones = sb("ones", 128, 128)
    hT = sb("hT", 128, KD, T)
    brT = [sb(f"brT{j}", 128, H, T) for j in range(3)]
    small = sb("small", 128, SMALL)
    arena = sb("arena", 128, ARENA)
    flag = ctx.enter_context(nc.sbuf_tensor("flag", [1, 1], I32))
    PS = ctx.enter_context(nc.psum_tensor("PS", [128, 8, 512], F32))

    ident = cst[:, C_ID:C_ID + 128]
    at = [0]

    def tiny(*shape):
        n = int(np.prod(shape[1:]))
        v = small[0:shape[0], at[0]:at[0] + n]
        at[0] += n
        assert at[0] <= SMALL
        if len(shape) == 3:
            v = v.rearrange("p (a b) -> p a b", b=shape[2])
        if len(shape) == 4:
            v = v.rearrange("p (a b c) -> p a b c", b=shape[2], c=shape[3])
        return v

    def place(start, *shape):
        n = int(np.prod(shape[1:]))
        assert start + n <= ARENA, (start, shape)
        v = arena[0:shape[0], start:start + n]
        if len(shape) == 3:
            v = v.rearrange("p (a b) -> p a b", b=shape[2])
        if len(shape) == 4:
            v = v.rearrange("p (a b c) -> p a b c", b=shape[2], c=shape[3])
        return v, start + n

    NV = 2 * KD + H + 1 + NB * H
    vecT = tiny(128, NV)
    tailT = tiny(128, NCT, HIST * (NB + 1))
    V_MIX, V_MEM, V_ML, V_GD, V_N0 = 0, KD, 2 * KD, 2 * KD + H, 2 * KD + H + 1
    cwT = tiny(128, NCT, NB * HIST + CW)
    ss = tiny(128, 5)
    rstd = tiny(128, 5)
    gffn = tiny(128, KD)
    bias4 = tiny(H, 5)
    brt = tiny(20, 1)
    m0 = tiny(H, NB)
    dec = tiny(128, H, NCH)
    gl = tiny(128, H, NCH)
    cols = tiny(128, 3, 8, H)
    hs4 = tiny(128, 12, H)
    nst = tiny(128, NB * H + H)
    rst = tiny(128, 3)
    negmax = tiny(128, H)
    psumx = tiny(128, H)
    COL_RS, COL_W, COL_IW, COL_EN, COL_G, COL_B, COL_EG, COL_KD = range(8)

    full = [sem(f"full{b}") for b in range(8)]
    free = [sem(f"free{b}") for b in range(8)]
    ring_full = [sem(f"ring_full{s}") for s in range(RING)]
    ring_used = sem("ring_used")
    uses, count = {}, [0] * 8

    def filled(name):
        b, n = uses[name]
        return full[b], n + 1

    def bank_of(name):
        return PS[:, uses[name][0], :]

    def freed(name):
        return free[uses[name][0]]

    dve_step, act_step, pool_step = sem("dve_step"), sem("act_step"), sem("pool_step")
    steps = {"dve": 0, "act": 0, "pool": 0}

    def dstep(ins):
        steps["dve"] += 1
        ins.then_inc(dve_step, 1)
        nc.vector.wait_ge(dve_step, steps["dve"])

    def astep(ins):
        steps["act"] += 1
        ins.then_inc(act_step, 1)
        nc.scalar.wait_ge(act_step, steps["act"])


    S = {}

    def sg(name):
        if name not in S:
            S[name] = sem(name)
        return S[name]

    def taken(name):
        b, n = uses[name]
        return free[b], n + 1

    def lv(t, k):
        return LEVELS * t + k

    KT, p = place(0, 128, H, MEM)
    memv, p = place(p, 128, 2, W)
    A0 = p
    xin, p = place(5828, 128, 5, D)
    memT, p = place(p, 128, KD, MEM)
    junk, p = place(p, 128, D)
    wg, p = place(p, 128, KD, 16)
    vrow, p = place(p, NV, 128)
    crow, p = place(p, NB * HIST + CW, CCH)
    memk, p = place(p, 128, 2, W)
    cin, p = place(A0, 128, NCT, HIST + SEQ)
    cis, p = place(p, 128, NCT, NB * (HIST + DS))
    q_t, p = place(p, 128, 3, W)
    k_t, p = place(p, 128, 3, W)
    v_a, p = place(p, 128, 3, H * DA)
    mo, p = place(p, 128, 3, W)
    gout, p = place(p, 128, 3, W)
    M0 = p
    qTt, p = place(p, 128, W)
    kTt, p = place(p, 128, W)
    qwTt, p = place(p, 128, W)
    dT, p = place(p, 128, W)
    sT, p = place(p, 128, W)
    num, p = place(p, 128, W)
    Cp, p = place(p, 128, H, DA)
    Cs0, p = place(p, 128, NB, DA)
    qwm, p = place(p, 128, NB, NS)
    sform, p = place(p, 128, 5, H * NS)
    nrow = sform[0:NB * H + H, 4, :]
    rset, _ = place(p - 640, H, T)
    Cs1, _ = place(M0, 128, NB, DA)
    Cs = [Cs0, Cs1]
    vblk, _ = place(A0 + 3780, NS, NB, DA)
    cvT, p = place(A0 + 3780, 128, NCT, T)
    stmp, _ = place(p, 128, 2, 4 * T)
    kT, p = place(p, 128, W)
    qT, p = place(p, 128, W)
    qdT, p = place(p, 128, W)
    kbT, p = place(p, 128, W)
    QKT, p = place(p, 128, W)
    assert p <= A0 + 3780 + 4 * 1536 + 12
    raw, p = place(A0, 128, 3, W)
    kb, p = place(p, 128, W)
    kbg, p = place(p, 128, W)
    kd, p = place(p, 128, W)
    qd, p = place(p, 128, W)
    dG, p = place(M0, 128, W)
    AT, p = place(p, 128, W)
    Tm, p = place(p, 128, W)
    Um, p = place(p, 128, W)
    Xm, p = place(p, 128, W)
    vn, p = place(p, 128, W)
    Sp, p = place(p, 128, W)
    Ss0, p = place(p, 128, NB, DH)
    qdm, p = place(p, 128, NB, NS)
    nwm, p = place(p, 128, NB, NS)
    Ss1, _ = place(A0 + 3780, 128, NB, DH)
    Ss = [Ss0, Ss1]
    vnb, _ = place(A0, NS, NB, DH)
    tails, _ = place(M0, HIST * (NB + 1), CCH)
    xq, p = place(A0, 128, 3, W)
    xqT, p = place(p, 128, H, T)
    pr, p = place(p, 128, H, MEM)
    prT, p = place(p, 128, 2, W)
    Kb = [None, None]
    Vb = [None, None]
    KTb = [None, None]
    for j in range(2):
        Kb[j], p = place(p, 128, 2, W)
        Vb[j], p = place(p, 128, 2, W)
        KTb[j], p = place(p, 128, H, MEM)
    qm, p = place(p, 128, H, NB * NS)
    spT, p = place(p, 128, 2, H * NS)
    X1 = p
    mixed, p = place(0, 128, 3, D)
    mixs = mixed[:, 2, 0:256].rearrange("p (a b) -> p a b", a=2)
    mixT, p = place(p, 128, KD, T)
    sig, p = place(p, 128, 2, W)
    x2, p = place(ARENA - 3 * D, 128, 3, D)
    assert X1 <= ARENA - 3 * D
    h2p, p = place(0, 128, 3, D)
    h2T, p = place(p, 128, KD, T)
    Pm, p = place(p, 128, 3, E * SLOTS)
    Pw, p = place(p, 128, 3, E * SLOTS)
    PwT, p = place(p, 128, E // 2, T)
    hg, p = place(p, 128, KD, 4 * SLOTS)
    assert p <= ARENA - 3 * D
    gfin = hT[:, :, :].rearrange("p a b -> p (a b)")[:, 0:D]
    outp, p = place(3 * D, 128, D)
    ea, p = place(p, 128, 2, 256)
    actb, p = place(p, 128, 2, 256)
    actT = [brT[0][:, :, :].rearrange("p a b -> p (a b)")[:, 256 * j:256 * j + 256] for j in range(2)]
    pws = [brT[1][:, :, :].rearrange("p a b -> p (a b)")[:, T * j:T * j + T] for j in range(2)]
    LG = tiny(128, 3, 20)
    oh = tiny(128, 3, 4)
    oh1 = tiny(128, 3, 4)
    oh2 = tiny(128, 3, 4)
    rtmp = tiny(128, 3, 4)
    rt1 = tiny(128, 12, 3)
    msk = tiny(128, 3, E)
    cmb = tiny(128, 3, E)
    rkm = tiny(128, 3, E)
    le4 = tiny(128, 3, E)
    wr = tiny(128, KD, 20)
    scrap = tiny(1, NSCRAP)
    oh3 = tiny(128, 3, 4)
    le12 = tiny(128, 12)
    lgT = sig[:, 0, 0:T]
    R0, R1, R2 = (brT[j][0:H] for j in range(3))
    ROW_I, ROW_F, ROW_A, ROW_B = (R0[:, j, :] for j in range(4))
    ROW_Z, ROW_E = R1[:, 0:2, :], R1[:, 2:4, :]
    ROW_RS, ROW_W, ROW_IW, ROW_EN = (R1[:, j, :] for j in range(4))
    ROW_M, ROW_BC, ROW_G, ROW_KD = (R2[:, j, :] for j in range(4))
    ROW_RL, ROW_EG = ROW_BC, ROW_A

    def forms(t):
        if t < 2:
            return qTt, kTt, qwTt, dT, sT
        return [sform[:, j, :] for j in range(5)]

    w_in = a["w_in"][0]

    def cols_of(w, c):
        return w[:, c:c + 512].rearrange("(c p) n -> p c n", p=128)

    units = []
    units.append(("kvK", cols_of(a["w_mem_kv"][0], 0)))
    units.append(("kvV", cols_of(a["w_mem_kv"][0], W)))
    for name, o in (("q", O_Q), ("k", O_K), ("v", O_V), ("mo", O_MO), ("g0", O_GQKV), ("g1", O_GQKV + W),
                    ("g2", O_GQKV + 2 * W), ("gout", O_GOUT), ("xq", O_XQ)):
        units.append((name, cols_of(w_in, o)))
    for j, w in enumerate(("w_br_mlstm", "w_br_gdn", "w_br_xattn")):
        units.append((("br", j), a[w][0].rearrange("(c p) n -> p c n", p=128)))
        for n in range(2):
            units.append((("gate", j, n), cols_of(w_in, O_GATE + j * D + n * 512)))
    for n in range(2):
        units.append((("out", n), cols_of(a["w_out"][0], n * 512)))
    NU = len(units)
    unit_no = {name: n for n, (name, _) in enumerate(units)}
    unit_last = {}

    def unit_ready(name):
        n = unit_no[name]
        return ring_full[n % RING], 16 * (n // RING + 1)

    def unit(name):
        return ring[:, unit_no[name] % RING, :]

    GROUP = [("hg", j, 4 + j) for j in range(4)]
    for pr_ in range(2):
        e0, e1 = 2 * pr_, 2 * pr_ + 1
        GROUP += [("gu", e0, 0), ("gu", e1, 1), ("aT", e0, 2), ("aT", e1, 2)]
        GROUP += [("dn", 2 * pr_, 3), ("dn", 2 * pr_ + 1, 4)]
        GROUP += [("y", 6 * pr_ + j, 5 + j % 3) for j in range(6)]
    g_uses, g_count = {}, [0] * 8
    for kind, j, b in GROUP:
        g_uses[(kind, j)] = (b, g_count[b])
        g_count[b] += 1
    SLOT_T = [3, 3, 2, 0, 0, 0, 0, 0]
    g_base = [0] * 8
    UPG = 12
    G_UNITS = [("g", 0), ("u", 0), ("g", 1), ("u", 1), ("d", 0), ("d", 1),
               ("g", 2), ("u", 2), ("g", 3), ("u", 3), ("d", 2), ("d", 3)]
    g_unit = {x: n for n, x in enumerate(G_UNITS)}
    G_LAST = [("gu", 0), ("gu", 0), ("gu", 1), ("gu", 1), ("dn", 1), ("dn", 1),
              ("gu", 2), ("gu", 2), ("gu", 3), ("gu", 3), ("dn", 3), ("dn", 3)]

    def gslot(x):
        return (NU + g_unit[x]) % RING

    def gready(x, p, g):
        n = NU + g_unit[x]
        return ring_full[n % RING], (4 * p + g) * (16 * UPG // RING) + 16 * (n // RING + 1)

    def g_order(kind, j, p, g):
        b, n = g_uses[(kind, j)]
        return b, (4 * p + g) * g_count[b] + (p * SLOT_T[b]) + (g_base[b] + n)

    def gfilled(kind, j, p, g):
        b, n = g_order(kind, j, p, g)
        return full[b], n + 1

    def gtaken(kind, j, p, g):
        b, n = g_order(kind, j, p, g)
        return free[b], n

    def moved(kind, j, p, g):
        b, n = g_order(kind, j, p, g)
        return free[b], n + 1

    def t_order(e, p):
        b = e % 3
        return b, p * (4 * g_count[b] + SLOT_T[b]) + (g_base[b] - SLOT_T[b] + e // 3)

    def gbank(kind, j):
        return PS[:, g_uses[(kind, j)][0], :]

    def gfull(kind, j):
        return full[g_uses[(kind, j)][0]]

    def gfree(kind, j):
        return free[g_uses[(kind, j)][0]]

    block = ctx.enter_context(nc.Block())

    @block.tensor
    def _(pe):
        def use(name, b):
            uses[name] = (b, count[b])
            if count[b]:
                pe.wait_ge(free[b], count[b])
            count[b] += 1
            return PS[:, b, :]

        pe.wait_ge(sg("cst_in"), 16)
        pe.wait_ge(sg("vrow_in"), 16 * 5)
        o = use("vec", 6)
        pe.transpose(o[:, 0:NV], vrow, ident[0:NV, 0:NV]).then_inc(full[6], 1)
        for j in (3, 4, 0, 1, 2):
            n = NS if j == 2 else 128
            pe.wait_ge(sg("x_norm"), (3, 4, 0, 1, 2).index(j) + 1)
            for hf in range(2):
                o = use(("xT", j, hf), (2 * j + hf) % 6)
                for c in range(4):
                    ins = pe.transpose(o[:, c * n:(c + 1) * n],
                                       xin[0:n, j, 512 * hf + 128 * c:512 * hf + 128 * c + 128],
                                       ident[0:n, 0:n])
                ins.then_inc(full[(2 * j + hf) % 6], 1)

        def samples(o, src, chunks, w, done):
            for k in range(chunks):
                for c in range(4):
                    ins = pe.matmul(o[NS * c:NS * c + NS, 0:128], src[:, k, SEQ:T], w(k)[:, 128 * c:128 * c + 128],
                                    start=(k == 0), stop=(k == chunks - 1))
            ins.then_inc(done, 1)

        def project(name, src, tiles, banks):
            pe.wait_ge(*unit_ready(name))
            for t, b in zip(tiles, banks):
                t0, n = TILES[t]
                o = use((name, t), b)
                if t == 2:
                    samples(o, src, KD, lambda k: unit(name)[:, 512 * k:512 * k + 512], full[b])
                    continue
                for k in range(KD):
                    ins = pe.matmul(o[0:n, :], src[:, k, t0:t0 + n], unit(name)[:, 512 * k:512 * k + 512],
                                    start=(k == 0), stop=(k == KD - 1))
                ins.then_inc(full[b], 1)
            unit_last[name] = (name, tiles[-1])

        pe.wait_ge(*taken(("xT", 4, 1)))
        project("kvK", memT, (0, 1), (0, 1))
        project("kvV", memT, (0, 1), (2, 3))
        pe.wait_ge(*taken(("kvK", 1)))
        for hf in range(2):
            o = use(("KT", hf), 4 + hf)
            for h in range(2):
                for m in range(2):
                    ins = pe.transpose(o[:, 256 * h + 128 * m:256 * h + 128 * m + 128],
                                       memk[:, m, 128 * (2 * hf + h):128 * (2 * hf + h) + 128], ident)
            ins.then_inc(full[4 + hf], 1)

        pe.wait_ge(sg("crow_in"), 32)
        o = use("crow", 7)
        nr = NB * HIST + CW
        for c in range(NCT):
            ins = pe.transpose(o[:, c * nr:(c + 1) * nr], crow[:, 128 * c:128 * c + 128], ident[0:nr, 0:nr])
        ins.then_inc(full[7], 1)

        pe.wait_ge(*taken(("xT", 2, 1)))
        pe.wait_ge(sg("wg_in"), 32)
        o = use("gates", 6)
        for j in range(4):
            for k in range(KD):
                ins = pe.matmul(o[32 * j:32 * j + 4, 0:T], wg[:, k, 4 * j:4 * j + 4], hT[:, k, :],
                                start=(k == 0), stop=(k == KD - 1))
        ins.then_inc(full[6], 1)

        for u, name in enumerate(("q", "k", "v", "mo")):
            b0 = 3 * (u % 2)
            project(name, hT, (0, 1, 2), (b0, b0 + 1, b0 + 2))
        for u in range(3):
            pe.wait_ge(*unit_ready(f"g{u}"))
            for c in range(4):
                b = (4 * u + c) % 6
                o = use(("cv", 4 * u + c), b)
                for k in range(KD):
                    ins = pe.matmul(o[:, 0:T], unit(f"g{u}")[:, 512 * k + 128 * c:512 * k + 128 * c + 128],
                                    hT[:, k, :], start=(k == 0), stop=(k == KD - 1))
                ins.then_inc(full[b], 1)
            unit_last[f"g{u}"] = ("cv", 4 * u + 3)
        project("gout", hT, (0, 1, 2), (0, 1, 2))

        pe.wait_ge(sg("rows"), 1)
        o = use("cols", 7)
        rows8 = (ROW_RS, ROW_W, ROW_IW, ROW_EN, ROW_G, ROW_B, ROW_EG, ROW_KD)
        for t, (t0, n) in enumerate(TILES):
            for j, r in enumerate(rows8):
                c = (t * 8 + j) * H
                ins = pe.transpose(o[0:n, c:c + H], r[:, t0:t0 + n], ident[0:H, 0:H])
        ins.then_inc(full[7], 1)
        o = use("dec", 6)
        for j, r in enumerate((ROW_IW, ROW_EG)):
            for h in range(H):
                c = (j * H + h) * NCH
                sel = cst[0:H, C_SEL + 128 * h:C_SEL + 128 * h + 128]
                pe.matmul(o[:, c:c + 4], sel, r[:, L - 1:SEQ:L], start=(j == 0 and h == 0), stop=False,
                          skip_group_check=True)
                ins = pe.matmul(o[:, c + 4:c + NCH], sel, r[:, SEQ + DS - 1:T:DS], start=False,
                                stop=(j == 1 and h == H - 1), skip_group_check=True)
        ins.then_inc(full[6], 1)

        def masked_rows(name, b, row, t):
            t0, n = TILES[t]
            neg = cst[0:n, C_NEGS:C_NEGS + n] if t == 2 else cst[0:n, C_NEGP:C_NEGP + n]
            o = use(name, b)
            pe.matmul(o[0:n, 0:H * n].rearrange("p (h l) -> p h l", h=H), ident[0:n, 0:n],
                      bc(neg.unsqueeze(1), n, H, n), start=True, stop=False)
            for h in range(H):
                ins = pe.matmul(o[0:n, h * n:(h + 1) * n], cst[0:H, C_SEL + 128 * h:C_SEL + 128 * h + n],
                                row[:, t0:t0 + n], start=False, stop=(h == H - 1))
            ins.then_inc(full[b], 1)

        def turn(name, b, src, n):
            o = use(name, b)
            for h in range(H):
                ins = pe.transpose(o[:, h * n:(h + 1) * n], src[:, 128 * h:128 * h + 128], ident[0:n, 0:n])
            ins.then_inc(full[b], 1)

        for t, (t0, n) in enumerate(TILES):
            qx, kx, qwx, dx, sx = forms(t)
            pe.wait_ge(*taken(("q", t)))
            turn(("qT", t), 0, q_t[0:n, t, :], n)
            pe.wait_ge(*taken(("k", t)))
            turn(("kT", t), 1, k_t[0:n, t, :], n)
            pe.wait_ge(sg("qw"), t + 1)
            turn(("qwT", t), 2, q_t[0:n, t, :], n)
            masked_rows(("dl", t), 4, ROW_RL, t)
            pe.wait_ge(*taken(("kT", t)))
            o = use(("sc", t), 3)
            for h in range(H):
                ins = pe.matmul(o[0:n, h * n:(h + 1) * n], kx[:, h * n:(h + 1) * n], qx[:, h * n:(h + 1) * n],
                                start=True, stop=True)
            ins.then_inc(full[3], 1)
            pe.wait_ge(sg("sT"), t + 1)
            pe.wait_ge(*taken(("v", t)))
            oo = [use(("num", t, 0), 5), use(("num", t, 1), 6)]
            for h in range(H):
                pe.matmul(oo[h // 2][0:n, (h % 2) * DA:(h % 2 + 1) * DA], sx[0:n, h * n:(h + 1) * n],
                          v_a[0:n, t, h * DA:(h + 1) * DA], start=(h % 2 == 0), stop=False,
                          skip_group_check=True)
            pe.wait_ge(*taken(("qwT", t)))
            pe.wait_ge(sg("kw"), t + 1)
            if t < 2:
                for c in range(2):
                    r = slice(L * c, L * c + L)
                    if t or c:
                        before = (t, c - 1) if c else (t - 1, 1)
                        pe.wait_ge(*taken(("Cu", *before, 0)))
                        pe.wait_ge(*taken(("Cu", *before, 1)))
                    else:
                        pe.wait_ge(sg("C0"), 1)
                    for h in range(H):
                        ins = pe.matmul(oo[h // 2][r, (h % 2) * DA:(h % 2 + 1) * DA],
                                        qwx[:, h * n + L * c:h * n + L * c + L], Cp[:, h, :],
                                        start=False, stop=(c == 1), skip_group_check=True)
                        if c == 1 and h % 2:
                            ins.then_inc(full[5 + h // 2], 1)
                    uu = [use(("Cu", t, c, 0), 7), use(("Cu", t, c, 1), 0)]
                    for h in range(H):
                        ins = pe.matmul(uu[h // 2][:, (h % 2) * DA:(h % 2 + 1) * DA],
                                        k_t[r, t, 128 * h:128 * h + 128], v_a[r, t, h * DA:(h + 1) * DA],
                                        start=(h % 2 == 0), stop=(h % 2 == 1), skip_group_check=True)
                        if h % 2:
                            ins.then_inc(full[uses[("Cu", t, c, h // 2)][0]], 1)
            else:
                for h in range(H):
                    pe.wait_ge(sg("qwm"), h + 1)
                    for b in range(NB):
                        ins = pe.matmul(oo[h // 2][0:n, (h % 2) * DA:(h % 2 + 1) * DA], qwm[:, b, :],
                                        Cs[h % 2][:, b, :], start=False, stop=(b == NB - 1),
                                        skip_group_check=True)
                    if h % 2:
                        ins.then_inc(full[5 + h // 2], 1)
                    pe.wait_ge(sg("vblk"), h + 1)
                    for g, (b0, b1) in enumerate(((0, 3), (3, 6), (6, 8))):
                        bk = (7, 0, 2)[g]
                        o = use(("Cs", h, g), bk)
                        pe.matmul(o[:, 0:(b1 - b0) * DA], k_t[0:n, t, 128 * h:128 * h + 128],
                                  vblk[:, b0:b1, :].rearrange("p b v -> p (b v)"),
                                  start=True, stop=True).then_inc(full[bk], 1)
            pe.wait_ge(sg("ha"), t + 1)
            turn(("haT", t), 1, num[0:n, :], n)
        pe.wait_ge(sg("nst"), 1)
        o = use("nT", 3)
        pe.transpose(o[0:NB * H + H, 0:128], nst, ident).then_inc(full[3], 1)

        pe.wait_ge(sg("tailT"), 1)
        for g in range(3):
            o = use(("tail", g), g)
            for c in range(4):
                ins = pe.transpose(o[0:HIST * (NB + 1), 128 * c:128 * c + 128], tailT[:, 4 * g + c, :], ident)
            ins.then_inc(full[g], 1)
        pe.wait_ge(sg("cvT"), 3)
        for t, (t0, n) in enumerate(TILES):
            for g in range(3):
                o = use(("raw", t, g), g)
                for c in range(4):
                    ins = pe.transpose(o[0:n, 128 * c:128 * c + 128], cvT[:, 4 * g + c, t0:t0 + n], ident)
                ins.then_inc(full[g], 1)
            masked_rows(("dG", t), 3, ROW_G, t)
            pe.wait_ge(sg("gq"), 4 * t + 1)
            turn(("kT2", t), 4, raw[0:n, 1, :], n)
            pe.wait_ge(sg("gq"), 4 * t + 2)
            turn(("kbT", t), 5, kb[0:n, :], n)
            pe.wait_ge(sg("gq"), 4 * t + 3)
            turn(("qT2", t), 6, raw[0:n, 0, :], n)
            pe.wait_ge(sg("gq"), 4 * t + 4)
            turn(("qdT", t), 7, qd[0:n, :], n)
            pe.wait_ge(*taken(("qT2", t)))
            pe.wait_ge(*taken(("qdT", t)))
            for name, b, x in ((("KK", t), 0, kbT), (("QK", t), 1, qT)):
                o = use(name, b)
                for h in range(H):
                    ins = pe.matmul(o[0:n, h * n:(h + 1) * n], kT[:, h * n:(h + 1) * n], x[:, h * n:(h + 1) * n],
                                    start=True, stop=True)
                ins.then_inc(full[b], 1)
            nl = 2 if t == 2 else LEVELS
            for k in range(nl):
                pe.wait_ge(sg("ATk"), lv(t, k) + 1)
                o = use(("X", t, k), 2)
                for h in range(H):
                    ins = pe.matmul(o[0:n, h * n:(h + 1) * n], dG[0:n, h * n:(h + 1) * n],
                                    ident[0:n, 0:n] if k == 0 else Tm[0:n, h * n:(h + 1) * n],
                                    start=True, stop=True)
                ins.then_inc(full[2], 1)
                if k == 0:
                    continue
                pe.wait_ge(*taken(("X", t, k)))
                o = use(("YT", t, k), 3)
                for h in range(H):
                    ins = pe.matmul(o[0:n, h * n:(h + 1) * n], Xm[0:n, h * n:(h + 1) * n],
                                    Um[0:n, h * n:(h + 1) * n], start=True, stop=True)
                ins.then_inc(full[3], 1)
                if k < nl - 1:
                    o = use(("Y", t, k), 4)
                    for h in range(H):
                        ins = pe.matmul(o[0:n, h * n:(h + 1) * n], Um[0:n, h * n:(h + 1) * n],
                                        Xm[0:n, h * n:(h + 1) * n], start=True, stop=True)
                    ins.then_inc(full[4], 1)
            pe.wait_ge(*taken(("YT", t, nl - 1)))
            pe.wait_ge(sg("gv"), t + 1)
            o = use(("wT", t), 5)
            for h in range(H):
                ins = pe.matmul(o[:, h * n:(h + 1) * n], kbg[0:n, 128 * h:128 * h + 128],
                                Um[0:n, h * n:(h + 1) * n], start=True, stop=True)
            ins.then_inc(full[5], 1)
            pe.wait_ge(*taken(("wT", t)))
            pe.wait_ge(*taken(("QK", t)))
            if t < 2:
                for c in range(2):
                    r = slice(L * c, L * c + L)
                    if t or c:
                        pe.wait_ge(*taken(("So", t, c - 1) if c else ("So", t - 1, 1)))
                    else:
                        pe.wait_ge(sg("S0"), 1)
                    o = use(("vn", t, c), 6)
                    for h in range(H):
                        hc = slice(h * n + L * c, h * n + L * c + L)
                        hv = slice(128 * h, 128 * h + 128)
                        pe.matmul(o[r, hv], Um[0:n, hc], raw[0:n, 2, hv], start=(h == 0), stop=False,
                                  skip_group_check=True)
                        ins = pe.matmul(o[r, hv], kbT[:, hc], Sp[:, hv], start=False, stop=(h == H - 1),
                                        skip_group_check=True)
                    ins.then_inc(full[6], 1)
                    pe.wait_ge(*taken(("vn", t, c)))
                    o = use(("So", t, c), 0)
                    for h in range(H):
                        hv = slice(128 * h, 128 * h + 128)
                        ins = pe.matmul(o[:, hv], kd[r, hv], vn[r, hv], start=True, stop=True)
                    ins.then_inc(full[0], 1)
                    o = use(("go", t, c), 7)
                    for h in range(H):
                        hc = slice(h * n + L * c, h * n + L * c + L)
                        hv = slice(128 * h, 128 * h + 128)
                        pe.matmul(o[r, hv], qdT[:, hc], Sp[:, hv], start=(h == 0), stop=False,
                                  skip_group_check=True)
                        ins = pe.matmul(o[r, hv], QKT[r, hc], vn[r, hv], start=False, stop=(h == H - 1),
                                        skip_group_check=True)
                    ins.then_inc(full[7], 1)
            else:
                for h in range(H):
                    hc, hv = slice(h * n, (h + 1) * n), slice(128 * h, 128 * h + 128)
                    pe.wait_ge(sg("nwm"), h + 1)
                    o = use(("vn2", h), 6)
                    pe.matmul(o[0:n, 0:DH], Um[0:n, hc], raw[0:n, 2, hv], start=True, stop=False)
                    for b in range(NB):
                        ins = pe.matmul(o[0:n, 0:DH], nwm[:, b, :], Ss[h % 2][:, b, :], start=False,
                                        stop=(b == NB - 1))
                    ins.then_inc(full[6], 1)
                    pe.wait_ge(sg("vnb"), h + 1)
                    o = use(("go2", h), 7)
                    for b in range(NB):
                        pe.matmul(o[0:n, 0:DH], qdm[:, b, :], Ss[h % 2][:, b, :], start=(b == 0), stop=False)
                    pe.matmul(o[0:n, 0:DH], QKT[0:n, hc], vn[0:n, hv], start=False,
                              stop=True).then_inc(full[7], 1)
                    for g in range(2):
                        o = use(("So2", h, g), g)
                        pe.matmul(o, kd[0:n, hv], vnb[:, 4 * g:4 * g + 4, :].rearrange("p b v -> p (b v)"),
                                  start=True, stop=True).then_inc(full[g], 1)
            pe.wait_ge(sg("hb"), t + 1)
            turn(("hbT", t), 5, kb[0:n, :], n)

        project("xq", hT, (0, 1, 2), (2, 3, 4))
        for t, (t0, n) in enumerate(TILES):
            pe.wait_ge(*taken(("xq", t)))
            turn(("xqT", t), t % 2, xq[0:n, t, :], n)
        for t in range(2):
            t0 = 128 * t
            pe.wait_ge(*taken(("xqT", t)))
            if t == 0:
                pe.wait_ge(*taken(("KT", 1)))
            for g in range(2):
                o = use(("xs", t, g), 2 + g)
                for h in (2 * g, 2 * g + 1):
                    ins = pe.matmul(o[:, MEM * (h % 2):MEM * (h % 2) + MEM], xqT[:, h, t0:t0 + 128], KT[:, h, :],
                                    start=True, stop=True)
                ins.then_inc(full[2 + g], 1)
            pe.wait_ge(sg("pr"), t + 1)
            for m in range(2):
                o = use(("prT", t, m), 4 + m)
                for h in range(H):
                    ins = pe.transpose(o[:, 128 * h:128 * h + 128], pr[:, h, 128 * m:128 * m + 128], ident)
                ins.then_inc(full[4 + m], 1)
            pe.wait_ge(*taken(("prT", t, 0)))
            pe.wait_ge(*taken(("prT", t, 1)))
            o = use(("hcT", t), 6)
            for h in range(H):
                for m in range(2):
                    ins = pe.matmul(o[:, 128 * h:128 * h + 128], memv[:, m, 128 * h:128 * h + 128],
                                    prT[:, m, 128 * h:128 * h + 128], start=(m == 0), stop=(m == 1))
            ins.then_inc(full[6], 1)
        pe.wait_ge(sg("qm"), 1)
        so = [use(("ss", 0), 0), use(("ss", 1), 1)]
        for b in range(NB):
            pe.wait_ge(sg(f"Kb{b % 2}"), 16 * (b // 2 + 1))
            for g in range(2):
                o = use(("KbT", b, g), 2 + g)
                for h in (2 * g, 2 * g + 1):
                    for m in range(2):
                        ins = pe.transpose(o[:, MEM * (h % 2) + 128 * m:MEM * (h % 2) + 128 * m + 128],
                                           Kb[b % 2][:, m, 128 * h:128 * h + 128], ident)
                ins.then_inc(full[2 + g], 1)
            pe.wait_ge(*taken(("KbT", b, 0)))
            pe.wait_ge(*taken(("KbT", b, 1)))
            for h in range(H):
                ins = pe.matmul(so[h // 2][0:NS, MEM * (h % 2):MEM * (h % 2) + MEM],
                                qm[:, h, NS * b:NS * b + NS], KTb[b % 2][:, h, :],
                                start=(b == 0 and h % 2 == 0), stop=(b == NB - 1), skip_group_check=True)
                if b == NB - 1 and h % 2:
                    ins.then_inc(full[h // 2], 1)
        pe.wait_ge(sg("pr"), 3)
        o = use("spT", 4)
        for m in range(2):
            for h in range(H):
                c = (m * H + h) * NS
                ins = pe.transpose(o[:, c:c + NS], pr[0:NS, h, 128 * m:128 * m + 128], ident[0:NS, 0:NS])
        ins.then_inc(full[4], 1)
        pe.wait_ge(*taken("spT"))
        for b in range(NB):
            pe.wait_ge(sg(f"Vb{b % 2}"), 16 * (b // 2 + 1))
            bk = 5 + b % 2
            o = use(("hcs", b), bk)
            for h in range(H):
                for m in range(2):
                    ins = pe.matmul(o[:, DS * h:DS * h + DS], Vb[b % 2][:, m, 128 * h:128 * h + 128],
                                    spT[:, m, NS * h + DS * b:NS * h + DS * b + DS],
                                    start=(m == 0), stop=(m == 1))
            ins.then_inc(full[bk], 1)

        pe.wait_ge(*taken(("haT", 2)))
        pe.wait_ge(*taken(("hbT", 2)))
        pe.wait_ge(*taken(("hcT", 1)))
        pe.wait_ge(*taken(("hcs", NB - 1)))
        step = 0
        for j in range(3):
            for nn in range(2):
                pe.wait_ge(*unit_ready(("gate", j, nn)))
                pe.wait_ge(*unit_ready(("br", j)))
                for t, (t0, n) in enumerate(TILES):
                    o = use(("mg", j, nn, t), 2 * (step % 3))
                    if t == 2:
                        samples(o, hT, KD, lambda k: unit(("gate", j, nn))[:, 512 * k:512 * k + 512],
                                full[2 * (step % 3)])
                        o = use(("mb", j, nn, t), 2 * (step % 3) + 1)
                        samples(o, brT[j], H, lambda k: unit(("br", j))[:, D * k + 512 * nn:D * k + 512 * nn + 512],
                                full[2 * (step % 3) + 1])
                        step += 1
                        continue
                    for k in range(KD):
                        ins = pe.matmul(o[0:n, :], hT[:, k, t0:t0 + n],
                                        unit(("gate", j, nn))[:, 512 * k:512 * k + 512],
                                        start=(k == 0), stop=(k == KD - 1))
                    ins.then_inc(full[2 * (step % 3)], 1)
                    o = use(("mb", j, nn, t), 2 * (step % 3) + 1)
                    for k in range(H):
                        ins = pe.matmul(o[0:n, :], brT[j][:, k, t0:t0 + n],
                                        unit(("br", j))[:, D * k + 512 * nn:D * k + 512 * nn + 512],
                                        start=(k == 0), stop=(k == H - 1))
                    ins.then_inc(full[2 * (step % 3) + 1], 1)
                    step += 1
                unit_last[("gate", j, nn)] = ("mb", j, nn, 2)
            unit_last[("br", j)] = ("mb", j, 1, 2)
        for t, (t0, n) in enumerate(TILES):
            pe.wait_ge(sg("mixed"), t + 1)
            for hf in range(2):
                o = use(("mixT", t, hf), 6 + hf)
                if t == 2:
                    pe.transpose(o[:, 0:128], mixs[:, hf, :], ident).then_inc(full[6 + hf], 1)
                    continue
                for c in range(4):
                    ins = pe.transpose(o[:, c * n:(c + 1) * n],
                                       mixed[0:n, t, 512 * hf + 128 * c:512 * hf + 128 * c + 128],
                                       ident[0:n, 0:n])
                ins.then_inc(full[6 + hf], 1)
        pe.wait_ge(*taken(("mixT", 2, 0)))
        pe.wait_ge(*taken(("mixT", 2, 1)))
        project(("out", 0), mixT, (0, 1, 2), (0, 1, 2))
        project(("out", 1), mixT, (0, 1, 2), (3, 4, 5))

        for t, (t0, n) in enumerate(TILES):
            pe.wait_ge(sg("h2p"), t + 1)
            for hf in range(2):
                o = use(("h2T", t, hf), 6 + hf)
                for c in range(4):
                    ins = pe.transpose(o[:, c * n:(c + 1) * n],
                                       h2p[0:n, t, 512 * hf + 128 * c:512 * hf + 128 * c + 128],
                                       ident[0:n, 0:n])
                ins.then_inc(full[6 + hf], 1)
        pe.wait_ge(*taken(("h2T", 2, 1)))
        pe.wait_ge(sg("wr_in"), 32)
        o = use("lgT", 0)
        for k in range(KD):
            ins = pe.matmul(o[0:20, 0:T], wr[:, k, :], h2T[:, k, :], start=(k == 0), stop=(k == KD - 1))
        ins.then_inc(full[0], 1)
        pe.wait_ge(*taken("lgT"))
        o = use("lg", 1)
        for t, (t0, n) in enumerate(TILES):
            ins = pe.transpose(o[0:n, 20 * t:20 * t + 20], lgT[0:20, t0:t0 + n], ident[0:20, 0:20])
        ins.then_inc(full[1], 1)
        pe.wait_ge(sg("msk"), 1)
        pe.wait_ge(sg("ones"), 1)
        o = use("rank", 2)
        for t, (t0, n) in enumerate(TILES):
            for u in range(t + 1):
                ins = pe.matmul(o[0:n, E * t:E * t + E],
                                cst[0:n, C_TRI:C_TRI + n] if u == t else ones[:, 0:n],
                                msk[0:TILES[u][1], u, :], start=(u == 0), stop=(u == t))
        for u, (t0, n) in enumerate(TILES):
            ins = pe.matmul(o[0:1, 3 * E:4 * E], ones[0:n, 0:1], msk[0:n, u, :], start=(u == 0), stop=(u == 2))
        ins.then_inc(full[2], 1)

        def slots_T(p=None):
            for e in range(E // 2):
                if p is None:
                    o = use(("PwT", e), e % 3)
                else:
                    b, n = t_order(e, p)
                    pe.wait_ge(free[b], n)
                    o = PS[:, b, :]
                for t, (t0, n) in enumerate(TILES):
                    ins = pe.transpose(o[:, t0:t0 + n], Pw[0:n, t, 128 * e:128 * e + 128], ident[0:n, 0:n])
                ins.then_inc(full[e % 3], 1)

        pe.wait_ge(sg("Pm"), 1)
        slots_T()
        for b in range(8):
            g_base[b] = count[b]

        def group(p, g):
            for j in range(4):
                pe.wait_ge(*gtaken("hg", j, p, g))
                o = gbank("hg", j)
                for c in (2 * j, 2 * j + 1):
                    for t, (t0, n) in enumerate(TILES):
                        ins = pe.matmul(o[:, 256 * (c % 2):256 * (c % 2) + 256], h2p[0:n, t, 128 * c:128 * c + 128],
                                        Pm[0:n, t, bass.ds(g * 256, 256)], start=(t == 0), stop=(t == 2))
                ins.then_inc(gfull("hg", j), 1)
            for pr_ in range(2):
                for e in (2 * pr_, 2 * pr_ + 1):
                    if e == 0:
                        pe.wait_ge(*moved("hg", 3, p, g))
                    pe.wait_ge(*gready(("g", e), p, g))
                    pe.wait_ge(*gready(("u", e), p, g))
                    pe.wait_ge(*gtaken("gu", e, p, g))
                    o = gbank("gu", e)
                    s0 = gslot(("g", e))
                    for k in range(KD):
                        for hf in range(2):
                            ins = pe.matmul(o[64 * hf:64 * hf + 64, :], hg[:, k, 64 * e:64 * e + 64],
                                            ring[:, s0:s0 + 2, 512 * k + 256 * hf:512 * k + 256 * hf + 256],
                                            start=(k == 0), stop=(k == KD - 1))
                    ins.then_inc(gfull("gu", e), 1)
                if pr_ == 1:
                    scatter(0, p, g)
                for e in (2 * pr_, 2 * pr_ + 1):
                    pe.wait_ge(sg("act"), (4 * p + g) * 4 + (e + 1))
                    pe.wait_ge(*gtaken("aT", e, p, g))
                    o = gbank("aT", e)
                    for c in range(2):
                        ins = pe.transpose(o[:, 128 * c:128 * c + 128], actb[:, e % 2, 128 * c:128 * c + 128], ident)
                    ins.then_inc(gfull("aT", e), 1)
                for e in (2 * pr_, 2 * pr_ + 1):
                    pe.wait_ge(*moved("aT", e, p, g))
                for x in range(2):
                    pe.wait_ge(*gready(("d", 2 * pr_ + x), p, g))
                for nn in range(2):
                    pe.wait_ge(*gtaken("dn", 2 * pr_ + nn, p, g))
                for nn in range(2):
                    o = gbank("dn", 2 * pr_ + nn)
                    for c in range(4):
                        hf, cc = c // 2, c % 2
                        for x in range(2):
                            w = ring[:, gslot(("d", 2 * pr_ + x)), D * c + 512 * nn:D * c + 512 * nn + 512]
                            ins = pe.matmul(o[64 * x:64 * x + 64, :],
                                            actT[x][:, 128 * cc + 64 * hf:128 * cc + 64 * hf + 64], w,
                                            start=(c == 0), stop=(c == 3))
                    ins.then_inc(gfull("dn", 2 * pr_ + nn), 1)
            scatter(1, p, g)

        def scatter(pr_, p, g):
            pe.wait_ge(sg("pws"), (4 * p + g) * 2 + (pr_ + 1))
            for nn in range(2):
                pe.wait_ge(*moved("dn", 2 * pr_ + nn, p, g))
            for t, (t0, n) in enumerate(TILES):
                for nn in range(2):
                    j = 6 * pr_ + 2 * t + nn
                    pe.wait_ge(*gtaken("y", j, p, g))
                    pe.matmul(gbank("y", j)[0:n, :], pws[pr_][:, t0:t0 + n], outp[:, 512 * nn:512 * nn + 512],
                              start=True, stop=True).then_inc(gfull("y", j), 1)

        with pe.Fori(0, G) as g:
            group(0, g)
        pe.wait_ge(sg("flag"), 1)
        most = pe.value_load(flag[0:1, 0:1], min_val=0, max_val=T)
        with pe.If(most > SLOTS):
            with pe.Fori(1, PASSES) as p:
                pe.wait_ge(sg("Pm"), p + 1)
                slots_T(p)
                with pe.Fori(0, G) as g:
                    group(p, g)

    @block.sync
    def _(sp):
        for j in (3, 4):
            sp.dma_start(xin[:, j, :], a["mem_prompt"][0, 128 * (j - 3):128 * (j - 2), :]).then_inc(sg(f"xin{j}"), 16)
        r = 0
        for x, n in ((a["norm_mix"][0], KD), (a["mem_norm"][0], KD), (a["mlstm_norm"][0], H),
                     (a["gdn_norm"][0], 1)):
            sp.dma_start(vrow[r:r + n, :], x.rearrange("(r c) -> r c", c=128)).then_inc(sg("vrow_in"), 16)
            r += n
        sp.dma_start(vrow[r:r + NB * H, :],
                     a["state_mlstm_n"][0].rearrange("b h k -> (b h) k")).then_inc(sg("vrow_in"), 16)
        sp.dma_start(cst[:, :], a["table"][:, 0:C_N]).then_inc(sg("cst_in"), 16)
        for j, (t0, n) in enumerate(TILES):
            x = a["x_prompt"][0, t0:t0 + n, :] if j < 2 else a["x_sample"].rearrange("b s d -> (b s) d")
            sp.dma_start(xin[0:n, j, :], x).then_inc(sg(f"xin{j}"), 16)
        sp.dma_start(wg[:, :, 0:8], w_in[:, O_IF:O_IF + 8].rearrange("(c p) n -> p c n", p=128)) \
            .then_inc(sg("wg_in"), 16)
        sp.dma_start(wg[:, :, 8:16], w_in[:, O_GAB:O_GAB + 8].rearrange("(c p) n -> p c n", p=128)) \
            .then_inc(sg("wg_in"), 16)
        for n, (name, src) in enumerate(units):
            if n >= RING:
                sp.wait_ge(*filled(unit_last[units[n - RING][0]]))
            sp.dma_start(unit(name).rearrange("p (c n) -> p c n", c=src.shape[1]), src) \
                .then_inc(ring_full[n % RING], 16)

        def load_group(p, g, first):
            for u, (kind, e) in enumerate(G_UNITS):
                if first and u < RING:
                    sp.wait_ge(*filled(unit_last[units[NU + u - RING][0]]))
                elif u < RING:
                    kd_, j = G_LAST[u + UPG - RING]
                    b, n = g_uses[(kd_, j)]
                    sp.wait_ge(full[b], prev_order(kd_, j, p, g))
                else:
                    sp.wait_ge(*gfilled(*G_LAST[u - RING], p, g))
                w = {"g": "w_exp_gate", "u": "w_exp_up", "d": "w_exp_down"}[kind]
                if kind == "d":
                    src = a[w][0, bass.ds(g * EG + e, 1)].rearrange("e (c p) n -> p (e c) n", p=128)
                else:
                    src = a[w][0, bass.ds(g * EG + e, 1)].rearrange("e (p c) n -> p (e c) n", p=128)
                sp.dma_start(ring[:, gslot((kind, e)), :].rearrange("p (c n) -> p c n", c=4 if kind == "d" else 8),
                             src).then_inc(ring_full[gslot((kind, e))], 16)

        def prev_order(kind, j, p, g):
            b, n = g_uses[(kind, j)]
            if isinstance(g, int):
                if g:
                    return (4 * p + (g - 1)) * g_count[b] + p * SLOT_T[b] + (g_base[b] + n + 1)
                return (4 * p - 1) * g_count[b] + (p - 1) * SLOT_T[b] + (g_base[b] + n + 1)
            return (4 * p + g) * g_count[b] + p * SLOT_T[b] + (g_base[b] + n + 1 - g_count[b])

        load_group(0, 0, True)
        with sp.Fori(1, G) as g:
            load_group(0, g, False)
        sp.wait_ge(sg("flag"), 1)
        most = sp.value_load(flag[0:1, 0:1], min_val=0, max_val=T)
        with sp.If(most > SLOTS):
            with sp.Fori(1, PASSES) as p:
                load_group(p, 0, False)
                with sp.Fori(1, G) as g:
                    load_group(p, g, False)
        for t, (t0, n) in enumerate(TILES):
            y = out["y_prompt"][0, t0:t0 + n, :] if t < 2 else out["y_sample"].rearrange("b s d -> (b s) d")
            sp.wait_ge(sg("y"), t + 1)
            sp.dma_start(y, x2[0:n, t, :]).then_inc(sg("y_out"), 16)
        sp.wait_ge(sg("y_out"), 48)

    @block.gpsimd
    def _(pool):
        small_in = sg("small_in")
        nsm = 0
        for dst, src in ((bias4[:, 0:1], a["b_igate"][0]), (bias4[:, 1:2], a["b_fgate"][0]),
                         (bias4[:, 2:3], a["dt_bias"][0]), (bias4[:, 3:4], a["a_log"][0]),
                         (brt[0:G, :], a["b_router_group"][0]), (brt[G:20, :], a["b_router_expert"][0])):
            pool.dma_start(dst, src.rearrange("(n a) -> n a", a=1)).then_inc(small_in, 16)
            nsm += 1
        pool.dma_start(rset, a["table"][0:H, C_RST:C_ALL]).then_inc(small_in, 16)
        pool.dma_start(m0, a["state_mlstm_m"][0].rearrange("b h -> h b"), allow_slow_non_contiguous=True).then_inc(small_in, 16)
        pool.dma_start(gffn, a["norm_ffn"][0].rearrange("(p c) -> p c", c=KD)).then_inc(small_in, 16)
        pool.dma_start(crow[0:NB * HIST, :], a["state_gdn_conv"][0].rearrange("b s c -> (b s) c")) \
            .then_inc(sg("crow_in"), 16)
        pool.dma_start(crow[NB * HIST:, :], a["conv_w"][0]).then_inc(sg("crow_in"), 16)
        pool.dma_start(wr[:, :, 0:G], a["w_router_group"][0].rearrange("(p c) n -> p c n", c=KD)).then_inc(sg("wr_in"), 16)
        pool.dma_start(wr[:, :, G:20], a["w_router_expert"][0].rearrange("(p c) n -> p c n", c=KD)).then_inc(sg("wr_in"), 16)
        pool.memset(ones[:, :], 1.0).then_inc(sg("ones"), 1)
        for m in range(2):
            pool.wait_ge(*taken(("kvK", m)))
            pool.dma_start(out["mem_k"][0, 0, 128 * m:128 * m + 128].rearrange("m h d -> m (h d)"),
                           memk[:, m, :]).then_inc(sg("memk_out"), 16)
            pool.wait_ge(*taken(("kvV", m)))
            pool.dma_start(out["mem_v"][0, 0, 128 * m:128 * m + 128].rearrange("m h d -> m (h d)"),
                           memv[:, m, :]).then_inc(sg("kv_out"), 16)
        pool.wait_ge(sg("rows"), 1)
        pool.dma_start(out["m_p"][0].rearrange("b h -> h b"), ROW_M[:, SEQ - 1:SEQ], allow_slow_non_contiguous=True).then_inc(sg("m_out"), 16)
        pool.dma_start(out["m_s"][0].rearrange("b h -> h b"), ROW_M[:, SEQ + DS - 1:T:DS], allow_slow_non_contiguous=True).then_inc(sg("m_out"), 16)
        for h in range(2):
            if h:
                pool.wait_ge(*filled(("haT", 1)))
            else:
                pool.wait_ge(*filled("gates"))
                pool.wait_ge(sg("memk_out"), 32)
            pool.dma_start(Cs[h][:, :, 0:DH], a["state_mlstm_C"][0, :, h].rearrange("b k v -> k b v")) \
                .then_inc(sg(f"Cs_in{h}"), 16)
        pool.wait_ge(sg("Cp"), 1)
        pool.dma_start(out["C_p"][0, 0].rearrange("h k v -> k h v"), Cp[:, :, 0:DH]).then_inc(sg("Cp_out"), 16)
        for h in range(H):
            pool.wait_ge(sg("Cs"), h + 1)
            pool.dma_start(out["C_s"][0, :, h].rearrange("b k v -> k b v"), Cs[h % 2][:, :, 0:DH]) \
                .then_inc(sg(f"Cs_out{h % 2}"), 16)
            if h < 2:
                pool.wait_ge(sg(f"Cs_out{h}"), 16)
                pool.dma_start(Cs[h][:, :, 0:DH], a["state_mlstm_C"][0, :, h + 2].rearrange("b k v -> k b v")) \
                    .then_inc(sg(f"Cs_in{h}"), 16)
        pool.wait_ge(*taken("nT"))
        pool.dma_start(out["n_s"][0].rearrange("b h k -> (b h) k"), nrow[0:NB * H, :]).then_inc(sg("n_out"), 16)
        pool.dma_start(out["n_p"][0, 0], nrow[NB * H:NB * H + H, :]).then_inc(sg("n_out"), 16)
        pool.wait_ge(*taken(("tail", 2)))
        pool.dma_start(out["conv_p"][0, 0], tails[0:HIST, :]).then_inc(sg("tail_out"), 16)
        pool.dma_start(out["conv_s"][0].rearrange("b s c -> (b s) c"), tails[HIST:, :]).then_inc(sg("tail_out"), 16)
        pool.wait_ge(sg("Cs_out1"), 32)
        pool.wait_ge(sg("Cs_out0"), 32)
        pool.wait_ge(sg("Cp_out"), 16)
        for h in range(2):
            if h:
                pool.wait_ge(*filled(("raw", 2, 2)))
            else:
                pool.wait_ge(*filled(("haT", 2)))
            pool.dma_start(Ss[h], a["state_gdn_S"][0, :, h].rearrange("b k v -> k b v")) \
                .then_inc(sg(f"Ss_in{h}"), 16)
        pool.wait_ge(sg("Spout"), 1)
        pool.dma_start(out["S_p"][0, 0].rearrange("h k v -> k h v"),
                       Sp.rearrange("p (h v) -> p h v", h=H)).then_inc(sg("Sp_out"), 16)
        for h in range(H):
            pool.wait_ge(sg("Ssd"), h + 1)
            pool.dma_start(out["S_s"][0, :, h].rearrange("b k v -> k b v"), Ss[h % 2]) \
                .then_inc(sg(f"Ss_out{h % 2}"), 16)
            if h < 2:
                pool.wait_ge(sg(f"Ss_out{h}"), 16)
                pool.dma_start(Ss[h], a["state_gdn_S"][0, :, h + 2].rearrange("b k v -> k b v")) \
                    .then_inc(sg(f"Ss_in{h}"), 16)
        for s in ("Ss_out0", "Ss_out1"):
            pool.wait_ge(sg(s), 32)
        pool.wait_ge(sg("Sp_out"), 16)
        pool.wait_ge(*filled(("hbT", 2)))
        for t, (t0, n) in enumerate(TILES):
            x = a["x_prompt"][0, t0:t0 + n, :] if t < 2 else a["x_sample"].rearrange("b s d -> (b s) d")
            pool.dma_start(x2[0:n, t, :], x).then_inc(sg("x2_in"), 16)
        for b in range(NB):
            if b >= 2:
                pool.wait_ge(*filled(("KbT", b - 2, 1)))
            pool.dma_start(Kb[b % 2], a["cache_mem_k"][0, b].rearrange("(c p) h d -> p c (h d)", p=128)) \
                .then_inc(sg(f"Kb{b % 2}"), 16)
            if b < 2:
                pool.dma_start(Vb[b], a["cache_mem_v"][0, b].rearrange("(c p) h d -> p c (h d)", p=128)) \
                    .then_inc(sg(f"Vb{b}"), 16)
        for b in range(2, NB):
            pool.wait_ge(*filled(("hcs", b - 2)))
            pool.dma_start(Vb[b % 2], a["cache_mem_v"][0, b].rearrange("(c p) h d -> p c (h d)", p=128)) \
                .then_inc(sg(f"Vb{b % 2}"), 16)
        pool.wait_ge(*filled((("out", 1), 2)))
        pool.dma_start(gfin, a["final_norm"].partition_broadcast(128)).then_inc(sg("gfin_in"), 16)
        for s, n in (("kv_out", 32), ("memk_out", 32), ("m_out", 32), ("n_out", 32), ("tail_out", 32), ("gfin_in", 16), ("wr_in", 32)):
            pool.wait_ge(sg(s), n)

    @block.scalar
    def _(act):
        def run(o, i, f, **kw):
            return act.activation(o, i, f, **kw)

        act.preload_act_table_set("natural_log_exp_and_others")
        for i, j in enumerate((3, 4, 0, 1, 2)):
            n = NS if j == 2 else 128
            act.wait_ge(sg(f"xin{j}"), 16)
            astep(run(junk[0:n, :], xin[0:n, j, :], ACT.Square, accum_out=ss[0:n, j:j + 1]))
            astep(run(rstd[0:n, j:j + 1], ss[0:n, j:j + 1], ACT.Ln, scale=1.0 / D, bias=EPS))
            run(rstd[0:n, j:j + 1], rstd[0:n, j:j + 1], ACT.Exp, scale=-0.5).then_inc(sg("rstd"), 1)

        def copy_out(name, o, i, scale=1.0, wait=True):
            if wait:
                act.wait_ge(*filled(name))
            run(o, i, ACT.Copy, scale=scale).then_inc(freed(name), 1)

        def rows_out(name, t, o, scale, f=ACT.Copy, done=None):
            act.wait_ge(*filled((name, t)))
            if t < 2:
                ins = run(o[:, t, :], bank_of((name, t)), f, scale=scale)
            else:
                for c in range(4):
                    ins = run(o[0:NS, t, 128 * c:128 * c + 128], bank_of((name, t))[NS * c:NS * c + NS, 0:128], f,
                              scale=scale)
            ins.then_inc(done or freed((name, t)), 1)

        for name, o in (("kvK", memk), ("kvV", memv)):
            for m in range(2):
                copy_out((name, m), o[:, m, :], bank_of((name, m)))
        for hf in range(2):
            copy_out(("KT", hf), KT[:, 2 * hf:2 * hf + 2, :].rearrange("p h m -> p (h m)"), bank_of(("KT", hf)))
        act.wait_ge(sg("small_in"), 16 * 9)
        astep(run(bias4[:, 4:5], bias4[:, 3:4], ACT.Exp))
        act.wait_ge(*filled("gates"))
        run(ROW_B, bank_of("gates")[96:100, 0:T], ACT.Exp, scale=-1.0).then_inc(sg("rowB"), 1)
        act.wait_ge(sg("rowZ"), 1)
        astep(run(ROW_E, ROW_E, ACT.Exp))
        run(ROW_E, ROW_E, ACT.Ln, bias=1.0).then_inc(sg("rowL"), 1)
        for t, (t0, n) in enumerate(TILES):
            rows_out("q", t, q_t, 1.0)
        for t, (t0, n) in enumerate(TILES):
            rows_out("k", t, k_t, QSCALE)
        act.wait_ge(sg("rowX"), 1)
        astep(run(ROW_EN, ROW_M, ACT.Exp, scale=-1.0))
        astep(run(ROW_EG, ROW_G, ACT.Exp))
        astep(run(ROW_W, ROW_W, ACT.Exp))
        astep(run(ROW_IW, ROW_IW, ACT.Exp))
        run(ROW_KD, ROW_KD, ACT.Exp).then_inc(sg("rows"), 1)
        act.preload_act_table_set("exp_and_others")
        for t, (t0, n) in enumerate(TILES):
            rows_out("mo", t, mo, 0.5, ACT.Tanh)
        for c in range(NCT):
            act.wait_ge(*filled(("cv", c)))
            run(cin[:, c, HIST:], bank_of(("cv", c))[:, 0:SEQ], ACT.Copy)
            run(cis[:, c, :].rearrange("p (b s) -> p b s", b=NB)[:, :, HIST:],
                bank_of(("cv", c))[:, SEQ:T].rearrange("p (b s) -> p b s", b=NB), ACT.Copy) \
                .then_inc(freed(("cv", c)), 1)
        for t, (t0, n) in enumerate(TILES):
            rows_out("gout", t, gout, 0.5, ACT.Tanh, sg("gout_e"))

        act.preload_act_table_set("natural_log_exp_and_others")
        for t, (t0, n) in enumerate(TILES):
            qx, kx, qwx, dx, sx = forms(t)
            if t == 1:
                act.wait_ge(*filled(("sc", 0)))
            copy_out(("qT", t), qx[:, 0:H * n], bank_of(("qT", t))[:, 0:H * n])
            copy_out(("kT", t), kx[:, 0:H * n], bank_of(("kT", t))[:, 0:H * n])
            act.wait_ge(*filled(("dl", t)))
            act.wait_ge(*taken("cols"))
            if t == 1:
                act.wait_ge(sg("dT_free"), 1)
            for h in range(H):
                ins = run(dx[0:n, h * n:(h + 1) * n], bank_of(("dl", t))[0:n, h * n:(h + 1) * n], ACT.Exp,
                          bias=cols[0:n, t, COL_RS, h:h + 1])
            ins.then_inc(freed(("dl", t)), 1)
            if t:
                act.wait_ge(*filled(("haT", t - 1)))
            for g in range(2):
                act.wait_ge(*filled(("num", t, g)))
                ins = run(num[0:n, 256 * g:256 * g + 256].rearrange("p (h v) -> p h v", h=2),
                          bank_of(("num", t, g))[0:n, 0:2 * DA].rearrange("p (h v) -> p h v", h=2)[:, :, 0:DH],
                          ACT.Copy)
            ins.then_inc(sg("num_in"), 1)
            act.wait_ge(sg("ms"), t + 1)
            astep(run(hs4[0:n, 3, :], hs4[0:n, 3, :], ACT.Ln, scale=1.0 / DH, bias=EPS))
            run(hs4[0:n, 4, :], hs4[0:n, 3, :], ACT.Exp, scale=-0.5).then_inc(sg("ms_r"), 1)
        copy_out("nT", nrow, bank_of("nT")[0:NB * H + H, 0:128])

        act.preload_act_table_set("exp_and_others")
        for g in range(3):
            act.wait_ge(sg("conv"), g + 1)
            if g == 2:
                act.wait_ge(sg("cvT"), 1)
            run(stmp[:, g % 2, :], cvT[:, 4 * g:4 * g + 4, :].rearrange("p c t -> p (c t)"), ACT.Tanh, scale=0.5) \
                .then_inc(sg("silu_e"), 1)
        act.preload_act_table_set("natural_log_exp_and_others")
        for g in range(3):
            if g == 0:
                act.wait_ge(*filled(("haT", 2)))
                act.wait_ge(sg("Cs"), 4)
                act.wait_ge(sg("Cs_out1"), 32)
            copy_out(("tail", g), tails[:, 512 * g:512 * g + 512], bank_of(("tail", g))[0:HIST * (NB + 1), :])
        for t, (t0, n) in enumerate(TILES):
            if t:
                act.wait_ge(*filled(("hbT", t - 1)))
            for g in range(3):
                act.wait_ge(*filled(("raw", t, g)))
                copy_out(("raw", t, g), raw[0:n, g, :], bank_of(("raw", t, g))[0:n, :], wait=False)
            act.wait_ge(sg("gss"), t + 1)
            astep(run(hs4[0:n, 0:2, :], hs4[0:n, 0:2, :], ACT.Ln, bias=EPS))
            run(hs4[0:n, 2:4, :], hs4[0:n, 0:2, :], ACT.Exp, scale=-0.5).then_inc(sg("gss_r"), 1)
            copy_out(("kT2", t), kT[:, 0:H * n], bank_of(("kT2", t))[:, 0:H * n])
            act.wait_ge(*filled(("dG", t)))
            if t == 0:
                act.wait_ge(sg("tail_out"), 32)
            for h in range(H):
                ins = run(dG[0:n, h * n:(h + 1) * n], bank_of(("dG", t))[0:n, h * n:(h + 1) * n], ACT.Exp,
                          bias=cols[0:n, t, COL_G, h:h + 1])
            ins.then_inc(freed(("dG", t)), 1)
            copy_out(("qT2", t), qT[:, 0:H * n], bank_of(("qT2", t))[:, 0:H * n])
            for k in range(1, 2 if t == 2 else LEVELS):
                copy_out(("X", t, k), Xm[0:n, 0:H * n], bank_of(("X", t, k))[0:n, 0:H * n])
            copy_out(("wT", t), kbT[:, 0:H * n], bank_of(("wT", t))[:, 0:H * n], scale=-1.0)
            if t < 2:
                for c in range(2):
                    r = slice(L * c, L * c + L)
                    copy_out(("vn", t, c), vn[r, :], bank_of(("vn", t, c))[r, :])
                    act.wait_ge(*filled(("go", t, c)))
                    copy_out(("go", t, c), Xm[r, :], bank_of(("go", t, c))[r, :], wait=False)
            else:
                for h in range(H):
                    copy_out(("vn2", h), vn[0:n, 128 * h:128 * h + 128], bank_of(("vn2", h))[0:n, 0:DH])
                    copy_out(("go2", h), Xm[0:n, 128 * h:128 * h + 128], bank_of(("go2", h))[0:n, 0:DH])
            act.wait_ge(sg("gs"), t + 1)
            astep(run(hs4[0:n, 6, :], hs4[0:n, 5, :], ACT.Ln, scale=1.0 / DH, bias=EPS))
            run(hs4[0:n, 7, :], hs4[0:n, 6, :], ACT.Exp, scale=-0.5).then_inc(sg("gs_r"), 1)

        act.wait_ge(*filled(("hbT", 2)))
        for t, (t0, n) in enumerate(TILES):
            rows_out("xq", t, xq, QSCALE)
        for t, (t0, n) in enumerate(TILES):
            copy_out(("xqT", t), xqT[:, :, t0:t0 + n],
                     bank_of(("xqT", t))[:, 0:H * n].rearrange("p (h l) -> p h l", h=H))
        for i in range(3):
            n = NS if i == 2 else 128
            act.wait_ge(sg("negmax"), i + 1)
            if i:
                act.wait_ge(*filled(("prT", i - 1, 1)))
            for h in range(H):
                name = ("xs", i, h // 2) if i < 2 else ("ss", h // 2)
                ins = run(pr[0:n, h, :], bank_of(name)[0:n, MEM * (h % 2):MEM * (h % 2) + MEM], ACT.Exp,
                          bias=negmax[0:n, h:h + 1], accum_out=psumx[0:n, h:h + 1])
                if h % 2:
                    ins.then_inc(freed(name), 1)
            if i == 0:
                act.wait_ge(sg("Ss_out1"), 32)
            if i < 2:
                copy_out(("prT", i, 0), prT[:, 0, :], bank_of(("prT", i, 0)))
                copy_out(("hcT", i), brT[2][:, :, 128 * i:128 * i + 128],
                         bank_of(("hcT", i)).rearrange("p (h l) -> p h l", h=H))
                if i == 1:
                    for b in range(NB):
                        if b >= 2:
                            act.wait_ge(*filled(("KbT", b - 1, 1)))
                        copy_out(("KbT", b, 1), KTb[b % 2][:, 2:4, :].rearrange("p h m -> p (h m)"),
                                 bank_of(("KbT", b, 1)))

        step = 0
        act.preload_act_table_set("exp_and_others")
        for j in range(3):
            for nn in range(2):
                for t, (t0, n) in enumerate(TILES):
                    wd = 512 if t < 2 else 128
                    act.wait_ge(*filled(("mg", j, nn, t)))
                    if step >= 2:
                        act.wait_ge(sg("sig_read"), step - 1)
                    run(sig[:, step % 2, 0:wd], bank_of(("mg", j, nn, t))[:, 0:wd], ACT.Tanh, scale=0.5) \
                        .then_inc(freed(("mg", j, nn, t)), 1)
                    step += 1
        for t, (t0, n) in enumerate(TILES):
            copy_out(("mixT", t, 0), mixT[:, 0:4, t0:t0 + n],
                     bank_of(("mixT", t, 0))[:, 0:4 * n].rearrange("p (c l) -> p c l", c=4), scale=0.5)

        def rms_x2(t, n, where):
            astep(run(where[0:n, :], x2[0:n, t, :], ACT.Square, accum_out=rst[0:n, t:t + 1]))
            astep(run(rst[0:n, t:t + 1], rst[0:n, t:t + 1], ACT.Ln, scale=1.0 / D, bias=EPS))
            run(rst[0:n, t:t + 1], rst[0:n, t:t + 1], ACT.Exp, scale=-0.5).then_inc(sg("rst"), 1)

        act.preload_act_table_set("natural_log_exp_and_others")
        for t, (t0, n) in enumerate(TILES):
            act.wait_ge(sg("x2"), t + 1)
            rms_x2(t, n, Pm[:, 0, :])
        act.wait_ge(sg("lge"), 1)
        run(rtmp, rtmp, ACT.Exp).then_inc(sg("lge_r"), 1)
        act.wait_ge(sg("top"), 1)
        run(rt1[:, 5, :], rt1[:, 4, :], ACT.Exp).then_inc(sg("top_r"), 1)

        def slots_out(p=None):
            for e in range(E // 2):
                b, k = uses[("PwT", e)] if p is None else t_order(e, p)
                act.wait_ge(full[b], k + 1)
                run(PwT[:, e, :], PS[:, b, 0:T], ACT.Copy).then_inc(free[b], 1)

        slots_out()
        act.preload_act_table_set("exp_and_others")

        def group(p, g):
            it = 4 * p + g
            for pr_ in range(2):
                act.wait_ge(sg("pws_free"), it * 2 + (pr_ + 1))
                run(pws[pr_], PwT[:, bass.ds(g * 2 + pr_, 1), :].rearrange("p a t -> p (a t)"), ACT.Copy) \
                    .then_inc(sg("pws"), 1)
            for pr_ in range(2):
                for e in (2 * pr_, 2 * pr_ + 1):
                    act.wait_ge(*gfilled("gu", e, p, g))
                    act.wait_ge(sg("ea_free"), it * 4 + (e + 1))
                    run(ea[:, e % 2, :], gbank("gu", e)[:, 0:256], ACT.Tanh, scale=0.5).then_inc(sg("ea"), 1)
                for e in (2 * pr_, 2 * pr_ + 1):
                    act.wait_ge(*gfilled("aT", e, p, g))
                    if e < 2:
                        act.wait_ge(sg("act_free"), it * 4 + (e + 1))
                    else:
                        act.wait_ge(*gfilled("dn", 1, p, g))
                    run(actT[e % 2], gbank("aT", e)[:, 0:256], ACT.Copy).then_inc(gfree("aT", e), 1)
                act.wait_ge(*gfilled("dn", 2 * pr_, p, g))
                act.wait_ge(sg("outp_free"), it * 2 + (pr_ + 1))
                run(outp[:, 0:512], gbank("dn", 2 * pr_), ACT.Copy).then_inc(gfree("dn", 2 * pr_), 1)

        with act.Fori(0, G) as g:
            group(0, g)
        act.wait_ge(sg("flag"), 1)
        most = act.value_load(flag[0:1, 0:1], min_val=0, max_val=T)
        with act.If(most > SLOTS):
            with act.Fori(1, PASSES) as p:
                slots_out(p)
                with act.Fori(0, G) as g:
                    group(p, g)
        act.preload_act_table_set("natural_log_exp_and_others")
        for t, (t0, n) in enumerate(TILES):
            act.wait_ge(sg("x3"), 1)
            rms_x2(t, n, Pw[:, 0, :])

    @block.vector
    def _(dve):
        tt, ts, stt = dve.tensor_tensor, dve.tensor_scalar, dve.scalar_tensor_tensor
        cp = dve.tensor_copy

        marks = [0]

        def mark(sem_, n=1):
            marks[0] = (marks[0] + 1) % NSCRAP
            dve.memset(scrap[:, marks[0]:marks[0] + 1], 0.0).then_inc(sem_, n)

        dve.wait_ge(*filled("vec"))
        cp(vecT, bank_of("vec")[:, 0:NV]).then_inc(freed("vec"), 1)
        for i, j in enumerate((3, 4, 0, 1, 2)):
            n = NS if j == 2 else 128
            dve.wait_ge(sg("rstd"), i + 1)
            ts(xin[0:n, j, :], xin[0:n, j, :], rstd[0:n, j:j + 1], None, ALU.mult).then_inc(sg("x_norm"), 1)
        dve.wait_ge(*taken("vec"))
        for j in (3, 4, 0, 1, 2):
            n = NS if j == 2 else 128
            for hf in range(2):
                g0 = (V_MEM if j > 2 else V_MIX) + 4 * hf
                dst = memT[:, 4 * hf:4 * hf + 4, 128 * (j - 3):128 * (j - 2)] if j > 2 else \
                    hT[:, 4 * hf:4 * hf + 4, TILES[j][0]:TILES[j][0] + n]
                dve.wait_ge(*filled(("xT", j, hf)))
                tt(dst, bank_of(("xT", j, hf))[:, 0:4 * n].rearrange("p (c l) -> p c l", c=4),
                   bc(vecT[:, g0:g0 + 4].unsqueeze(2), 128, 4, n), ALU.mult).then_inc(freed(("xT", j, hf)), 1)

        dve.wait_ge(*filled("crow"))
        cp(cwT, bank_of("crow")[:, 0:NCT * (NB * HIST + CW)].rearrange("p (c r) -> p c r", c=NCT)) \
            .then_inc(freed("crow"), 1)

        dve.wait_ge(sg("small_in"), 16 * 9)
        dve.wait_ge(*filled("gates"))
        gt = bank_of("gates")
        ts(ROW_Z[:, 0, :], gt[32:32 + H, 0:T], bias4[:, 1:2], None, ALU.add)
        dstep(ts(ROW_Z[:, 1, :], gt[64:64 + H, 0:T], bias4[:, 2:3], None, ALU.add))
        stt(ROW_E, ROW_Z, -1.0, ROW_Z, ALU.mult, ALU.min).then_inc(sg("rowZ"), 1)
        dstep(ts(ROW_I, gt[0:H, 0:T], bias4[:, 0:1], None, ALU.add))
        dve.wait_ge(sg("rowB"), 1)
        dstep(ts(ROW_B, ROW_B, 1.0, None, ALU.add))
        dve.reciprocal(ROW_B, ROW_B).then_inc(freed("gates"), 1)
        dve.wait_ge(sg("rowL"), 1)
        dstep(stt(ROW_F, ROW_Z[:, 0, :], 0.0, ROW_E[:, 0, :], ALU.min, ALU.subtract))
        dstep(stt(ROW_A, ROW_Z[:, 1, :], 0.0, ROW_E[:, 1, :], ALU.max, ALU.add))
        dstep(ts(ROW_A, ROW_A, bias4[:, 4:5], -1.0, ALU.mult, ALU.mult))
        dve.wait_ge(sg("cst_in"), 16)
        dstep(dve.tensor_tensor_scan(ROW_BC, rset, ROW_F, 0.0, ALU.mult, ALU.add))
        dstep(dve.tensor_tensor_scan(ROW_G, rset, ROW_A, 0.0, ALU.mult, ALU.add))
        dstep(dve.tensor_tensor_scan(ROW_M[:, 0:SEQ], ROW_F[:, 0:SEQ], ROW_I[:, 0:SEQ], 0.0, ALU.add, ALU.max))

        def steps_of(r):
            return r[:, SEQ:T].rearrange("p (b s) -> p b s", b=NB)

        def chunks_of(r):
            return r[:, 0:SEQ].rearrange("p (c s) -> p c s", c=SEQ // L)

        fs, is_, ms = steps_of(ROW_F), steps_of(ROW_I), steps_of(ROW_M)
        for s in range(DS):
            dstep(tt(ms[:, :, s], m0 if s == 0 else ms[:, :, s - 1], fs[:, :, s], ALU.add))
            dstep(tt(ms[:, :, s], ms[:, :, s], is_[:, :, s], ALU.max))
        dstep(tt(ROW_RS, ROW_I, ROW_BC, ALU.subtract))
        dstep(tt(ROW_RL, ROW_BC, ROW_M, ALU.subtract))
        nch = SEQ // L
        for part, c, n in ((chunks_of, nch, L), (steps_of, NB, DS)):
            rl, rs, g, m = part(ROW_RL), part(ROW_RS), part(ROW_G), part(ROW_M)
            tt(part(ROW_W), rs, bc(rl[:, :, n - 1:n], H, c, n), ALU.add)
            tt(part(ROW_KD), bc(g[:, :, n - 1:n], H, c, n), g, ALU.subtract)
            if c == nch:
                tt(part(ROW_IW)[:, 1:, :], rl[:, 1:, :], bc(m[:, 0:c - 1, n - 1:n], H, c - 1, n), ALU.add)
                cp(part(ROW_IW)[:, 0, :], rl[:, 0, :])
            else:
                ins = tt(part(ROW_IW), rl, bc(m0.unsqueeze(2), H, c, n), ALU.add)
        ins.then_inc(sg("rowX"), 1)
        dve.wait_ge(sg("x_norm"), 5)
        for t, (t0, n) in enumerate(TILES):
            va = v_a[0:n, t, :].rearrange("p (h v) -> p h v", h=H)
            dve.wait_ge(*filled(("v", t)))
            dve.memset(va[:, :, DH:DA], 1.0)
            if t < 2:
                ins = cp(va[:, :, 0:DH], bank_of(("v", t)).rearrange("p (h v) -> p h v", h=H))
            else:
                for h in range(H):
                    ins = cp(va[:, h, 0:DH], bank_of(("v", t))[NS * h:NS * h + NS, 0:DH])
            ins.then_inc(freed(("v", t)), 1)
        for t, (t0, n) in enumerate(TILES):
            dve.wait_ge(*taken(("mo", t)))
            dstep(ts(mo[0:n, t, :], mo[0:n, t, :], 0.5, 0.5, ALU.mult, ALU.add))
        dve.memset(cin[:, :, 0:HIST], 0.0)
        cp(cis.rearrange("p c (b s) -> p c b s", b=NB)[:, :, :, 0:HIST],
           cwT[:, :, 0:NB * HIST].rearrange("p c (b s) -> p c b s", b=NB))
        dve.wait_ge(sg("memk_out"), 32)
        dve.memset(Cp, 0.0).then_inc(sg("C0"), 1)
        for t, (t0, n) in enumerate(TILES):
            dve.wait_ge(sg("gout_e"), t + 1)
            dstep(ts(gout[0:n, t, :], gout[0:n, t, :], 0.5, 0.5, ALU.mult, ALU.add))
            if t < 2:
                ins = tt(gout[:, t, :], gout[:, t, :], bank_of(("gout", t)), ALU.mult)
            else:
                for c in range(4):
                    gs_ = gout[0:NS, t, 128 * c:128 * c + 128]
                    ins = tt(gs_, gs_, bank_of(("gout", t))[NS * c:NS * c + NS, 0:128], ALU.mult)
            ins.then_inc(freed(("gout", t)), 1)
        dve.wait_ge(*filled("cols"))
        for t, (t0, n) in enumerate(TILES):
            src = bank_of("cols")[0:n, 32 * t:32 * t + 32].rearrange("p (q h) -> p q h", h=H)
            ins = cp(cols[0:n, t, :, :], src)
            steps["dve"] += 1
            ins.then_inc(dve_step, 1)
        dve.wait_ge(dve_step, steps["dve"])
        for t, (t0, n) in enumerate(TILES):
            ins = ts(cols[0:n, t, COL_G, :], cols[0:n, t, COL_G, :], -1.0, None, ALU.mult)
        ins.then_inc(freed("cols"), 1)
        dve.wait_ge(*taken("cols"))
        dve.wait_ge(*filled("dec"))
        dstep(cp(dec, bank_of("dec")[:, 0:H * NCH].rearrange("p (h c) -> p h c", h=H)))
        cp(gl, bank_of("dec")[:, H * NCH:2 * H * NCH].rearrange("p (h c) -> p h c", h=H)) \
            .then_inc(freed("dec"), 1)
        dve.wait_ge(*taken("dec"))

        def spread(c, t, n, width=DH):
            return bc(cols[0:n, t, c, :].unsqueeze(2), n, H, width)

        def heads(x):
            return x.rearrange("p (h v) -> p h v", h=H)

        for t, (t0, n) in enumerate(TILES):
            qx, kx, qwx, dx, sx = forms(t)
            dve.wait_ge(*filled(("qT", t)))
            tt(heads(q_t[0:n, t, :]), heads(q_t[0:n, t, :]), spread(COL_IW, t, n), ALU.mult).then_inc(sg("qw"), 1)
            dve.wait_ge(*filled(("kT", t)))
            tt(heads(k_t[0:n, t, :]), heads(k_t[0:n, t, :]), spread(COL_W, t, n), ALU.mult).then_inc(sg("kw"), 1)
            dve.wait_ge(*filled(("qwT", t)))
            if t == 1:
                dve.wait_ge(*filled(("num", 0, 1)))
            cp(qwx[:, 0:H * n], bank_of(("qwT", t))[:, 0:H * n]).then_inc(freed(("qwT", t)), 1)
            dve.wait_ge(*taken(("dl", t)))
            dve.wait_ge(*filled(("sc", t)))
            dstep(tt(sx[0:n, 0:H * n], bank_of(("sc", t))[0:n, 0:H * n], dx[0:n, 0:H * n], ALU.mult))
            mark(freed(("sc", t)), 1)
            mark(sg("sT"), 1)

            def update(t, c):
                ch = 2 * t + c
                for g in range(2):
                    dve.wait_ge(*filled(("Cu", t, c, g)))
                    for h in (2 * g, 2 * g + 1):
                        u = bank_of(("Cu", t, c, g))[:, (h % 2) * DA:(h % 2 + 1) * DA]
                        ins = stt(Cp[:, h, :], Cp[:, h, :], dec[:, h, ch:ch + 1], u, ALU.mult, ALU.add)
                    ins.then_inc(freed(("Cu", t, c, g)), 1)
                dve.wait_ge(*taken(("Cu", t, c, 1)))

            if t < 2:
                update(t, 0)
                update(t, 1)
                if t == 1:
                    cp(nst[:, NB * H:], Cp[:, :, DH]).then_inc(sg("Cp"), 1)
            else:
                for h in range(H):
                    C = Cs[h % 2]
                    dve.wait_ge(sg(f"Cs_in{h % 2}"), 16 * (h // 2 + 1))
                    cp(C[:, :, DH], vecT[:, V_N0 + h:V_N0 + NB * H:H])
                    if h:
                        dve.wait_ge(*filled(("Cs", h - 1, 2)))
                    if h == 0:
                        dve.wait_ge(*taken(("qwT", t)))
                    tt(qwm, bc(qwx[:, h * n:(h + 1) * n].unsqueeze(1), 128, NB, n),
                       cst[:, C_BROW:C_BROW + NB * n].rearrange("p (b l) -> p b l", b=NB), ALU.mult) \
                        .then_inc(sg("qwm"), 1)
                    tt(vblk, bc(v_a[0:n, t, h * DA:(h + 1) * DA].unsqueeze(1), n, NB, DA),
                       bc(cst[0:n, C_BCOL:C_BCOL + NB].unsqueeze(2), n, NB, DA), ALU.mult) \
                        .then_inc(sg("vblk"), 1)
                    for g, (b0, b1) in enumerate(((0, 3), (3, 6), (6, 8))):
                        dve.wait_ge(*filled(("Cs", h, g)))
                        for b in range(b0, b1):
                            u = bank_of(("Cs", h, g))[:, (b - b0) * DA:(b - b0 + 1) * DA]
                            ins = stt(C[:, b, :], C[:, b, :], dec[:, h, 4 + b:5 + b], u, ALU.mult, ALU.add)
                        ins.then_inc(freed(("Cs", h, g)), 1)
                    dve.wait_ge(*taken(("Cs", h, 2)))
                    cp(nst[:, h:NB * H:H], C[:, :, DH]).then_inc(sg("Cs"), 1)
            dve.wait_ge(sg("num_in"), t + 1)
            for g in range(2):
                ins = cp(hs4[0:n, 0, 2 * g:2 * g + 2],
                         bank_of(("num", t, g))[0:n, 0:2 * DA].rearrange("p (h v) -> p h v", h=2)[:, :, DH])
                ins.then_inc(freed(("num", t, g)), 1)
            dve.wait_ge(*taken(("num", t, 1)))
            dve.wait_ge(*taken(("num", t, 0)))
            dstep(stt(hs4[0:n, 1, :], hs4[0:n, 0, :], -1.0, hs4[0:n, 0, :], ALU.mult, ALU.max))
            dstep(tt(hs4[0:n, 1, :], hs4[0:n, 1, :], cols[0:n, t, COL_EN, :], ALU.max))
            dstep(dve.reciprocal(hs4[0:n, 1, :], hs4[0:n, 1, :]))
            dstep(tt(dx[0:n, 0:128 * H] if t < 2 else dT[0:n, :], num[0:n, :], num[0:n, :], ALU.mult))
            dstep(dve.tensor_reduce(hs4[0:n, 2, :], heads(dT[0:n, :]), AX.X, ALU.add))
            if t == 0:
                mark(sg("dT_free"), 1)
            dstep(tt(hs4[0:n, 2, :], hs4[0:n, 2, :], hs4[0:n, 1, :], ALU.mult))
            tt(hs4[0:n, 3, :], hs4[0:n, 2, :], hs4[0:n, 1, :], ALU.mult).then_inc(sg("ms"), 1)
            dve.wait_ge(sg("ms_r"), t + 1)
            dstep(tt(hs4[0:n, 5, :], hs4[0:n, 4, :], hs4[0:n, 1, :], ALU.mult))
            dstep(tt(heads(num[0:n, :]), heads(num[0:n, :]), bc(hs4[0:n, 5, :].unsqueeze(2), n, H, DH), ALU.mult))
            tt(num[0:n, :], num[0:n, :], mo[0:n, t, :], ALU.mult).then_inc(sg("ha"), 1)
            dve.wait_ge(*filled(("haT", t)))
            tt(brT[0][:, :, t0:t0 + n], bank_of(("haT", t))[:, 0:H * n].rearrange("p (h l) -> p h l", h=H),
               bc(vecT[:, V_ML:V_ML + H].unsqueeze(2), 128, H, n), ALU.mult).then_inc(freed(("haT", t)), 1)
        dve.wait_ge(*taken(("haT", 2)))
        dve.wait_ge(sg("Cs"), 4)
        mark(sg("nst"), 1)

        tl = tailT.rearrange("p c (b s) -> p c b s", s=HIST)
        dve.wait_ge(*taken(("cv", NCT - 1)))
        cp(tl[:, :, 0, :], cin[:, :, SEQ:SEQ + HIST])
        cp(tl[:, :, 1:, :], cis.rearrange("p c (b s) -> p c b s", b=NB)[:, :, :, DS:DS + HIST]) \
            .then_inc(sg("tailT"), 1)
        dve.wait_ge(*filled(("Cs", H - 1, 2)))
        for g in range(3):
            for j in range(CW):
                for c in range(4 * g, 4 * g + 4):
                    w = cwT[:, c, NB * HIST + j:NB * HIST + j + 1]
                    xp = cin[:, c, j:j + SEQ]
                    xs = cis[:, c, :].rearrange("p (b s) -> p b s", b=NB)[:, :, j:j + DS]
                    op_, os_ = cvT[:, c, 0:SEQ], cvT[:, c, SEQ:T].rearrange("p (b s) -> p b s", b=NB)
                    if j == 0:
                        ts(op_, xp, w, None, ALU.mult)
                        ins = ts(os_, xs, w, None, ALU.mult)
                    else:
                        stt(op_, xp, w, op_, ALU.mult, ALU.add)
                        ins = stt(os_, xs, w, os_, ALU.mult, ALU.add)
                if j < CW - 1:
                    dstep(ins)
            ins.then_inc(sg("conv"), 1)
        for g in range(3):
            if g == 2:
                pass
            e = stmp[:, g % 2, :]
            v = cvT[:, 4 * g:4 * g + 4, :].rearrange("p c t -> p (c t)")
            dve.wait_ge(sg("silu_e"), g + 1)
            dstep(ts(e, e, 0.5, 0.5, ALU.mult, ALU.add))
            tt(v, v, e, ALU.mult).then_inc(sg("cvT"), 1)
            dve.wait_ge(sg("cvT"), g + 1)

        dve.memset(Sp, 0.0).then_inc(sg("S0"), 1)
        for t, (t0, n) in enumerate(TILES):
            dve.wait_ge(*taken(("raw", t, 2)))
            q, k, v = (heads(raw[0:n, j, :]) for j in range(3))
            dstep(tt(kd[0:n, :], raw[0:n, 0, :], raw[0:n, 0, :], ALU.mult))
            dstep(tt(kbg[0:n, :], raw[0:n, 1, :], raw[0:n, 1, :], ALU.mult))
            dstep(dve.tensor_reduce(hs4[0:n, 0, :], heads(kd[0:n, :]), AX.X, ALU.add))
            dve.tensor_reduce(hs4[0:n, 1, :], heads(kbg[0:n, :]), AX.X, ALU.add).then_inc(sg("gss"), 1)
            dve.wait_ge(sg("gss_r"), t + 1)
            s4 = lambda j: hs4[0:n, j, :]
            wide = lambda x: bc(x.unsqueeze(2), n, H, DH)
            dstep(tt(s4(4), s4(3), cols[0:n, t, COL_B, :], ALU.mult))
            dstep(tt(s4(8), s4(4), cols[0:n, t, COL_EG, :], ALU.mult))
            dstep(tt(s4(9), s4(3), cols[0:n, t, COL_KD, :], ALU.mult))
            dstep(ts(s4(2), s4(2), QSCALE, None, ALU.mult))
            dstep(tt(s4(10), s4(2), cols[0:n, t, COL_EG, :], ALU.mult))
            tt(heads(kbg[0:n, :]), k, wide(s4(8)), ALU.mult)
            tt(heads(kd[0:n, :]), k, wide(s4(9)), ALU.mult)
            tt(heads(kb[0:n, :]), k, wide(s4(4)), ALU.mult)
            tt(heads(qd[0:n, :]), q, wide(s4(10)), ALU.mult)
            tt(v, v, spread(COL_B, t, n), ALU.mult).then_inc(sg("gv"), 1)
            dve.wait_ge(sg("gv"), t + 1)
            tt(k, k, wide(s4(3)), ALU.mult).then_inc(sg("gq"), 1)
            tt(q, q, wide(s4(2)), ALU.mult).then_inc(sg("gq"), 1)
            mark(sg("gq"), 1)
            mark(sg("gq"), 1)
            dve.wait_ge(*filled(("kbT", t)))
            cp(kbT[:, 0:H * n], bank_of(("kbT", t))[:, 0:H * n]).then_inc(freed(("kbT", t)), 1)
            dve.wait_ge(*filled(("qdT", t)))
            cp(qdT[:, 0:H * n], bank_of(("qdT", t))[:, 0:H * n]).then_inc(freed(("qdT", t)), 1)
            dve.wait_ge(*taken(("dG", t)))
            dve.wait_ge(*filled(("KK", t)))
            tt(AT[0:n, 0:H * n], bank_of(("KK", t))[0:n, 0:H * n], dG[0:n, 0:H * n], ALU.mult) \
                .then_inc(freed(("KK", t)), 1)
            dve.wait_ge(*filled(("QK", t)))
            tt(QKT[0:n, 0:H * n], bank_of(("QK", t))[0:n, 0:H * n], dG[0:n, 0:H * n], ALU.mult) \
                .then_inc(freed(("QK", t)), 1)
            dve.wait_ge(*taken(("QK", t)))
            blocks = lambda x: x[0:n, 0:H * n].rearrange("p (h l) -> p h l", h=H)
            idb = bc(ident[0:n, 0:n].unsqueeze(1), n, H, n)
            nl = 2 if t == 2 else LEVELS
            for lev in range(nl):
                mk_ = cst[0:n, C_LVL + 128 * lev:C_LVL + 128 * lev + n]
                tt(blocks(dG), blocks(AT), bc(mk_.unsqueeze(1), n, H, n), ALU.mult).then_inc(sg("ATk"), 1)
                dve.wait_ge(sg("ATk"), lv(t, lev) + 1)
                if lev == 0:
                    dstep(tt(blocks(Um), idb, blocks(dG), ALU.subtract))
                    dve.wait_ge(*filled(("X", t, 0)))
                    tt(blocks(Tm), idb, bank_of(("X", t, 0))[0:n, 0:H * n].rearrange("p (h l) -> p h l", h=H),
                       ALU.subtract).then_inc(freed(("X", t, 0)), 1)
                    dve.wait_ge(*taken(("X", t, 0)))
                    continue
                if lev < nl - 1:
                    dve.wait_ge(*filled(("Y", t, lev)))
                    tt(Tm[0:n, 0:H * n], Tm[0:n, 0:H * n], bank_of(("Y", t, lev))[0:n, 0:H * n], ALU.subtract) \
                        .then_inc(freed(("Y", t, lev)), 1)
                    dve.wait_ge(*taken(("Y", t, lev)))
                dve.wait_ge(*filled(("YT", t, lev)))
                tt(Um[0:n, 0:H * n], Um[0:n, 0:H * n], bank_of(("YT", t, lev))[0:n, 0:H * n], ALU.subtract) \
                    .then_inc(freed(("YT", t, lev)), 1)
                dve.wait_ge(*taken(("YT", t, lev)))
            if t < 2:
                for c in range(2):
                    ch = 2 * t + c
                    dve.wait_ge(*filled(("go", t, c)))
                    dve.wait_ge(*filled(("So", t, c)))
                    for h in range(H):
                        hv = slice(128 * h, 128 * h + 128)
                        ins = stt(Sp[:, hv], Sp[:, hv], gl[:, h, ch:ch + 1], bank_of(("So", t, c))[:, hv],
                                  ALU.mult, ALU.add)
                    ins.then_inc(freed(("So", t, c)), 1)
                    dve.wait_ge(*taken(("So", t, c)))
                if t == 1:
                    mark(sg("Spout"), 1)
            else:
                dve.wait_ge(*taken(("wT", t)))
                for h in range(H):
                    if h:
                        dve.wait_ge(*filled(("So2", h - 1, 1)))
                    dve.wait_ge(sg(f"Ss_in{h % 2}"), 16 * (h // 2 + 1))
                    brow = cst[:, C_BROW:C_BROW + NB * n].rearrange("p (b l) -> p b l", b=NB)
                    tt(qdm, bc(qdT[:, h * n:(h + 1) * n].unsqueeze(1), 128, NB, n), brow, ALU.mult)
                    tt(nwm, bc(kbT[:, h * n:(h + 1) * n].unsqueeze(1), 128, NB, n), brow, ALU.mult) \
                        .then_inc(sg("nwm"), 1)
                    dve.wait_ge(*taken(("vn2", h)))
                    tt(vnb, bc(vn[0:n, 128 * h:128 * h + 128].unsqueeze(1), n, NB, DH),
                       bc(cst[0:n, C_BCOL:C_BCOL + NB].unsqueeze(2), n, NB, DH), ALU.mult).then_inc(sg("vnb"), 1)
                    for g in range(2):
                        dve.wait_ge(*filled(("So2", h, g)))
                        for b in range(4 * g, 4 * g + 4):
                            ins = stt(Ss[h % 2][:, b, :], Ss[h % 2][:, b, :], gl[:, h, 4 + b:5 + b],
                                      bank_of(("So2", h, g))[:, 128 * (b - 4 * g):128 * (b - 4 * g) + 128],
                                      ALU.mult, ALU.add)
                        ins.then_inc(freed(("So2", h, g)), 1)
                    mark(sg("Ssd"), 1)
                    dve.wait_ge(sg("Ssd"), h + 1)
            dve.wait_ge(*taken(("go", t, 1) if t < 2 else ("go2", H - 1)))
            dstep(tt(AT[0:n, :], Xm[0:n, :], Xm[0:n, :], ALU.mult))
            dve.tensor_reduce(hs4[0:n, 5, :], heads(AT[0:n, :]), AX.X, ALU.add).then_inc(sg("gs"), 1)
            dve.wait_ge(sg("gs_r"), t + 1)
            dstep(tt(heads(kb[0:n, :]), heads(Xm[0:n, :]), wide(s4(7)), ALU.mult))
            tt(kb[0:n, :], kb[0:n, :], gout[0:n, t, :], ALU.mult).then_inc(sg("hb"), 1)
            dve.wait_ge(*filled(("hbT", t)))
            ts(brT[1][:, :, t0:t0 + n], bank_of(("hbT", t))[:, 0:H * n].rearrange("p (h l) -> p h l", h=H),
               vecT[:, V_GD:V_GD + 1], None, ALU.mult).then_inc(freed(("hbT", t)), 1)

        dve.wait_ge(*taken(("hbT", 2)))
        dve.wait_ge(*taken(("xqT", 2)))
        tt(qm.rearrange("p h (b l) -> p h b l", b=NB), bc(xqT[:, :, SEQ:T].unsqueeze(2), 128, H, NB, NS),
           bc(cst[:, C_BROW:C_BROW + NB * NS].rearrange("p (b l) -> p b l", b=NB).unsqueeze(1),
              128, H, NB, NS), ALU.mult).then_inc(sg("qm"), 1)
        for i in range(3):
            n = NS if i == 2 else 128
            names = [("xs", i, g) if i < 2 else ("ss", g) for g in range(2)]
            if i == 2:
                for b in range(NB):
                    dve.wait_ge(*filled(("KbT", b, 0)))
                    if b >= 2:
                        dve.wait_ge(*filled(("KbT", b - 1, 1)))
                    cp(KTb[b % 2][:, 0:2, :].rearrange("p h m -> p (h m)"), bank_of(("KbT", b, 0))) \
                        .then_inc(freed(("KbT", b, 0)), 1)
            for g in range(2):
                dve.wait_ge(*filled(names[g]))
                ins = dve.tensor_reduce(negmax[0:n, 2 * g:2 * g + 2],
                                        bank_of(names[g])[0:n, :].rearrange("p (h m) -> p h m", h=2),
                                        AX.X, ALU.max, negate=True)
            ins.then_inc(sg("negmax"), 1)
            dve.wait_ge(*taken(names[1]))
            dstep(dve.reciprocal(psumx[0:n, :], psumx[0:n, :]))
            tt(pr[0:n], pr[0:n], bc(psumx[0:n, :].unsqueeze(2), n, H, MEM), ALU.mult).then_inc(sg("pr"), 1)
            if i == 0:
                dve.wait_ge(sg("Ss_out1"), 32)
            if i < 2:
                if i:
                    dve.wait_ge(*filled(("hcT", 0)))
                dve.wait_ge(*filled(("prT", i, 1)))
                cp(prT[:, 1, :], bank_of(("prT", i, 1))).then_inc(freed(("prT", i, 1)), 1)
            else:
                dve.wait_ge(*filled("spT"))
                cp(spT, bank_of("spT")[:, 0:2 * H * NS].rearrange("p (m c) -> p m c", m=2)) \
                    .then_inc(freed("spT"), 1)
        for b in range(NB):
            dve.wait_ge(*filled(("hcs", b)))
            cp(brT[2][:, :, SEQ + DS * b:SEQ + DS * b + DS],
               bank_of(("hcs", b))[:, 0:DS * H].rearrange("p (h l) -> p h l", h=H)) \
                .then_inc(freed(("hcs", b)), 1)

        step = 0
        for j in range(3):
            for nn in range(2):
                for t, (t0, n) in enumerate(TILES):
                    wd = 512 if t < 2 else 128
                    s = sig[:, step % 2, 0:wd]
                    mx = mixed[:, t, 512 * nn:512 * nn + 512] if t < 2 else mixs[:, nn, :]
                    dve.wait_ge(*taken(("mg", j, nn, t)))
                    dve.wait_ge(*filled(("mb", j, nn, t)))
                    o = bank_of(("mb", j, nn, t))[:, 0:wd]
                    dst = mx if j == 0 else s
                    stt(dst, s, 1.0, o, ALU.add, ALU.mult).then_inc(freed(("mb", j, nn, t)), 1)
                    dve.wait_ge(*taken(("mb", j, nn, t)))
                    if j:
                        dstep(tt(mx, mx, s, ALU.add))
                    mark(sg("sig_read"), 1)
                    step += 1
        for t in range(3):
            mark(sg("mixed"), 1)
        for t, (t0, n) in enumerate(TILES):
            dve.wait_ge(*filled(("mixT", t, 1)))
            ts(mixT[:, 4:8, t0:t0 + n], bank_of(("mixT", t, 1))[:, 0:4 * n].rearrange("p (c l) -> p c l", c=4),
               0.5, None, ALU.mult) \
                .then_inc(freed(("mixT", t, 1)), 1)
        dve.wait_ge(sg("x2_in"), 48)
        for nn in range(2):
            for t, (t0, n) in enumerate(TILES):
                name = (("out", nn), t)
                dve.wait_ge(*filled(name))
                if t < 2:
                    xx = x2[:, t, 512 * nn:512 * nn + 512]
                    ins = tt(xx, xx, bank_of(name), ALU.add)
                else:
                    for c in range(4):
                        xx = x2[0:NS, t, 512 * nn + 128 * c:512 * nn + 128 * c + 128]
                        ins = tt(xx, xx, bank_of(name)[NS * c:NS * c + NS, 0:128], ALU.add)
                ins.then_inc(freed(name), 1)
        for t, (t0, n) in enumerate(TILES):
            dve.wait_ge(*taken((("out", 1), t)))
            mark(sg("x2"), 1)

        for t, (t0, n) in enumerate(TILES):
            dve.wait_ge(sg("rst"), t + 1)
            ts(h2p[0:n, t, :].rearrange("p (c f) -> p f c", c=KD), x2[0:n, t, :].rearrange("p (f c) -> p f c", c=KD),
               rst[0:n, t:t + 1], None, ALU.mult).then_inc(sg("h2p"), 1)
        for t, (t0, n) in enumerate(TILES):
            for hf in range(2):
                dve.wait_ge(*filled(("h2T", t, hf)))
                tt(h2T[:, 4 * hf:4 * hf + 4, t0:t0 + n],
                   bank_of(("h2T", t, hf))[:, 0:4 * n].rearrange("p (c l) -> p c l", c=4),
                   bc(gffn[:, 4 * hf:4 * hf + 4].unsqueeze(2), 128, 4, n), ALU.mult) \
                    .then_inc(freed(("h2T", t, hf)), 1)
        dve.wait_ge(*filled("lgT"))
        ts(lgT[0:20, :], bank_of("lgT")[0:20, 0:T], brt, None, ALU.add).then_inc(freed("lgT"), 1)
        dstep(dve.memset(LG, 0.0))
        dve.wait_ge(*filled("lg"))
        for t, (t0, n) in enumerate(TILES):
            ins = cp(LG[0:n, t, :], bank_of("lg")[0:n, 20 * t:20 * t + 20])
        ins.then_inc(freed("lg"), 1)
        dve.wait_ge(*taken("lg"))
        first = cst[:, C_FIRST:C_FIRST + 3 * EG]
        flat = lambda x: x.rearrange("p t e -> p (t e)")
        w4 = lambda x: bc(x.unsqueeze(2), 128, 3, 4)

        def best(o, x, m):
            dstep(dve.tensor_reduce(m, x, AX.X, ALU.max))
            dstep(tt(le4[:, :, 0:4], x, w4(m), ALU.is_equal))
            dstep(cp(le4[:, :, 4:8], le4[:, :, 0:4]))
            dstep(cp(flat(oh2), le4[:, :, 4:8]))
            dstep(dve.tensor_tensor_scan(le12, first, flat(oh2), 0.0, ALU.mult, ALU.add))
            dstep(stt(flat(o), le12, 1.0, flat(oh2), ALU.is_equal, ALU.mult))

        best(oh, LG[:, :, 0:G], rt1[:, 0, :])
        tt(rtmp, LG[:, :, 0:G], w4(rt1[:, 0, :]), ALU.subtract).then_inc(sg("lge"), 1)
        le = LG[:, :, G:20]
        lesel = rkm[:, :, 0:4]
        for g in range(G):
            dstep(tt(le4[:, :, 4 * g:4 * g + 4], le[:, :, 4 * g:4 * g + 4], bc(oh[:, :, g:g + 1], 128, 3, 4), ALU.mult))
        dstep(tt(le4[:, :, 0:8], le4[:, :, 0:8], le4[:, :, 8:16], ALU.add))
        dstep(tt(lesel, le4[:, :, 0:4], le4[:, :, 4:8], ALU.add))
        best(oh1, lesel, rt1[:, 1, :])
        dstep(stt(lesel, oh1, NEG, lesel, ALU.mult, ALU.add))
        best(oh3, lesel, rt1[:, 2, :])
        tt(rt1[:, 4, :], rt1[:, 2, :], rt1[:, 1, :], ALU.subtract).then_inc(sg("top"), 1)
        dve.wait_ge(sg("lge_r"), 1)
        dstep(dve.tensor_reduce(rt1[:, 3, :], rtmp, AX.X, ALU.add))
        dstep(dve.reciprocal(rt1[:, 3, :], rt1[:, 3, :]))
        dve.wait_ge(sg("top_r"), 1)
        dstep(ts(rt1[:, 6, :], rt1[:, 5, :], 1.0, None, ALU.add))
        dstep(dve.reciprocal(rt1[:, 6, :], rt1[:, 6, :]))
        dstep(tt(rt1[:, 6, :], rt1[:, 6, :], rt1[:, 3, :], ALU.mult))
        dstep(tt(rt1[:, 7, :], rt1[:, 6, :], rt1[:, 5, :], ALU.mult))
        dstep(tt(rtmp, oh1, w4(rt1[:, 6, :]), ALU.mult))
        dstep(tt(le4[:, :, 0:4], oh3, w4(rt1[:, 7, :]), ALU.mult))
        dstep(tt(rtmp, rtmp, le4[:, :, 0:4], ALU.add))
        dstep(tt(oh1, oh1, oh3, ALU.add))
        for g in range(G):
            tt(cmb[:, :, 4 * g:4 * g + 4], rtmp, bc(oh[:, :, g:g + 1], 128, 3, 4), ALU.mult)
            ins = tt(msk[:, :, 4 * g:4 * g + 4], oh1, bc(oh[:, :, g:g + 1], 128, 3, 4), ALU.mult)
        ins.then_inc(sg("msk"), 1)
        dve.wait_ge(sg("msk"), 1)
        dve.wait_ge(*filled("rank"))
        dstep(dve.memset(rkm, 0.0))
        for t, (t0, n) in enumerate(TILES):
            dstep(stt(rkm[0:n, t, :], bank_of("rank")[0:n, E * t:E * t + E], 1.0, msk[0:n, t, :], ALU.add, ALU.mult))
        dstep(dve.tensor_reduce(rt1[0:1, 11, 0:1], bank_of("rank")[0:1, 3 * E:4 * E], AX.X, ALU.max))
        cp(flag[0:1, 0:1], rt1[0:1, 11, 0:1]).then_inc(sg("flag"), 1)
        mark(freed("rank"), 1)

        def choices(p):
            k = 0

            def then(ins):
                nonlocal k
                k += 1
                ins.then_inc(sg("choice"), 1)
                dve.wait_ge(sg("choice"), 7 * p + k)

            then(ts(le4, rkm, -1.0, None, ALU.add))
            for t, (t0, n) in enumerate(TILES):
                P4 = Pm[0:n, t, :].rearrange("p (e j) -> p e j", e=E)
                W4 = Pw[0:n, t, :].rearrange("p (e j) -> p e j", e=E)
                then(tt(P4, bc(cst[0:n, C_IOTA:C_IOTA + SLOTS].unsqueeze(1), n, E, SLOTS),
                        bc(le4[0:n, t, :].unsqueeze(2), n, E, SLOTS), ALU.is_equal))
                then(tt(W4, P4, bc(cmb[0:n, t, :].unsqueeze(2), n, E, SLOTS), ALU.mult))
            mark(sg("Pm"))

        choices(0)
        mark(sg("pws_free"), 2)
        mark(sg("ea_free"), 2)
        mark(sg("act_free"), 2)
        mark(sg("outp_free"), 1)

        def group(p, g):
            it = 4 * p + g
            for j in range(4):
                dve.wait_ge(*gfilled("hg", j, p, g))
                tt(hg[:, 2 * j:2 * j + 2, :], gbank("hg", j).rearrange("p (c l) -> p c l", c=2),
                   bc(gffn[:, 2 * j:2 * j + 2].unsqueeze(2), 128, 2, 256), ALU.mult).then_inc(gfree("hg", j), 1)
            for pr_ in range(2):
                for e in (2 * pr_, 2 * pr_ + 1):
                    ee, ab = ea[:, e % 2, :], actb[:, e % 2, :]
                    dve.wait_ge(sg("ea"), it * 4 + (e + 1))
                    stt(ee, ee, 1.0, gbank("gu", e)[:, 0:256], ALU.add, ALU.mult).then_inc(sg("silu"), 1)
                    dve.wait_ge(sg("silu"), it * 4 + (e + 1))
                    stt(ab, ee, 0.5, gbank("gu", e)[:, 256:512], ALU.mult, ALU.mult).then_inc(sg("act"), 1)
                    dve.wait_ge(sg("act"), it * 4 + (e + 1))
                    mark(gfree("gu", e), 1)
                    mark(sg("ea_free"), 1)
                if pr_ == 1:
                    add_y(0, p, g)
                dve.wait_ge(*gfilled("dn", 2 * pr_ + 1, p, g))
                if pr_ == 1:
                    pass
                dve.wait_ge(sg("outp_free"), it * 2 + (pr_ + 1))
                cp(outp[:, 512:1024], gbank("dn", 2 * pr_ + 1)).then_inc(gfree("dn", 2 * pr_ + 1), 1)
            add_y(1, p, g)
            mark(sg("act_free"), 4)
            mark(sg("pws_free"), 2)

        def add_y(pr_, p, g):
            it = 4 * p + g
            for t, (t0, n) in enumerate(TILES):
                for nn in range(2):
                    j = 6 * pr_ + 2 * t + nn
                    dve.wait_ge(*gfilled("y", j, p, g))
                    xx = x2[0:n, t, 512 * nn:512 * nn + 512]
                    ins = tt(xx, xx, gbank("y", j)[0:n, :], ALU.add)
                    ins.then_inc(gfree("y", j), 1)
            mark(sg("outp_free"), 1)

        with dve.Fori(0, G) as g:
            group(0, g)
        dve.wait_ge(sg("flag"), 1)
        most = dve.value_load(flag[0:1, 0:1], min_val=0, max_val=T)
        with dve.If(most > SLOTS):
            with dve.Fori(1, PASSES) as p:
                for e in (2, 3):
                    dve.wait_ge(*moved("dn", e, p - 1, G - 1))
                dve.wait_ge(*moved("y", 11, p - 1, G - 1))
                ts(rkm, rkm, -float(SLOTS), None, ALU.add).then_inc(sg("shift"), 1)
                dve.wait_ge(sg("shift"), p)
                choices(p)
                with dve.Fori(0, G) as g:
                    group(p, g)
        mark(sg("x3"), 1)
        dve.wait_ge(sg("gfin_in"), 16)
        for t, (t0, n) in enumerate(TILES):
            dve.wait_ge(sg("rst"), 4 + t)
            stt(x2[0:n, t, :], x2[0:n, t, :], rst[0:n, t:t + 1], gfin[0:n, :], ALU.mult, ALU.mult) \
                .then_inc(sg("y"), 1)

    ctx.close()


_OUTS = [("y_prompt", (1, SEQ, D)), ("y_sample", (NB, DS, D)),
         ("mem_k", (1, 1, MEM, H, DH)), ("mem_v", (1, 1, MEM, H, DH)),
         ("C_p", (1, 1, H, DH, DH)), ("n_p", (1, 1, H, DH)), ("m_p", (1, 1, H)), ("S_p", (1, 1, H, DH, DH)),
         ("conv_p", (1, 1, HIST, CCH)),
         ("C_s", (1, NB, H, DH, DH)), ("n_s", (1, NB, H, DH)), ("m_s", (1, NB, H)), ("S_s", (1, NB, H, DH, DH)),
         ("conv_s", (1, NB, HIST, CCH))]


def kernel(**inputs):
    import concourse.bacc as bacc
    from concourse.bass_utils import run_bass_kernel_spmd

    nc = bacc.Bacc("TRN2", target_bir_lowering=False, num_devices=1)
    arrays, a, out = {}, {}, {}
    for name in inputs:
        x = np.ascontiguousarray(inputs[name])
        arrays[f"in_{name}"] = x
        a[name] = nc.dram_tensor(f"in_{name}", x.shape, mybir.dt.from_np(x.dtype), kind="ExternalInput").ap()
    arrays["in_table"] = constants()
    a["table"] = nc.dram_tensor("in_table", (128, C_ALL), F32, kind="ExternalInput").ap()
    for name, shape in _OUTS:
        out[name] = nc.dram_tensor(f"out_{name}", shape, F32, kind="ExternalOutput").ap()
    build(nc, a, out)
    r = run_bass_kernel_spmd(nc, [arrays], core_ids=[0])
    return tuple(r.results[0][f"out_{name}"] for name, _ in _OUTS)
```

```python
from contextlib import ExitStack

import numpy as np
import concourse.bass as bass
from concourse import mybir

F32 = mybir.dt.float32
I32 = mybir.dt.int32
ALU = mybir.AluOpType
ACT = mybir.ActivationFunctionType
AX = mybir.AxisListType

D = 1024
KD = D // 128
SEQ, NB, DS = 256, 8, 4
NS = NB * DS
T = SEQ + NS
TILES = [(0, 128), (128, 128), (SEQ, NS)]
H, DH = 4, 128
W = H * DH
DA = DH + 1
L = 64
NCH = SEQ // L + NB
CW = 4
CCH = 3 * W
NCT = CCH // 128
HIST = CW - 1
MEM = 256
G, EG = 4, 4
E = G * EG
FE = 512
SLOTS = 64
EPS = 1e-6
NEG = -1e30
RING, UNIT = 6, 4096
RING0 = 4
NSCRAP = 40
ARENA, SMALL = 19040, 1600
QSCALE = DH ** -0.5
PASSES = -(-T // SLOTS)
LEVELS = 6

O_Q, O_K, O_V = 0, W, 2 * W
O_IF = 3 * W
O_MO = O_IF + 2 * H
O_GQKV = O_MO + W
O_GAB = O_GQKV + CCH
O_GOUT = O_GAB + 2 * H
O_XQ = O_GOUT + W
O_GATE = O_XQ + W

C_ID, C_NEGP, C_NEGS, C_LVL = 0, 128, 256, 288
C_SEL = C_LVL + LEVELS * 128
C_BROW = C_SEL + H * 128
C_BCOL = C_BROW + NB * NS
C_IOTA = C_BCOL + NB
C_TRI = C_IOTA + SLOTS
C_FIRST = C_TRI + 128
C_N = C_FIRST + 3 * EG
C_RST = C_N
C_ALL = C_RST + T


def constants():
    t = np.zeros((128, C_ALL), np.float32)
    s, l = np.arange(128)[:, None], np.arange(128)[None, :]
    t[:, C_ID:C_ID + 128] = s == l
    t[:, C_NEGP:C_NEGP + 128] = np.where((s // L == l // L) & (s <= l), 0, NEG)
    t[:NS, C_NEGS:C_NEGS + NS] = np.where((s // DS == l // DS) & (s <= l), 0, NEG)[:NS, :NS]
    for k in range(LEVELS):
        n = 1 << k
        t[:, C_LVL + 128 * k:C_LVL + 128 * (k + 1)] = (s // n + 1 == l // n) & (l // n % 2 == 1)
    for h in range(H):
        t[h, C_SEL + 128 * h:C_SEL + 128 * (h + 1)] = 1
    for b in range(NB):
        t[:, C_BROW + NS * b:C_BROW + NS * (b + 1)] = np.arange(NS) // DS == b
        t[:NS, C_BCOL + b] = np.arange(NS) // DS == b
    t[:, C_IOTA:C_IOTA + SLOTS] = np.arange(SLOTS)
    t[:, C_TRI:C_TRI + 128] = s < l
    n = np.arange(T)
    t[:, C_RST:C_RST + T] = np.where(n < SEQ, n % L != 0, n % DS != 0)
    t[:, C_FIRST:C_FIRST + 3 * EG] = np.arange(3 * EG) % EG != 0
    return t


def bc(ap, *shape):
    return ap.to_broadcast(list(shape))


def build(nc, a, out):
    ctx = ExitStack()

    def sb(name, *shape):
        return ctx.enter_context(nc.sbuf_tensor(name, list(shape), F32))

    def sem(name):
        return ctx.enter_context(nc.semaphore(name))

    ring = sb("ring", 128, RING, UNIT)
    cst = sb("cst", 128, C_N)
    ones = sb("ones", 128, 128)
    hT = sb("hT", 128, KD, T)
    brT = [sb(f"brT{j}", 128, H, T) for j in range(3)]
    small = sb("small", 128, SMALL)
    arena = sb("arena", 128, ARENA)
    flag = ctx.enter_context(nc.sbuf_tensor("flag", [1, 1], I32))
    PS = ctx.enter_context(nc.psum_tensor("PS", [128, 8, 512], F32))

    ident = cst[:, C_ID:C_ID + 128]
    at = [0]

    def tiny(*shape):
        n = int(np.prod(shape[1:]))
        v = small[0:shape[0], at[0]:at[0] + n]
        at[0] += n
        assert at[0] <= SMALL
        if len(shape) == 3:
            v = v.rearrange("p (a b) -> p a b", b=shape[2])
        if len(shape) == 4:
            v = v.rearrange("p (a b c) -> p a b c", b=shape[2], c=shape[3])
        return v

    def place(start, *shape):
        n = int(np.prod(shape[1:]))
        assert start + n <= ARENA, (start, shape)
        v = arena[0:shape[0], start:start + n]
        if len(shape) == 3:
            v = v.rearrange("p (a b) -> p a b", b=shape[2])
        if len(shape) == 4:
            v = v.rearrange("p (a b c) -> p a b c", b=shape[2], c=shape[3])
        return v, start + n

    NV = 2 * KD + H + 1 + NB * H
    vecT = tiny(128, NV)
    tailT = tiny(128, NCT, HIST * (NB + 1))
    V_MIX, V_MEM, V_ML, V_GD, V_N0 = 0, KD, 2 * KD, 2 * KD + H, 2 * KD + H + 1
    cwT = tiny(128, NCT, NB * HIST + CW)
    ss = tiny(128, 5)
    rstd = tiny(128, 5)
    gffn = tiny(128, KD)
    bias4 = tiny(H, 5)
    brt = tiny(20, 1)
    m0 = tiny(H, NB)
    dec = tiny(128, H, NCH)
    gl = tiny(128, H, NCH)
    cols = tiny(128, 3, 8, H)
    hs4 = tiny(128, 12, H)
    nst = tiny(128, NB * H + H)
    rst = tiny(128, 3)
    negmax = tiny(128, H)
    psumx = tiny(128, H)
    COL_RS, COL_W, COL_IW, COL_EN, COL_G, COL_B, COL_EG, COL_KD = range(8)

    full = [sem(f"full{b}") for b in range(8)]
    free = [sem(f"free{b}") for b in range(8)]
    ring_full = [sem(f"ring_full{s}") for s in range(RING)]
    ring_used = sem("ring_used")
    uses, count = {}, [0] * 8

    def filled(name):
        b, n = uses[name]
        return full[b], n + 1

    def bank_of(name):
        return PS[:, uses[name][0], :]

    def freed(name):
        return free[uses[name][0]]

    dve_step, act_step, pool_step = sem("dve_step"), sem("act_step"), sem("pool_step")
    steps = {"dve": 0, "act": 0, "pool": 0}

    def dstep(ins):
        steps["dve"] += 1
        ins.then_inc(dve_step, 1)
        nc.vector.wait_ge(dve_step, steps["dve"])

    def astep(ins):
        steps["act"] += 1
        ins.then_inc(act_step, 1)
        nc.scalar.wait_ge(act_step, steps["act"])


    S = {}

    def sg(name):
        if name not in S:
            S[name] = sem(name)
        return S[name]

    def taken(name):
        b, n = uses[name]
        return free[b], n + 1

    def lv(t, k):
        return LEVELS * t + k

    def spare(start, *shape):
        n = int(np.prod(shape[1:]))
        assert start + n <= (RING - RING0) * UNIT
        v = ring[0:shape[0], RING0:RING, :].rearrange("p a b -> p (a b)")[:, start:start + n]
        if len(shape) == 3:
            v = v.rearrange("p (a b) -> p a b", b=shape[2])
        return v, start + n

    KT, p = place(0, 128, H, MEM)
    memv, p = place(p, 128, 2, W)
    A0 = p
    xin, p = place(5828, 128, 5, D)
    memT, p = place(p, 128, KD, MEM)
    junk, p = place(p, 128, D)
    wg, p = place(p, 128, KD, 16)
    vrow, p = place(p, NV, 128)
    crow, p = place(p, NB * HIST + CW, CCH)
    memk, p = place(p, 128, 2, W)
    cin, p = place(A0, 128, NCT, HIST + SEQ)
    cis, p = place(p, 128, NCT, NB * (HIST + DS))
    B0 = p
    q_t, p = place(p, 128, 3, W)
    k_t, p = place(p, 128, 3, W)
    v_a, p = place(p, 128, 3, H * DA)
    mo, p = place(p, 128, 3, W)
    gout, p = place(p, 128, 3, W)
    M0 = p
    qTt, p = place(p, 128, W)
    kTt, p = place(p, 128, W)
    qwTt, p = place(p, 128, W)
    dT, p = place(p, 128, W)
    sT, p = place(p, 128, W)
    num, p = place(p, 128, W)
    Cp, p = place(p, 128, H, DA)
    Cs0, p = place(p, 128, NB, DA)
    qwm, p = place(p, 128, NB, NS)
    sform, p = place(p, 128, 5, H * NS)
    nrow = sform[0:NB * H + H, 0, :]
    rset, _ = place(p - 640, H, T)
    cvT, p = spare(0, 128, NCT, T)
    stmp, _ = spare(p, 128, 2, 4 * T)
    kT, p = spare(p, 128, W)
    qT, p = spare(p, 128, W)
    qdT, p = spare(p, 128, W)
    kbT, p = spare(p, 128, W)
    QKT, p = spare(p, 128, W)
    Ss1, p = spare(p, 128, NB, DH)
    Cs1, p = spare(p, 128, NB, DA)
    vblk, _ = spare(0, NS, NB, DA)
    Cs = [Cs0, Cs1]
    tails, _ = place(M0, HIST * (NB + 1), CCH)
    mixed, p = place(B0, 128, 2, D)
    mixs, p = place(p, 128, 2, 4 * NS)
    sig, p = place(p, 128, 2, W)
    B1 = p
    mixT, p = place(p, 128, KD, T)
    xq, p = place(A0, 128, 3, W)
    xqT, p = place(p, 128, H, T)
    pr, p = place(p, 128, H, MEM)
    assert p <= B0
    spT, _ = place(A0, 128, 2, NB * 4 * NS)
    hcs, _ = place(A0 + 2 * NB * 4 * NS, 128, 128)
    prT, p = place(B1, 128, 2, W)
    qm, p = place(p, 128, H, NB * NS)
    assert p <= M0 - 3 * W
    Kb, Vb, KTb = [None, None], [None, None], [None, None]
    Kb[0], p = place(M0 + 3 * W, 128, 2, W)
    Vb[0], p = place(p, 128, 2, W)
    Kb[1], p = place(p, 128, 2, W)
    KTb[1], p = place(B0, 128, H, MEM)
    Vb[1], p = place(p, 128, 2, W)
    KTb[0], p = place(p, 128, H, MEM)
    assert p <= B1
    raw, p = place(A0, 128, 3, W)
    kb, p = place(p, 128, W)
    kbg, p = place(p, 128, W)
    kd, p = place(p, 128, W)
    qd, p = place(p, 128, W)
    dG, p = place(M0, 128, W)
    AT, p = place(p, 128, W)
    Tm, p = place(p, 128, W)
    Um, p = place(p, 128, W)
    Xm, p = place(p, 128, W)
    vn, p = place(p, 128, W)
    Sp, p = place(p, 128, W)
    Ss0, p = place(p, 128, NB, DH)
    qdm, p = place(p, 128, NB, NS)
    nwm, p = place(p, 128, NB, NS)
    Ss = [Ss0, Ss1]
    vnb, _ = spare(0, NS, NB, DH)
    rowG, _ = place(p, H, T)
    x2, p = place(ARENA - 3 * D, 128, 3, D)
    h2p, p = place(0, 128, 3, D)
    h2T, p = place(p, 128, KD, T)
    Pm, p = place(p, 128, 3, E * SLOTS)
    Pw, p = place(p, 128, 3, E * SLOTS)
    PwT, p = place(p, 128, E // 2, T)
    hg, p = place(p, 128, KD, 4 * SLOTS)
    assert p <= ARENA - 3 * D
    lgT, _ = place(3 * D + KD * T, 20, T)
    gfin = hT[:, :, :].rearrange("p a b -> p (a b)")[:, 0:D]
    outp, p = place(3 * D, 128, D)
    ea, p = place(p, 128, 2, 256)
    actb, p = place(p, 128, 2, 256)
    actT = [brT[0][:, :, :].rearrange("p a b -> p (a b)")[:, 256 * j:256 * j + 256] for j in range(2)]
    pws = [brT[1][:, :, :].rearrange("p a b -> p (a b)")[:, T * j:T * j + T] for j in range(2)]
    LG = tiny(128, 3, 20)
    oh = tiny(128, 3, 4)
    oh1 = tiny(128, 3, 4)
    oh2 = tiny(128, 3, 4)
    rtmp = tiny(128, 3, 4)
    rt1 = tiny(128, 12, 3)
    msk = tiny(128, 3, E)
    cmb = tiny(128, 3, E)
    rkm = tiny(128, 3, E)
    le4 = tiny(128, 3, E)
    wr = tiny(128, KD, 20)
    scrap = tiny(1, NSCRAP)
    oh3 = tiny(128, 3, 4)
    le12 = tiny(128, 12)
    R0, R1, R2 = (brT[j][0:H] for j in range(3))
    ROW_I, ROW_F, ROW_A, ROW_B = (R0[:, j, :] for j in range(4))
    ROW_Z, ROW_E = R1[:, 0:2, :], R1[:, 2:4, :]
    ROW_RS, ROW_W, ROW_IW, ROW_EN = (R1[:, j, :] for j in range(4))
    ROW_M, ROW_BC, ROW_G, ROW_KD = (R2[:, j, :] for j in range(4))
    ROW_RL, ROW_EG = ROW_BC, ROW_A

    def forms(t):
        if t < 2:
            return qTt, kTt, qwTt, dT, sT
        return [sform[:, j, :] for j in range(5)]

    w_in = a["w_in"][0]

    def cols_of(w, c):
        return w[:, c:c + 512].rearrange("(c p) n -> p c n", p=128)

    units = []
    units.append(("kvK", cols_of(a["w_mem_kv"][0], 0)))
    units.append(("kvV", cols_of(a["w_mem_kv"][0], W)))
    for name, o in (("q", O_Q), ("k", O_K), ("v", O_V), ("mo", O_MO), ("g0", O_GQKV), ("g1", O_GQKV + W),
                    ("g2", O_GQKV + 2 * W), ("gout", O_GOUT), ("xq", O_XQ)):
        units.append((name, cols_of(w_in, o)))
    for j, w in ((0, "w_br_mlstm"), (2, "w_br_xattn"), (1, "w_br_gdn")):
        units.append((("br", j), a[w][0].rearrange("(c p) n -> p c n", p=128)))
        for n in range(2):
            units.append((("gate", j, n), cols_of(w_in, O_GATE + j * D + n * 512)))
    for n in range(2):
        units.append((("out", n), cols_of(a["w_out"][0], n * 512)))
    NU = len(units)
    unit_no = {name: n for n, (name, _) in enumerate(units)}
    unit_last = {}

    def unit_ready(name):
        n = unit_no[name]
        return ring_full[n % RING0], 16 * (n // RING0 + 1)

    def unit(name):
        return ring[:, unit_no[name] % RING0, :]

    GROUP = [("hg", j, 4 + j) for j in range(4)]
    for pr_ in range(2):
        e0, e1 = 2 * pr_, 2 * pr_ + 1
        GROUP += [("gu", e0, 0), ("gu", e1, 1), ("aT", e0, 2), ("aT", e1, 2)]
        GROUP += [("dn", 2 * pr_, 3), ("dn", 2 * pr_ + 1, 4)]
        GROUP += [("y", 6 * pr_ + j, 5 + j % 3) for j in range(6)]
    g_uses, g_count = {}, [0] * 8
    for kind, j, b in GROUP:
        g_uses[(kind, j)] = (b, g_count[b])
        g_count[b] += 1
    SLOT_T = [3, 3, 2, 0, 0, 0, 0, 0]
    g_base = [0] * 8
    UPG = 12
    G_UNITS = [("g", 0), ("u", 0), ("g", 1), ("u", 1), ("d", 0), ("d", 1),
               ("g", 2), ("u", 2), ("g", 3), ("u", 3), ("d", 2), ("d", 3)]
    g_unit = {x: n for n, x in enumerate(G_UNITS)}
    G_LAST = [("gu", 0), ("gu", 0), ("gu", 1), ("gu", 1), ("dn", 1), ("dn", 1),
              ("gu", 2), ("gu", 2), ("gu", 3), ("gu", 3), ("dn", 3), ("dn", 3)]

    G_SLOTS = [4, 5, 2, 3, 0, 1]
    slot_before = [max((n for n in range(NU) if n % RING0 == s_), default=-1) if s_ < RING0 else -1
                   for s_ in range(RING)]

    def gslot(x):
        return G_SLOTS[g_unit[x] % RING]

    def gready(x, p, g):
        s_ = gslot(x)
        before = slot_before[s_] // RING0 + 1
        return ring_full[s_], (4 * p + g) * (16 * UPG // RING) + 16 * (before + g_unit[x] // RING + 1)

    def g_order(kind, j, p, g):
        b, n = g_uses[(kind, j)]
        return b, (4 * p + g) * g_count[b] + (p * SLOT_T[b]) + (g_base[b] + n)

    def gfilled(kind, j, p, g):
        b, n = g_order(kind, j, p, g)
        return full[b], n + 1

    def gtaken(kind, j, p, g):
        b, n = g_order(kind, j, p, g)
        return free[b], n

    def moved(kind, j, p, g):
        b, n = g_order(kind, j, p, g)
        return free[b], n + 1

    def t_order(e, p):
        b = e % 3
        return b, p * (4 * g_count[b] + SLOT_T[b]) + (g_base[b] - SLOT_T[b] + e // 3)

    def gbank(kind, j):
        return PS[:, g_uses[(kind, j)][0], :]

    def gfull(kind, j):
        return full[g_uses[(kind, j)][0]]

    def gfree(kind, j):
        return free[g_uses[(kind, j)][0]]

    FILL = [[[0], [1], [2], [3], [4, 5]], [[6], [7], [8], [9], [10, 11]], [[12], [13], [14], [], [], []]]
    PARTS = [(j, nn, t, x) for j in (0, 2) for nn in range(2) for t in range(3) for x in ((0, 1, 2) if t < 2 else (3,))]
    PART_AT = [{"raw": 3, "forms": 1, "KK": 1, "level": 1, "vn": 1, "hb": 1}] * 2 + \
        [{"raw": 1, "forms": 1, "KK": 1, "level": 1, "vn": 1, "hb": 1}]
    block = ctx.enter_context(nc.Block())

    @block.tensor
    def _(pe):
        def use(name, b):
            uses[name] = (b, count[b])
            if count[b]:
                pe.wait_ge(free[b], count[b])
            count[b] += 1
            return PS[:, b, :]

        pe.wait_ge(sg("cst_in"), 16)
        pe.wait_ge(sg("vrow_in"), 16 * 5)
        o = use("vec", 6)
        pe.transpose(o[:, 0:NV], vrow, ident[0:NV, 0:NV]).then_inc(full[6], 1)
        for j in (3, 4, 0, 1, 2):
            n = NS if j == 2 else 128
            pe.wait_ge(sg("x_norm"), (3, 4, 0, 1, 2).index(j) + 1)
            for hf in range(2):
                o = use(("xT", j, hf), (2 * j + hf) % 6)
                for c in range(4):
                    ins = pe.transpose(o[:, c * n:(c + 1) * n],
                                       xin[0:n, j, 512 * hf + 128 * c:512 * hf + 128 * c + 128],
                                       ident[0:n, 0:n])
                ins.then_inc(full[(2 * j + hf) % 6], 1)

        def samples(o, src, chunks, w, done):
            for k in range(chunks):
                for c in range(4):
                    ins = pe.matmul(o[NS * c:NS * c + NS, 0:128], src[:, k, SEQ:T], w(k)[:, 128 * c:128 * c + 128],
                                    start=(k == 0), stop=(k == chunks - 1))
            ins.then_inc(done, 1)

        def project(name, src, tiles, banks):
            pe.wait_ge(*unit_ready(name))
            for t, b in zip(tiles, banks):
                t0, n = TILES[t]
                o = use((name, t), b)
                if t == 2:
                    samples(o, src, KD, lambda k: unit(name)[:, 512 * k:512 * k + 512], full[b])
                    continue
                for k in range(KD):
                    ins = pe.matmul(o[0:n, :], src[:, k, t0:t0 + n], unit(name)[:, 512 * k:512 * k + 512],
                                    start=(k == 0), stop=(k == KD - 1))
                ins.then_inc(full[b], 1)
            unit_last[name] = (name, tiles[-1])

        pe.wait_ge(*taken(("xT", 4, 1)))
        project("kvK", memT, (0, 1), (0, 1))
        project("kvV", memT, (0, 1), (2, 3))
        pe.wait_ge(*taken(("kvK", 1)))
        for hf in range(2):
            o = use(("KT", hf), 4 + hf)
            for h in range(2):
                for m in range(2):
                    ins = pe.transpose(o[:, 256 * h + 128 * m:256 * h + 128 * m + 128],
                                       memk[:, m, 128 * (2 * hf + h):128 * (2 * hf + h) + 128], ident)
            ins.then_inc(full[4 + hf], 1)

        pe.wait_ge(sg("crow_in"), 32)
        o = use("crow", 7)
        nr = NB * HIST + CW
        for c in range(NCT):
            ins = pe.transpose(o[:, c * nr:(c + 1) * nr], crow[:, 128 * c:128 * c + 128], ident[0:nr, 0:nr])
        ins.then_inc(full[7], 1)

        pe.wait_ge(*taken(("xT", 2, 1)))
        pe.wait_ge(sg("wg_in"), 32)
        o = use("gates", 6)
        for j in range(4):
            for k in range(KD):
                ins = pe.matmul(o[32 * j:32 * j + 4, 0:T], wg[:, k, 4 * j:4 * j + 4], hT[:, k, :],
                                start=(k == 0), stop=(k == KD - 1))
        ins.then_inc(full[6], 1)

        for u, name in enumerate(("q", "k", "v", "mo")):
            b0 = 3 * (u % 2)
            project(name, hT, (0, 1, 2), (b0, b0 + 1, b0 + 2))
        pe.wait_ge(sg("rows"), 1)
        o = use("cols", 7)
        rows8 = (ROW_RS, ROW_W, ROW_IW, ROW_EN, ROW_G, ROW_B, ROW_EG, ROW_KD)
        for t, (t0, n) in enumerate(TILES):
            for j, r in enumerate(rows8):
                c = (t * 8 + j) * H
                ins = pe.transpose(o[0:n, c:c + H], r[:, t0:t0 + n], ident[0:H, 0:H])
        ins.then_inc(full[7], 1)
        o = use("dec", 6)
        for j, r in enumerate((ROW_IW, ROW_EG)):
            for h in range(H):
                c = (j * H + h) * NCH
                sel = cst[0:H, C_SEL + 128 * h:C_SEL + 128 * h + 128]
                pe.matmul(o[:, c:c + 4], sel, r[:, L - 1:SEQ:L], start=(j == 0 and h == 0), stop=False,
                          skip_group_check=True)
                ins = pe.matmul(o[:, c + 4:c + NCH], sel, r[:, SEQ + DS - 1:T:DS], start=False,
                                stop=(j == 1 and h == H - 1), skip_group_check=True)
        ins.then_inc(full[6], 1)

        def masked_rows(name, b, row, t):
            t0, n = TILES[t]
            neg = cst[0:n, C_NEGS:C_NEGS + n] if t == 2 else cst[0:n, C_NEGP:C_NEGP + n]
            o = use(name, b)
            pe.matmul(o[0:n, 0:H * n].rearrange("p (h l) -> p h l", h=H), ident[0:n, 0:n],
                      bc(neg.unsqueeze(1), n, H, n), start=True, stop=False)
            for h in range(H):
                ins = pe.matmul(o[0:n, h * n:(h + 1) * n], cst[0:H, C_SEL + 128 * h:C_SEL + 128 * h + n],
                                row[:, t0:t0 + n], start=False, stop=(h == H - 1))
            ins.then_inc(full[b], 1)

        def turn(name, b, src, n):
            o = use(name, b)
            for h in range(H):
                ins = pe.transpose(o[:, h * n:(h + 1) * n], src[:, 128 * h:128 * h + 128], ident[0:n, 0:n])
            ins.then_inc(full[b], 1)

        def fill(k):
            b = 6 + k % 2
            if k < NCT:
                u, c = f"g{k // 4}", k % 4
                if c == 0:
                    pe.wait_ge(*unit_ready(u))
                o = use(("cv", k), b)
                for kk in range(KD):
                    ins = pe.matmul(o[:, 0:T], unit(u)[:, 512 * kk + 128 * c:512 * kk + 128 * c + 128],
                                    hT[:, kk, :], start=(kk == 0), stop=(kk == KD - 1))
                ins.then_inc(full[b], 1)
                unit_last[u] = ("cv", k)
            elif k < NCT + 3:
                project("gout", hT, (k - NCT,), (b,))

        def fill_at(t, point):
            for k in FILL[t][point]:
                fill(k)

        for t, (t0, n) in enumerate(TILES):
            qx, kx, qwx, dx, sx = forms(t)
            pe.wait_ge(*taken(("q", t)))
            turn(("qT", t), 0, q_t[0:n, t, :], n)
            pe.wait_ge(*taken(("k", t)))
            turn(("kT", t), 1, k_t[0:n, t, :], n)
            pe.wait_ge(sg("qw"), t + 1)
            turn(("qwT", t), 2, q_t[0:n, t, :], n)
            masked_rows(("dl", t), 3, ROW_RL, t)
            fill_at(t, 0)
            pe.wait_ge(*taken(("kT", t)))
            o = use(("sc", t), 0)
            for h in range(H):
                ins = pe.matmul(o[0:n, h * n:(h + 1) * n], kx[:, h * n:(h + 1) * n], qx[:, h * n:(h + 1) * n],
                                start=True, stop=True)
            ins.then_inc(full[0], 1)
            fill_at(t, 1)
            pe.wait_ge(sg("sT"), t + 1)
            pe.wait_ge(*taken(("v", t)))
            oo = [use(("num", t, 0), 4), use(("num", t, 1), 5)]
            for h in range(H):
                pe.matmul(oo[h // 2][0:n, (h % 2) * DA:(h % 2 + 1) * DA], sx[0:n, h * n:(h + 1) * n],
                          v_a[0:n, t, h * DA:(h + 1) * DA], start=(h % 2 == 0), stop=False,
                          skip_group_check=True)
            pe.wait_ge(*taken(("qwT", t)))
            pe.wait_ge(sg("kw"), t + 1)
            if t < 2:
                for c in range(2):
                    r = slice(L * c, L * c + L)
                    if t or c:
                        before = (t, c - 1) if c else (t - 1, 1)
                        pe.wait_ge(*taken(("Cu", *before, 0)))
                        pe.wait_ge(*taken(("Cu", *before, 1)))
                    else:
                        pe.wait_ge(sg("C0"), 1)
                    for h in range(H):
                        ins = pe.matmul(oo[h // 2][r, (h % 2) * DA:(h % 2 + 1) * DA],
                                        qwx[:, h * n + L * c:h * n + L * c + L], Cp[:, h, :],
                                        start=False, stop=(c == 1), skip_group_check=True)
                        if c == 1 and h % 2:
                            ins.then_inc(full[4 + h // 2], 1)
                    uu = [use(("Cu", t, c, 0), 1), use(("Cu", t, c, 1), 2)]
                    for h in range(H):
                        ins = pe.matmul(uu[h // 2][:, (h % 2) * DA:(h % 2 + 1) * DA],
                                        k_t[r, t, 128 * h:128 * h + 128], v_a[r, t, h * DA:(h + 1) * DA],
                                        start=(h % 2 == 0), stop=(h % 2 == 1), skip_group_check=True)
                        if h % 2:
                            ins.then_inc(full[uses[("Cu", t, c, h // 2)][0]], 1)
                    fill_at(t, 2 + c)
            else:
                for h in range(H):
                    pe.wait_ge(sg("qwm"), h + 1)
                    for b in range(NB):
                        ins = pe.matmul(oo[h // 2][0:n, (h % 2) * DA:(h % 2 + 1) * DA], qwm[:, b, :],
                                        Cs[h % 2][:, b, :], start=False, stop=(b == NB - 1),
                                        skip_group_check=True)
                    if h % 2:
                        ins.then_inc(full[4 + h // 2], 1)
                    pe.wait_ge(sg("vblk"), h + 1)
                    for g, (b0, b1) in enumerate(((0, 3), (3, 6), (6, 8))):
                        bk = (1, 2, 3)[g]
                        o = use(("Cs", h, g), bk)
                        pe.matmul(o[:, 0:(b1 - b0) * DA], k_t[0:n, t, 128 * h:128 * h + 128],
                                  vblk[:, b0:b1, :].rearrange("p b v -> p (b v)"),
                                  start=True, stop=True).then_inc(full[bk], 1)
                    fill_at(t, 2 + h)
            if t < 2:
                fill_at(t, 4)
            pe.wait_ge(sg("ha"), t + 1)
            turn(("haT", t), 0, num[0:n, :], n)
        pe.wait_ge(sg("nst"), 1)
        o = use("nT", 3)
        pe.transpose(o[0:NB * H + H, 0:128], nst, ident).then_inc(full[3], 1)

        def scores(so, b):
            pe.wait_ge(*taken(("KbT", b, 0)))
            pe.wait_ge(*taken(("KbT", b, 1)))
            for h in range(H):
                ins = pe.matmul(so[NS * h:NS * h + NS, 0:MEM], qm[:, h, NS * b:NS * b + NS], KTb[b % 2][:, h, :],
                                start=(b == 0), stop=(b == NB - 1))
            if b == NB - 1:
                ins.then_inc(full[0], 1)
            else:
                ins.then_inc(sg("K_read"), 1)

        pe.wait_ge(sg("tailT"), 1)
        for g in range(3):
            o = use(("tail", g), g)
            for c in range(4):
                ins = pe.transpose(o[0:HIST * (NB + 1), 128 * c:128 * c + 128], tailT[:, 4 * g + c, :], ident)
            ins.then_inc(full[g], 1)
        project("xq", hT, (0, 1, 2), (2, 3, 4))
        for t, (t0, n) in enumerate(TILES):
            pe.wait_ge(*taken(("xq", t)))
            turn(("xqT", t), t % 2, xq[0:n, t, :], n)
        for t in range(2):
            t0 = 128 * t
            pe.wait_ge(*taken(("xqT", t)))
            if t == 0:
                pe.wait_ge(*taken(("KT", 1)))
            for g in range(2):
                o = use(("xs", t, g), 2 + g)
                for h in (2 * g, 2 * g + 1):
                    ins = pe.matmul(o[:, MEM * (h % 2):MEM * (h % 2) + MEM], xqT[:, h, t0:t0 + 128], KT[:, h, :],
                                    start=True, stop=True)
                ins.then_inc(full[2 + g], 1)
            pe.wait_ge(sg("pr"), t + 1)
            for m in range(2):
                o = use(("prT", t, m), 4 + m)
                for h in range(H):
                    ins = pe.transpose(o[:, 128 * h:128 * h + 128], pr[:, h, 128 * m:128 * m + 128], ident)
                ins.then_inc(full[4 + m], 1)
            pe.wait_ge(*taken(("prT", t, 0)))
            pe.wait_ge(*taken(("prT", t, 1)))
            o = use(("hcT", t), 6)
            for h in range(H):
                for m in range(2):
                    ins = pe.matmul(o[:, 128 * h:128 * h + 128], memv[:, m, 128 * h:128 * h + 128],
                                    prT[:, m, 128 * h:128 * h + 128], start=(m == 0), stop=(m == 1))
            ins.then_inc(full[6], 1)
        pe.wait_ge(sg("qm"), 1)
        so = use("ss", 0)
        for b in range(NB):
            pe.wait_ge(sg(f"Kb{b % 2}"), 16 * (b // 2 + 1))
            for g in range(2):
                o = use(("KbT", b, g), 2 + g + 2 * (b % 2))
                for h in (2 * g, 2 * g + 1):
                    for m in range(2):
                        ins = pe.transpose(o[:, MEM * (h % 2) + 128 * m:MEM * (h % 2) + 128 * m + 128],
                                           Kb[b % 2][:, m, 128 * h:128 * h + 128], ident)
                ins.then_inc(full[2 + g + 2 * (b % 2)], 1)
            if b:
                scores(so, b - 1)
        scores(so, NB - 1)
        pe.wait_ge(sg("pr"), 3)
        o = use("spT", 1)
        for m in range(2):
            ins = pe.transpose(o[:, 128 * m:128 * m + 128], pr[:, 0, 128 * m:128 * m + 128], ident)
        ins.then_inc(full[1], 1)
        pe.wait_ge(*taken("spT"))
        o = use("hcs", 6)
        for b in range(NB):
            pe.wait_ge(sg(f"Vb{b % 2}"), 16 * (b // 2 + 1))
            for m in range(2):
                for h in range(H):
                    ins = pe.matmul(o[NS * h:NS * h + NS, 0:128],
                                    spT[:, m, 128 * b + NS * h:128 * b + NS * h + NS],
                                    Vb[b % 2][:, m, 128 * h:128 * h + 128],
                                    start=(b == 0 and m == 0), stop=(b == NB - 1 and m == 1))
            if b < NB - 1:
                ins.then_inc(sg("V_read"), 1)
        ins.then_inc(full[6], 1)
        pe.wait_ge(*taken("hcs"))
        o = use("hcsT", 7)
        pe.transpose(o[:, 0:128], hcs, ident).then_inc(full[7], 1)

        def merge_part(j, nn, t, x):
            t0, n = TILES[t]
            if x in (0, 3):
                merges[0] += 1
                use(("mg", j, nn, t), 5 + merges[0] % 2)
            bg = 5 + merges[0] % 2
            wg_ = lambda k: unit(("gate", j, nn))[:, 512 * k:512 * k + 512]
            wb_ = lambda k: unit(("br", j))[:, D * k + 512 * nn:D * k + 512 * nn + 512]
            if t == 0 and x == 0:
                pe.wait_ge(*unit_ready(("gate", j, nn)))
            if x < 2:
                for k in range(4 * x, 4 * x + 4):
                    ins = pe.matmul(PS[:, bg, :], hT[:, k, t0:t0 + n], wg_(k), start=(k == 0), stop=(k == KD - 1))
                if x == 1:
                    ins.then_inc(full[bg], 1)
            if x == 2:
                if t == 0 and nn == 0:
                    pe.wait_ge(*unit_ready(("br", j)))
                o = use(("mb", j, nn, t), 7)
                for k in range(H):
                    ins = pe.matmul(o, brT[j][:, k, t0:t0 + n], wb_(k), start=(k == 0), stop=(k == H - 1))
                ins.then_inc(full[7], 1)
            if x == 3:
                samples(PS[:, bg, :], hT, KD, wg_, full[bg])
                samples(use(("mb", j, nn, t), 7), brT[j], H, wb_, full[7])
                unit_last[("gate", j, nn)] = ("mb", j, nn, 2)
                unit_last[("br", j)] = ("mb", j, nn, 2)

        def part_at(t, point):
            for _ in range(PART_AT[t][point]):
                if parts_done[0] < len(PARTS):
                    merge_part(*PARTS[parts_done[0]])
                    parts_done[0] += 1

        parts_done, merges = [0], [0]
        pe.wait_ge(*taken("hcsT"))
        pe.wait_ge(sg("rowG"), 1)
        pe.wait_ge(sg("cvT"), 3)
        for t, (t0, n) in enumerate(TILES):
            for g in range(3):
                o = use(("raw", t, g), g)
                for c in range(4):
                    ins = pe.transpose(o[0:n, 128 * c:128 * c + 128], cvT[:, 4 * g + c, t0:t0 + n], ident)
                ins.then_inc(full[g], 1)
            masked_rows(("dG", t), 3, rowG, t)
            part_at(t, "raw")
            pe.wait_ge(sg("gq"), 4 * t + 1)
            turn(("kT2", t), 4, raw[0:n, 1, :], n)
            pe.wait_ge(sg("gq"), 4 * t + 2)
            turn(("kbT", t), 0, kb[0:n, :], n)
            pe.wait_ge(sg("gq"), 4 * t + 3)
            turn(("qT2", t), 1, raw[0:n, 0, :], n)
            pe.wait_ge(sg("gq"), 4 * t + 4)
            turn(("qdT", t), 2, qd[0:n, :], n)
            part_at(t, "forms")
            pe.wait_ge(*taken(("qT2", t)))
            pe.wait_ge(*taken(("qdT", t)))
            for name, b, x in ((("KK", t), 3, kbT), (("QK", t), 4, qT)):
                o = use(name, b)
                for h in range(H):
                    ins = pe.matmul(o[0:n, h * n:(h + 1) * n], kT[:, h * n:(h + 1) * n], x[:, h * n:(h + 1) * n],
                                    start=True, stop=True)
                ins.then_inc(full[b], 1)
            part_at(t, "KK")
            nl = 2 if t == 2 else LEVELS
            for k in range(nl):
                pe.wait_ge(sg("ATk"), lv(t, k) + 1)
                o = use(("X", t, k), 0)
                for h in range(H):
                    ins = pe.matmul(o[0:n, h * n:(h + 1) * n], dG[0:n, h * n:(h + 1) * n],
                                    ident[0:n, 0:n] if k == 0 else Tm[0:n, h * n:(h + 1) * n],
                                    start=True, stop=True)
                ins.then_inc(full[0], 1)
                if k == 0:
                    continue
                pe.wait_ge(*taken(("X", t, k)))
                o = use(("YT", t, k), 1)
                for h in range(H):
                    ins = pe.matmul(o[0:n, h * n:(h + 1) * n], Xm[0:n, h * n:(h + 1) * n],
                                    Um[0:n, h * n:(h + 1) * n], start=True, stop=True)
                ins.then_inc(full[1], 1)
                if k < nl - 1:
                    o = use(("Y", t, k), 2)
                    for h in range(H):
                        ins = pe.matmul(o[0:n, h * n:(h + 1) * n], Um[0:n, h * n:(h + 1) * n],
                                        Xm[0:n, h * n:(h + 1) * n], start=True, stop=True)
                    ins.then_inc(full[2], 1)
                part_at(t, "level")
            pe.wait_ge(*taken(("YT", t, nl - 1)))
            pe.wait_ge(sg("gv"), t + 1)
            o = use(("wT", t), 3)
            for h in range(H):
                ins = pe.matmul(o[:, h * n:(h + 1) * n], kbg[0:n, 128 * h:128 * h + 128],
                                Um[0:n, h * n:(h + 1) * n], start=True, stop=True)
            ins.then_inc(full[3], 1)
            pe.wait_ge(*taken(("wT", t)))
            pe.wait_ge(*taken(("QK", t)))
            if t < 2:
                for c in range(2):
                    r = slice(L * c, L * c + L)
                    if t or c:
                        pe.wait_ge(*taken(("So", t, c - 1) if c else ("So", t - 1, 1)))
                    else:
                        pe.wait_ge(sg("S0"), 1)
                    o = use(("vn", t, c), 4)
                    for h in range(H):
                        hc = slice(h * n + L * c, h * n + L * c + L)
                        hv = slice(128 * h, 128 * h + 128)
                        pe.matmul(o[r, hv], Um[0:n, hc], raw[0:n, 2, hv], start=(h == 0), stop=False,
                                  skip_group_check=True)
                        ins = pe.matmul(o[r, hv], kbT[:, hc], Sp[:, hv], start=False, stop=(h == H - 1),
                                        skip_group_check=True)
                    ins.then_inc(full[4], 1)
                    part_at(t, "vn")
                    pe.wait_ge(*taken(("vn", t, c)))
                    o = use(("So", t, c), 0)
                    for h in range(H):
                        hv = slice(128 * h, 128 * h + 128)
                        ins = pe.matmul(o[:, hv], kd[r, hv], vn[r, hv], start=True, stop=True)
                    ins.then_inc(full[0], 1)
                    o = use(("go", t, c), 1)
                    for h in range(H):
                        hc = slice(h * n + L * c, h * n + L * c + L)
                        hv = slice(128 * h, 128 * h + 128)
                        pe.matmul(o[r, hv], qdT[:, hc], Sp[:, hv], start=(h == 0), stop=False,
                                  skip_group_check=True)
                        ins = pe.matmul(o[r, hv], QKT[r, hc], vn[r, hv], start=False, stop=(h == H - 1),
                                        skip_group_check=True)
                    ins.then_inc(full[1], 1)
            else:
                for h in range(H):
                    hc, hv = slice(h * n, (h + 1) * n), slice(128 * h, 128 * h + 128)
                    pe.wait_ge(sg("nwm"), h + 1)
                    o = use(("vn2", h), 4)
                    pe.matmul(o[0:n, 0:DH], Um[0:n, hc], raw[0:n, 2, hv], start=True, stop=False)
                    for b in range(NB):
                        ins = pe.matmul(o[0:n, 0:DH], nwm[:, b, :], Ss[h % 2][:, b, :], start=False,
                                        stop=(b == NB - 1))
                    ins.then_inc(full[4], 1)
                    part_at(t, "vn")
                    pe.wait_ge(sg("vnb"), h + 1)
                    o = use(("go2", h), 1)
                    for b in range(NB):
                        pe.matmul(o[0:n, 0:DH], qdm[:, b, :], Ss[h % 2][:, b, :], start=(b == 0), stop=False)
                    pe.matmul(o[0:n, 0:DH], QKT[0:n, hc], vn[0:n, hv], start=False,
                              stop=True).then_inc(full[1], 1)
                    for g in range(2):
                        bk = (0, 3)[g]
                        o = use(("So2", h, g), bk)
                        pe.matmul(o, kd[0:n, hv], vnb[:, 4 * g:4 * g + 4, :].rearrange("p b v -> p (b v)"),
                                  start=True, stop=True).then_inc(full[bk], 1)
            part_at(t, "hb")
            pe.wait_ge(sg("hb"), t + 1)
            turn(("hbT", t), 2, kb[0:n, :], n)

        while parts_done[0] < len(PARTS):
            merge_part(*PARTS[parts_done[0]])
            parts_done[0] += 1
        pe.wait_ge(*taken(("hbT", 2)))
        for nn in range(2):
            for t in range(3):
                for x in (0, 1, 2) if t < 2 else (3,):
                    merge_part(1, nn, t, x)
        for t, (t0, n) in enumerate(TILES):
            pe.wait_ge(sg("mixed"), t + 1)
            for hf in range(2):
                o = use(("mixT", t, hf), 6 + hf)
                if t == 2:
                    pe.transpose(o[:, 0:128], mixs[:, hf, :], ident).then_inc(full[6 + hf], 1)
                    continue
                for c in range(4):
                    ins = pe.transpose(o[:, c * n:(c + 1) * n],
                                       mixed[0:n, t, 512 * hf + 128 * c:512 * hf + 128 * c + 128],
                                       ident[0:n, 0:n])
                ins.then_inc(full[6 + hf], 1)
        pe.wait_ge(*taken(("mixT", 2, 0)))
        pe.wait_ge(*taken(("mixT", 2, 1)))
        project(("out", 0), mixT, (0, 1, 2), (0, 1, 2))
        project(("out", 1), mixT, (0, 1, 2), (3, 4, 5))

        for t, (t0, n) in enumerate(TILES):
            pe.wait_ge(sg("h2p"), t + 1)
            for hf in range(2):
                o = use(("h2T", t, hf), 6 + hf)
                for c in range(4):
                    ins = pe.transpose(o[:, c * n:(c + 1) * n],
                                       h2p[0:n, t, 512 * hf + 128 * c:512 * hf + 128 * c + 128],
                                       ident[0:n, 0:n])
                ins.then_inc(full[6 + hf], 1)
        pe.wait_ge(*taken(("h2T", 2, 1)))
        pe.wait_ge(sg("wr_in"), 32)
        o = use("lgT", 0)
        for k in range(KD):
            ins = pe.matmul(o[0:20, 0:T], wr[:, k, :], h2T[:, k, :], start=(k == 0), stop=(k == KD - 1))
        ins.then_inc(full[0], 1)
        pe.wait_ge(*taken("lgT"))
        o = use("lg", 1)
        for t, (t0, n) in enumerate(TILES):
            ins = pe.transpose(o[0:n, 20 * t:20 * t + 20], lgT[0:20, t0:t0 + n], ident[0:20, 0:20])
        ins.then_inc(full[1], 1)
        pe.wait_ge(sg("msk"), 1)
        pe.wait_ge(sg("ones"), 1)
        o = use("rank", 2)
        for t, (t0, n) in enumerate(TILES):
            for u in range(t + 1):
                ins = pe.matmul(o[0:n, E * t:E * t + E],
                                cst[0:n, C_TRI:C_TRI + n] if u == t else ones[:, 0:n],
                                msk[0:TILES[u][1], u, :], start=(u == 0), stop=(u == t))
        for u, (t0, n) in enumerate(TILES):
            ins = pe.matmul(o[0:1, 3 * E:4 * E], ones[0:n, 0:1], msk[0:n, u, :], start=(u == 0), stop=(u == 2))
        ins.then_inc(full[2], 1)

        def slots_T(p=None):
            for e in range(E // 2):
                if p is None:
                    o = use(("PwT", e), e % 3)
                else:
                    b, n = t_order(e, p)
                    pe.wait_ge(free[b], n)
                    o = PS[:, b, :]
                for t, (t0, n) in enumerate(TILES):
                    ins = pe.transpose(o[:, t0:t0 + n], Pw[0:n, t, 128 * e:128 * e + 128], ident[0:n, 0:n])
                ins.then_inc(full[e % 3], 1)

        pe.wait_ge(sg("Pm"), 1)
        slots_T()
        for b in range(8):
            g_base[b] = count[b]

        def group(p, g):
            for j in range(4):
                pe.wait_ge(*gtaken("hg", j, p, g))
                o = gbank("hg", j)
                for c in (2 * j, 2 * j + 1):
                    for t, (t0, n) in enumerate(TILES):
                        ins = pe.matmul(o[:, 256 * (c % 2):256 * (c % 2) + 256], h2p[0:n, t, 128 * c:128 * c + 128],
                                        Pm[0:n, t, bass.ds(g * 256, 256)], start=(t == 0), stop=(t == 2))
                ins.then_inc(gfull("hg", j), 1)
            for pr_ in range(2):
                for e in (2 * pr_, 2 * pr_ + 1):
                    if e == 0:
                        pe.wait_ge(*moved("hg", 3, p, g))
                    pe.wait_ge(*gready(("g", e), p, g))
                    pe.wait_ge(*gready(("u", e), p, g))
                    pe.wait_ge(*gtaken("gu", e, p, g))
                    o = gbank("gu", e)
                    s0 = gslot(("g", e))
                    for k in range(KD):
                        for hf in range(2):
                            ins = pe.matmul(o[64 * hf:64 * hf + 64, :], hg[:, k, 64 * e:64 * e + 64],
                                            ring[:, s0:s0 + 2, 512 * k + 256 * hf:512 * k + 256 * hf + 256],
                                            start=(k == 0), stop=(k == KD - 1))
                    ins.then_inc(gfull("gu", e), 1)
                if pr_ == 1:
                    scatter(0, p, g)
                for e in (2 * pr_, 2 * pr_ + 1):
                    pe.wait_ge(sg("act"), (4 * p + g) * 4 + (e + 1))
                    pe.wait_ge(*gtaken("aT", e, p, g))
                    o = gbank("aT", e)
                    for c in range(2):
                        ins = pe.transpose(o[:, 128 * c:128 * c + 128], actb[:, e % 2, 128 * c:128 * c + 128], ident)
                    ins.then_inc(gfull("aT", e), 1)
                for e in (2 * pr_, 2 * pr_ + 1):
                    pe.wait_ge(*moved("aT", e, p, g))
                for x in range(2):
                    pe.wait_ge(*gready(("d", 2 * pr_ + x), p, g))
                for nn in range(2):
                    pe.wait_ge(*gtaken("dn", 2 * pr_ + nn, p, g))
                for nn in range(2):
                    o = gbank("dn", 2 * pr_ + nn)
                    for c in range(4):
                        hf, cc = c // 2, c % 2
                        for x in range(2):
                            w = ring[:, gslot(("d", 2 * pr_ + x)), D * c + 512 * nn:D * c + 512 * nn + 512]
                            ins = pe.matmul(o[64 * x:64 * x + 64, :],
                                            actT[x][:, 128 * cc + 64 * hf:128 * cc + 64 * hf + 64], w,
                                            start=(c == 0), stop=(c == 3))
                    ins.then_inc(gfull("dn", 2 * pr_ + nn), 1)
            scatter(1, p, g)

        def scatter(pr_, p, g):
            pe.wait_ge(sg("pws"), (4 * p + g) * 2 + (pr_ + 1))
            for nn in range(2):
                pe.wait_ge(*moved("dn", 2 * pr_ + nn, p, g))
            for t, (t0, n) in enumerate(TILES):
                for nn in range(2):
                    j = 6 * pr_ + 2 * t + nn
                    pe.wait_ge(*gtaken("y", j, p, g))
                    pe.matmul(gbank("y", j)[0:n, :], pws[pr_][:, t0:t0 + n], outp[:, 512 * nn:512 * nn + 512],
                              start=True, stop=True).then_inc(gfull("y", j), 1)

        with pe.Fori(0, G) as g:
            group(0, g)
        pe.wait_ge(sg("flag"), 1)
        most = pe.value_load(flag[0:1, 0:1], min_val=0, max_val=T)
        with pe.If(most > SLOTS):
            with pe.Fori(1, PASSES) as p:
                pe.wait_ge(sg("Pm"), p + 1)
                slots_T(p)
                with pe.Fori(0, G) as g:
                    group(p, g)

    @block.sync
    def _(sp):
        for j in (3, 4):
            sp.dma_start(xin[:, j, :], a["mem_prompt"][0, 128 * (j - 3):128 * (j - 2), :]).then_inc(sg(f"xin{j}"), 16)
        r = 0
        for x, n in ((a["norm_mix"][0], KD), (a["mem_norm"][0], KD), (a["mlstm_norm"][0], H),
                     (a["gdn_norm"][0], 1)):
            sp.dma_start(vrow[r:r + n, :], x.rearrange("(r c) -> r c", c=128)).then_inc(sg("vrow_in"), 16)
            r += n
        sp.dma_start(vrow[r:r + NB * H, :],
                     a["state_mlstm_n"][0].rearrange("b h k -> (b h) k")).then_inc(sg("vrow_in"), 16)
        sp.dma_start(cst[:, :], a["table"][:, 0:C_N]).then_inc(sg("cst_in"), 16)
        for j, (t0, n) in enumerate(TILES):
            x = a["x_prompt"][0, t0:t0 + n, :] if j < 2 else a["x_sample"].rearrange("b s d -> (b s) d")
            sp.dma_start(xin[0:n, j, :], x).then_inc(sg(f"xin{j}"), 16)
        sp.dma_start(wg[:, :, 0:8], w_in[:, O_IF:O_IF + 8].rearrange("(c p) n -> p c n", p=128)) \
            .then_inc(sg("wg_in"), 16)
        sp.dma_start(wg[:, :, 8:16], w_in[:, O_GAB:O_GAB + 8].rearrange("(c p) n -> p c n", p=128)) \
            .then_inc(sg("wg_in"), 16)
        for n, (name, src) in enumerate(units):
            if n >= RING0:
                sp.wait_ge(*filled(unit_last[units[n - RING0][0]]))
            sp.dma_start(unit(name).rearrange("p (c n) -> p c n", c=src.shape[1]), src) \
                .then_inc(ring_full[n % RING0], 16)

        def load_group(p, g, first):
            for u, (kind, e) in enumerate(G_UNITS):
                if first and G_SLOTS[u % RING] >= RING0 and u < RING:
                    if u == 0:
                        sp.wait_ge(*filled(("hbT", 2)))
                        sp.wait_ge(sg("Ss_out1"), 32)
                elif first and u < RING:
                    sp.wait_ge(*filled(unit_last[units[slot_before[G_SLOTS[u]]][0]]))
                elif u < RING:
                    kd_, j = G_LAST[u + UPG - RING]
                    b, n = g_uses[(kd_, j)]
                    sp.wait_ge(full[b], prev_order(kd_, j, p, g))
                else:
                    sp.wait_ge(*gfilled(*G_LAST[u - RING], p, g))
                w = {"g": "w_exp_gate", "u": "w_exp_up", "d": "w_exp_down"}[kind]
                if kind == "d":
                    src = a[w][0, bass.ds(g * EG + e, 1)].rearrange("e (c p) n -> p (e c) n", p=128)
                else:
                    src = a[w][0, bass.ds(g * EG + e, 1)].rearrange("e (p c) n -> p (e c) n", p=128)
                sp.dma_start(ring[:, gslot((kind, e)), :].rearrange("p (c n) -> p c n", c=4 if kind == "d" else 8),
                             src).then_inc(ring_full[gslot((kind, e))], 16)

        def prev_order(kind, j, p, g):
            b, n = g_uses[(kind, j)]
            if isinstance(g, int):
                if g:
                    return (4 * p + (g - 1)) * g_count[b] + p * SLOT_T[b] + (g_base[b] + n + 1)
                return (4 * p - 1) * g_count[b] + (p - 1) * SLOT_T[b] + (g_base[b] + n + 1)
            return (4 * p + g) * g_count[b] + p * SLOT_T[b] + (g_base[b] + n + 1 - g_count[b])

        load_group(0, 0, True)
        with sp.Fori(1, G) as g:
            load_group(0, g, False)
        sp.wait_ge(sg("flag"), 1)
        most = sp.value_load(flag[0:1, 0:1], min_val=0, max_val=T)
        with sp.If(most > SLOTS):
            with sp.Fori(1, PASSES) as p:
                load_group(p, 0, False)
                with sp.Fori(1, G) as g:
                    load_group(p, g, False)
        for t, (t0, n) in enumerate(TILES):
            y = out["y_prompt"][0, t0:t0 + n, :] if t < 2 else out["y_sample"].rearrange("b s d -> (b s) d")
            sp.wait_ge(sg("y"), t + 1)
            sp.dma_start(y, x2[0:n, t, :]).then_inc(sg("y_out"), 16)
        sp.wait_ge(sg("y_out"), 48)

    @block.gpsimd
    def _(pool):
        small_in = sg("small_in")
        nsm = 0
        for dst, src in ((bias4[:, 0:1], a["b_igate"][0]), (bias4[:, 1:2], a["b_fgate"][0]),
                         (bias4[:, 2:3], a["dt_bias"][0]), (bias4[:, 3:4], a["a_log"][0]),
                         (brt[0:G, :], a["b_router_group"][0]), (brt[G:20, :], a["b_router_expert"][0])):
            pool.dma_start(dst, src.rearrange("(n a) -> n a", a=1)).then_inc(small_in, 16)
            nsm += 1
        pool.dma_start(rset, a["table"][0:H, C_RST:C_ALL]).then_inc(small_in, 16)
        pool.dma_start(m0, a["state_mlstm_m"][0].rearrange("b h -> h b"), allow_slow_non_contiguous=True).then_inc(small_in, 16)
        pool.dma_start(gffn, a["norm_ffn"][0].rearrange("(p c) -> p c", c=KD)).then_inc(small_in, 16)
        pool.dma_start(crow[0:NB * HIST, :], a["state_gdn_conv"][0].rearrange("b s c -> (b s) c")) \
            .then_inc(sg("crow_in"), 16)
        pool.dma_start(crow[NB * HIST:, :], a["conv_w"][0]).then_inc(sg("crow_in"), 16)
        pool.dma_start(wr[:, :, 0:G], a["w_router_group"][0].rearrange("(p c) n -> p c n", c=KD)).then_inc(sg("wr_in"), 16)
        pool.dma_start(wr[:, :, G:20], a["w_router_expert"][0].rearrange("(p c) n -> p c n", c=KD)).then_inc(sg("wr_in"), 16)
        pool.memset(ones[:, :], 1.0).then_inc(sg("ones"), 1)
        for m in range(2):
            pool.wait_ge(*taken(("kvK", m)))
            pool.dma_start(out["mem_k"][0, 0, 128 * m:128 * m + 128].rearrange("m h d -> m (h d)"),
                           memk[:, m, :]).then_inc(sg("memk_out"), 16)
            pool.wait_ge(*taken(("kvV", m)))
            pool.dma_start(out["mem_v"][0, 0, 128 * m:128 * m + 128].rearrange("m h d -> m (h d)"),
                           memv[:, m, :]).then_inc(sg("kv_out"), 16)
        pool.wait_ge(sg("rows"), 1)
        pool.dma_start(out["m_p"][0].rearrange("b h -> h b"), ROW_M[:, SEQ - 1:SEQ], allow_slow_non_contiguous=True).then_inc(sg("m_out"), 16)
        pool.dma_start(out["m_s"][0].rearrange("b h -> h b"), ROW_M[:, SEQ + DS - 1:T:DS], allow_slow_non_contiguous=True).then_inc(sg("m_out"), 16)
        for h in range(2):
            if h == 0:
                pool.wait_ge(*filled("gates"))
                pool.wait_ge(sg("memk_out"), 32)
            pool.dma_start(Cs[h][:, :, 0:DH], a["state_mlstm_C"][0, :, h].rearrange("b k v -> k b v")) \
                .then_inc(sg(f"Cs_in{h}"), 16)
        pool.wait_ge(sg("Cp"), 1)
        pool.dma_start(out["C_p"][0, 0].rearrange("h k v -> k h v"), Cp[:, :, 0:DH]).then_inc(sg("Cp_out"), 16)
        for h in range(H):
            pool.wait_ge(sg("Cs"), h + 1)
            pool.dma_start(out["C_s"][0, :, h].rearrange("b k v -> k b v"), Cs[h % 2][:, :, 0:DH]) \
                .then_inc(sg(f"Cs_out{h % 2}"), 16)
            if h < 2:
                pool.wait_ge(sg(f"Cs_out{h}"), 16)
                pool.dma_start(Cs[h][:, :, 0:DH], a["state_mlstm_C"][0, :, h + 2].rearrange("b k v -> k b v")) \
                    .then_inc(sg(f"Cs_in{h}"), 16)
        pool.wait_ge(*taken("nT"))
        pool.dma_start(out["n_s"][0].rearrange("b h k -> (b h) k"), nrow[0:NB * H, :]).then_inc(sg("n_out"), 16)
        pool.dma_start(out["n_p"][0, 0], nrow[NB * H:NB * H + H, :]).then_inc(sg("n_out"), 16)
        pool.wait_ge(*taken(("tail", 2)))
        pool.dma_start(out["conv_p"][0, 0], tails[0:HIST, :]).then_inc(sg("tail_out"), 16)
        pool.dma_start(out["conv_s"][0].rearrange("b s c -> (b s) c"), tails[HIST:, :]).then_inc(sg("tail_out"), 16)
        pool.wait_ge(sg("Cs_out1"), 32)
        pool.wait_ge(sg("Cs_out0"), 32)
        pool.wait_ge(sg("Cp_out"), 16)
        pool.wait_ge(*filled(("haT", 2)))
        for b in range(NB):
            if b >= 2:
                pool.wait_ge(*filled(("KbT", b - 2, 1)))
            pool.dma_start(Kb[b % 2], a["cache_mem_k"][0, b].rearrange("(c p) h d -> p c (h d)", p=128)) \
                .then_inc(sg(f"Kb{b % 2}"), 16)
            if b < 2:
                pool.dma_start(Vb[b], a["cache_mem_v"][0, b].rearrange("(c p) h d -> p c (h d)", p=128)) \
                    .then_inc(sg(f"Vb{b}"), 16)
        for b in range(2, NB):
            pool.wait_ge(sg("V_read"), b - 1)
            pool.dma_start(Vb[b % 2], a["cache_mem_v"][0, b].rearrange("(c p) h d -> p c (h d)", p=128)) \
                .then_inc(sg(f"Vb{b % 2}"), 16)
        pool.wait_ge(*filled("hcs"))
        for h in range(2):
            pool.dma_start(Ss[h], a["state_gdn_S"][0, :, h].rearrange("b k v -> k b v")) \
                .then_inc(sg(f"Ss_in{h}"), 16)
        pool.wait_ge(sg("Spout"), 1)
        pool.dma_start(out["S_p"][0, 0].rearrange("h k v -> k h v"),
                       Sp.rearrange("p (h v) -> p h v", h=H)).then_inc(sg("Sp_out"), 16)
        for h in range(H):
            pool.wait_ge(sg("Ssd"), h + 1)
            pool.dma_start(out["S_s"][0, :, h].rearrange("b k v -> k b v"), Ss[h % 2]) \
                .then_inc(sg(f"Ss_out{h % 2}"), 16)
            if h < 2:
                pool.wait_ge(sg(f"Ss_out{h}"), 16)
                pool.dma_start(Ss[h], a["state_gdn_S"][0, :, h + 2].rearrange("b k v -> k b v")) \
                    .then_inc(sg(f"Ss_in{h}"), 16)
        for s in ("Ss_out0", "Ss_out1"):
            pool.wait_ge(sg(s), 32)
        pool.wait_ge(sg("Sp_out"), 16)
        pool.wait_ge(*filled(("hbT", 2)))
        for t, (t0, n) in enumerate(TILES):
            x = a["x_prompt"][0, t0:t0 + n, :] if t < 2 else a["x_sample"].rearrange("b s d -> (b s) d")
            pool.dma_start(x2[0:n, t, :], x).then_inc(sg("x2_in"), 16)
        pool.wait_ge(*filled((("out", 1), 2)))
        pool.dma_start(gfin, a["final_norm"].partition_broadcast(128)).then_inc(sg("gfin_in"), 16)
        for s, n in (("kv_out", 32), ("memk_out", 32), ("m_out", 32), ("n_out", 32), ("tail_out", 32), ("gfin_in", 16), ("wr_in", 32)):
            pool.wait_ge(sg(s), n)

    @block.scalar
    def _(act):
        def run(o, i, f, **kw):
            return act.activation(o, i, f, **kw)

        act.preload_act_table_set("natural_log_exp_and_others")
        for i, j in enumerate((3, 4, 0, 1, 2)):
            n = NS if j == 2 else 128
            act.wait_ge(sg(f"xin{j}"), 16)
            astep(run(junk[0:n, :], xin[0:n, j, :], ACT.Square, accum_out=ss[0:n, j:j + 1]))
            astep(run(rstd[0:n, j:j + 1], ss[0:n, j:j + 1], ACT.Ln, scale=1.0 / D, bias=EPS))
            run(rstd[0:n, j:j + 1], rstd[0:n, j:j + 1], ACT.Exp, scale=-0.5).then_inc(sg("rstd"), 1)

        def copy_out(name, o, i, scale=1.0, wait=True):
            if wait:
                act.wait_ge(*filled(name))
            run(o, i, ACT.Copy, scale=scale).then_inc(freed(name), 1)

        def rows_out(name, t, o, scale, f=ACT.Copy, done=None):
            act.wait_ge(*filled((name, t)))
            if t < 2:
                ins = run(o[:, t, :], bank_of((name, t)), f, scale=scale)
            else:
                for c in range(4):
                    ins = run(o[0:NS, t, 128 * c:128 * c + 128], bank_of((name, t))[NS * c:NS * c + NS, 0:128], f,
                              scale=scale)
            ins.then_inc(done or freed((name, t)), 1)

        for name, o in (("kvK", memk), ("kvV", memv)):
            for m in range(2):
                copy_out((name, m), o[:, m, :], bank_of((name, m)))
        for hf in range(2):
            copy_out(("KT", hf), KT[:, 2 * hf:2 * hf + 2, :].rearrange("p h m -> p (h m)"), bank_of(("KT", hf)))
        act.wait_ge(sg("small_in"), 16 * 9)
        astep(run(bias4[:, 4:5], bias4[:, 3:4], ACT.Exp))
        act.wait_ge(*filled("gates"))
        run(ROW_B, bank_of("gates")[96:100, 0:T], ACT.Exp, scale=-1.0).then_inc(sg("rowB"), 1)
        act.wait_ge(sg("rowZ"), 1)
        astep(run(ROW_E, ROW_E, ACT.Exp))
        run(ROW_E, ROW_E, ACT.Ln, bias=1.0).then_inc(sg("rowL"), 1)
        for t, (t0, n) in enumerate(TILES):
            rows_out("q", t, q_t, 1.0)
        for t, (t0, n) in enumerate(TILES):
            rows_out("k", t, k_t, QSCALE)
        act.wait_ge(sg("rowX"), 1)
        astep(run(ROW_EN, ROW_M, ACT.Exp, scale=-1.0))
        astep(run(ROW_EG, ROW_G, ACT.Exp))
        astep(run(ROW_W, ROW_W, ACT.Exp))
        astep(run(ROW_IW, ROW_IW, ACT.Exp))
        run(ROW_KD, ROW_KD, ACT.Exp).then_inc(sg("rows"), 1)
        act.preload_act_table_set("exp_and_others")
        for t, (t0, n) in enumerate(TILES):
            rows_out("mo", t, mo, 0.5, ACT.Tanh)
        def fill_at(t, point):
            for k in FILL[t][point]:
                if k < NCT:
                    act.wait_ge(*filled(("cv", k)))
                    run(cin[:, k, HIST:], bank_of(("cv", k))[:, 0:SEQ], ACT.Copy)
                    run(cis[:, k, :].rearrange("p (b s) -> p b s", b=NB)[:, :, HIST:],
                        bank_of(("cv", k))[:, SEQ:T].rearrange("p (b s) -> p b s", b=NB), ACT.Copy) \
                        .then_inc(freed(("cv", k)), 1)
                elif k < NCT + 3:
                    rows_out("gout", k - NCT, gout, 1.0)

        act.preload_act_table_set("natural_log_exp_and_others")
        for t, (t0, n) in enumerate(TILES):
            qx, kx, qwx, dx, sx = forms(t)
            if t == 1:
                act.wait_ge(*filled(("sc", 0)))
            copy_out(("qT", t), qx[:, 0:H * n], bank_of(("qT", t))[:, 0:H * n])
            copy_out(("kT", t), kx[:, 0:H * n], bank_of(("kT", t))[:, 0:H * n])
            act.wait_ge(*filled(("dl", t)))
            act.wait_ge(*taken("cols"))
            if t == 1:
                act.wait_ge(sg("dT_free"), 1)
            for h in range(H):
                ins = run(dx[0:n, h * n:(h + 1) * n], bank_of(("dl", t))[0:n, h * n:(h + 1) * n], ACT.Exp,
                          bias=cols[0:n, t, COL_RS, h:h + 1])
            ins.then_inc(freed(("dl", t)), 1)
            fill_at(t, 0)
            fill_at(t, 1)
            for point in (2, 3) if t < 2 else (2, 3, 4, 5):
                fill_at(t, point)
            if t:
                act.wait_ge(*filled(("haT", t - 1)))
            for g in range(2):
                act.wait_ge(*filled(("num", t, g)))
                ins = run(num[0:n, 256 * g:256 * g + 256].rearrange("p (h v) -> p h v", h=2),
                          bank_of(("num", t, g))[0:n, 0:2 * DA].rearrange("p (h v) -> p h v", h=2)[:, :, 0:DH],
                          ACT.Copy)
            ins.then_inc(sg("num_in"), 1)
            if t < 2:
                fill_at(t, 4)
            act.wait_ge(sg("ms"), t + 1)
            astep(run(hs4[0:n, 3, :], hs4[0:n, 3, :], ACT.Ln, scale=1.0 / DH, bias=EPS))
            run(hs4[0:n, 4, :], hs4[0:n, 3, :], ACT.Exp, scale=-0.5).then_inc(sg("ms_r"), 1)
        act.wait_ge(*filled(("haT", 2)))
        run(rowG, ROW_G, ACT.Copy).then_inc(sg("rowG"), 1)
        copy_out("nT", nrow, bank_of("nT")[0:NB * H + H, 0:128])

        act.preload_act_table_set("exp_and_others")
        act.wait_ge(sg("ha"), 3)
        for t, (t0, n) in enumerate(TILES):
            ins = run(mo[0:n, t, :], gout[0:n, t, :], ACT.Tanh, scale=0.5)
        ins.then_inc(sg("gout_e"), 1)
        for g in range(3):
            if g == 0:
                act.wait_ge(*filled(("haT", 2)))
            copy_out(("tail", g), tails[:, 512 * g:512 * g + 512], bank_of(("tail", g))[0:HIST * (NB + 1), :])
        act.wait_ge(sg("conv"), 3)
        for t, (t0, n) in enumerate(TILES):
            rows_out("xq", t, xq, QSCALE)
        for g in range(2):
            run(stmp[:, g % 2, :], cvT[:, 4 * g:4 * g + 4, :].rearrange("p c t -> p (c t)"), ACT.Tanh, scale=0.5) \
                .then_inc(sg("silu_e"), 1)
        for t, (t0, n) in enumerate(TILES):
            copy_out(("xqT", t), xqT[:, :, t0:t0 + n],
                     bank_of(("xqT", t))[:, 0:H * n].rearrange("p (h l) -> p h l", h=H))
        for i in range(2):
            act.wait_ge(sg("negmax"), i + 1)
            if i:
                act.wait_ge(*filled(("prT", i - 1, 1)))
            for h in range(H):
                name = ("xs", i, h // 2)
                ins = run(pr[:, h, :], bank_of(name)[:, MEM * (h % 2):MEM * (h % 2) + MEM], ACT.Exp,
                          bias=negmax[:, h:h + 1], accum_out=psumx[:, h:h + 1])
                if h % 2:
                    ins.then_inc(freed(name), 1)
            copy_out(("prT", i, 0), prT[:, 0, :], bank_of(("prT", i, 0)))
            copy_out(("hcT", i), brT[2][:, :, 128 * i:128 * i + 128],
                     bank_of(("hcT", i)).rearrange("p (h l) -> p h l", h=H))
        act.wait_ge(sg("cvT"), 1)
        run(stmp[:, 0, :], cvT[:, 8:12, :].rearrange("p c t -> p (c t)"), ACT.Tanh, scale=0.5) \
            .then_inc(sg("silu_e"), 1)
        for b in range(NB):
            if b >= 2:
                act.wait_ge(sg("K_read"), b - 1)
            copy_out(("KbT", b, 1), KTb[b % 2][:, 2:4, :].rearrange("p h m -> p (h m)"),
                     bank_of(("KbT", b, 1)))
        act.wait_ge(sg("negmax"), 3)
        act.wait_ge(*filled(("prT", 1, 1)))
        run(pr[:, 0, :], bank_of("ss")[:, 0:MEM], ACT.Exp, bias=negmax[:, 0:1], accum_out=psumx[:, 0:1]) \
            .then_inc(freed("ss"), 1)
        copy_out("hcs", hcs, bank_of("hcs")[:, 0:128])

        steps_m, parts_done = [0], [0]

        def merge_out(j, nn, t):
            wd = 512 if t < 2 else 128
            act.wait_ge(*filled(("mg", j, nn, t)))
            if steps_m[0] >= 2:
                act.wait_ge(sg("sig_read"), steps_m[0] - 1)
            run(sig[:, steps_m[0] % 2, 0:wd], bank_of(("mg", j, nn, t))[:, 0:wd], ACT.Tanh, scale=0.5) \
                .then_inc(freed(("mg", j, nn, t)), 1)
            steps_m[0] += 1

        def part():
            j, nn, t, x = PARTS[parts_done[0]]
            parts_done[0] += 1
            if x >= 2:
                merge_out(j, nn, t)

        def part_at(t, point):
            for _ in range(PART_AT[t][point]):
                if parts_done[0] < len(PARTS):
                    part()

        for t, (t0, n) in enumerate(TILES):
            if t:
                act.wait_ge(*filled(("hbT", t - 1)))
            else:
                act.wait_ge(*filled("hcsT"))
            for g in range(3):
                act.wait_ge(*filled(("raw", t, g)))
                copy_out(("raw", t, g), raw[0:n, g, :], bank_of(("raw", t, g))[0:n, :], wait=False)
            act.preload_act_table_set("natural_log_exp_and_others")
            act.wait_ge(sg("gss"), t + 1)
            astep(run(hs4[0:n, 0:2, :], hs4[0:n, 0:2, :], ACT.Ln, bias=EPS))
            run(hs4[0:n, 2:4, :], hs4[0:n, 0:2, :], ACT.Exp, scale=-0.5).then_inc(sg("gss_r"), 1)
            act.preload_act_table_set("exp_and_others")
            part_at(t, "raw")
            copy_out(("kT2", t), kT[:, 0:H * n], bank_of(("kT2", t))[:, 0:H * n])
            act.wait_ge(*filled(("dG", t)))
            if t == 0:
                act.wait_ge(sg("tail_out"), 32)
            for h in range(H):
                ins = run(dG[0:n, h * n:(h + 1) * n], bank_of(("dG", t))[0:n, h * n:(h + 1) * n], ACT.Exp,
                          bias=cols[0:n, t, COL_G, h:h + 1])
            ins.then_inc(freed(("dG", t)), 1)
            copy_out(("qT2", t), qT[:, 0:H * n], bank_of(("qT2", t))[:, 0:H * n])
            part_at(t, "forms")
            part_at(t, "KK")
            for k in range(1, 2 if t == 2 else LEVELS):
                copy_out(("X", t, k), Xm[0:n, 0:H * n], bank_of(("X", t, k))[0:n, 0:H * n])
                part_at(t, "level")
            copy_out(("wT", t), kbT[:, 0:H * n], bank_of(("wT", t))[:, 0:H * n], scale=-1.0)
            if t < 2:
                for c in range(2):
                    r = slice(L * c, L * c + L)
                    copy_out(("vn", t, c), vn[r, :], bank_of(("vn", t, c))[r, :])
                    part_at(t, "vn")
                    act.wait_ge(*filled(("go", t, c)))
                    copy_out(("go", t, c), Xm[r, :], bank_of(("go", t, c))[r, :], wait=False)
            else:
                for h in range(H):
                    copy_out(("vn2", h), vn[0:n, 128 * h:128 * h + 128], bank_of(("vn2", h))[0:n, 0:DH])
                    part_at(t, "vn")
                    copy_out(("go2", h), Xm[0:n, 128 * h:128 * h + 128], bank_of(("go2", h))[0:n, 0:DH])
            part_at(t, "hb")
            act.preload_act_table_set("natural_log_exp_and_others")
            act.wait_ge(sg("gs"), t + 1)
            astep(run(hs4[0:n, 6, :], hs4[0:n, 5, :], ACT.Ln, scale=1.0 / DH, bias=EPS))
            run(hs4[0:n, 7, :], hs4[0:n, 6, :], ACT.Exp, scale=-0.5).then_inc(sg("gs_r"), 1)
            act.preload_act_table_set("exp_and_others")

        while parts_done[0] < len(PARTS):
            part()
        for nn in range(2):
            for t in range(3):
                merge_out(1, nn, t)
        for t, (t0, n) in enumerate(TILES):
            copy_out(("mixT", t, 0), mixT[:, 0:4, t0:t0 + n],
                     bank_of(("mixT", t, 0))[:, 0:4 * n].rearrange("p (c l) -> p c l", c=4), scale=0.5)

        def rms_x2(t, n, where):
            astep(run(where[0:n, :], x2[0:n, t, :], ACT.Square, accum_out=rst[0:n, t:t + 1]))
            astep(run(rst[0:n, t:t + 1], rst[0:n, t:t + 1], ACT.Ln, scale=1.0 / D, bias=EPS))
            run(rst[0:n, t:t + 1], rst[0:n, t:t + 1], ACT.Exp, scale=-0.5).then_inc(sg("rst"), 1)

        act.preload_act_table_set("natural_log_exp_and_others")
        for t, (t0, n) in enumerate(TILES):
            act.wait_ge(sg("x2"), t + 1)
            rms_x2(t, n, Pm[:, 0, :])
        act.wait_ge(sg("lge"), 1)
        run(rtmp, rtmp, ACT.Exp).then_inc(sg("lge_r"), 1)
        act.wait_ge(sg("top"), 1)
        run(rt1[:, 5, :], rt1[:, 4, :], ACT.Exp).then_inc(sg("top_r"), 1)

        def slots_out(p=None):
            for e in range(E // 2):
                b, k = uses[("PwT", e)] if p is None else t_order(e, p)
                act.wait_ge(full[b], k + 1)
                run(PwT[:, e, :], PS[:, b, 0:T], ACT.Copy).then_inc(free[b], 1)

        slots_out()
        act.preload_act_table_set("exp_and_others")

        def group(p, g):
            it = 4 * p + g
            for pr_ in range(2):
                act.wait_ge(sg("pws_free"), it * 2 + (pr_ + 1))
                run(pws[pr_], PwT[:, bass.ds(g * 2 + pr_, 1), :].rearrange("p a t -> p (a t)"), ACT.Copy) \
                    .then_inc(sg("pws"), 1)
            for pr_ in range(2):
                for e in (2 * pr_, 2 * pr_ + 1):
                    act.wait_ge(*gfilled("gu", e, p, g))
                    act.wait_ge(sg("ea_free"), it * 4 + (e + 1))
                    run(ea[:, e % 2, :], gbank("gu", e)[:, 0:256], ACT.Tanh, scale=0.5).then_inc(sg("ea"), 1)
                for e in (2 * pr_, 2 * pr_ + 1):
                    act.wait_ge(*gfilled("aT", e, p, g))
                    if e < 2:
                        act.wait_ge(sg("act_free"), it * 4 + (e + 1))
                    else:
                        act.wait_ge(*gfilled("dn", 1, p, g))
                    run(actT[e % 2], gbank("aT", e)[:, 0:256], ACT.Copy).then_inc(gfree("aT", e), 1)
                act.wait_ge(*gfilled("dn", 2 * pr_, p, g))
                act.wait_ge(sg("outp_free"), it * 2 + (pr_ + 1))
                run(outp[:, 0:512], gbank("dn", 2 * pr_), ACT.Copy).then_inc(gfree("dn", 2 * pr_), 1)

        with act.Fori(0, G) as g:
            group(0, g)
        act.wait_ge(sg("flag"), 1)
        most = act.value_load(flag[0:1, 0:1], min_val=0, max_val=T)
        with act.If(most > SLOTS):
            with act.Fori(1, PASSES) as p:
                slots_out(p)
                with act.Fori(0, G) as g:
                    group(p, g)
        act.preload_act_table_set("natural_log_exp_and_others")
        for t, (t0, n) in enumerate(TILES):
            act.wait_ge(sg("x3"), 1)
            rms_x2(t, n, Pw[:, 0, :])

    @block.vector
    def _(dve):
        tt, ts, stt = dve.tensor_tensor, dve.tensor_scalar, dve.scalar_tensor_tensor
        cp = dve.tensor_copy

        marks = [0]

        def mark(sem_, n=1):
            marks[0] = (marks[0] + 1) % NSCRAP
            dve.memset(scrap[:, marks[0]:marks[0] + 1], 0.0).then_inc(sem_, n)

        dve.wait_ge(*filled("vec"))
        cp(vecT, bank_of("vec")[:, 0:NV]).then_inc(freed("vec"), 1)
        for i, j in enumerate((3, 4, 0, 1, 2)):
            n = NS if j == 2 else 128
            dve.wait_ge(sg("rstd"), i + 1)
            ts(xin[0:n, j, :], xin[0:n, j, :], rstd[0:n, j:j + 1], None, ALU.mult).then_inc(sg("x_norm"), 1)
        dve.wait_ge(*taken("vec"))
        for j in (3, 4, 0, 1, 2):
            n = NS if j == 2 else 128
            for hf in range(2):
                g0 = (V_MEM if j > 2 else V_MIX) + 4 * hf
                dst = memT[:, 4 * hf:4 * hf + 4, 128 * (j - 3):128 * (j - 2)] if j > 2 else \
                    hT[:, 4 * hf:4 * hf + 4, TILES[j][0]:TILES[j][0] + n]
                dve.wait_ge(*filled(("xT", j, hf)))
                tt(dst, bank_of(("xT", j, hf))[:, 0:4 * n].rearrange("p (c l) -> p c l", c=4),
                   bc(vecT[:, g0:g0 + 4].unsqueeze(2), 128, 4, n), ALU.mult).then_inc(freed(("xT", j, hf)), 1)

        dve.wait_ge(*filled("crow"))
        cp(cwT, bank_of("crow")[:, 0:NCT * (NB * HIST + CW)].rearrange("p (c r) -> p c r", c=NCT)) \
            .then_inc(freed("crow"), 1)

        dve.wait_ge(sg("small_in"), 16 * 9)
        dve.wait_ge(*filled("gates"))
        gt = bank_of("gates")
        ts(ROW_Z[:, 0, :], gt[32:32 + H, 0:T], bias4[:, 1:2], None, ALU.add)
        dstep(ts(ROW_Z[:, 1, :], gt[64:64 + H, 0:T], bias4[:, 2:3], None, ALU.add))
        stt(ROW_E, ROW_Z, -1.0, ROW_Z, ALU.mult, ALU.min).then_inc(sg("rowZ"), 1)
        dstep(ts(ROW_I, gt[0:H, 0:T], bias4[:, 0:1], None, ALU.add))
        dve.wait_ge(sg("rowB"), 1)
        dstep(ts(ROW_B, ROW_B, 1.0, None, ALU.add))
        dve.reciprocal(ROW_B, ROW_B).then_inc(freed("gates"), 1)
        dve.wait_ge(sg("rowL"), 1)
        dstep(stt(ROW_F, ROW_Z[:, 0, :], 0.0, ROW_E[:, 0, :], ALU.min, ALU.subtract))
        dstep(stt(ROW_A, ROW_Z[:, 1, :], 0.0, ROW_E[:, 1, :], ALU.max, ALU.add))
        dstep(ts(ROW_A, ROW_A, bias4[:, 4:5], -1.0, ALU.mult, ALU.mult))
        dve.wait_ge(sg("cst_in"), 16)
        dstep(dve.tensor_tensor_scan(ROW_BC, rset, ROW_F, 0.0, ALU.mult, ALU.add))
        dstep(dve.tensor_tensor_scan(ROW_G, rset, ROW_A, 0.0, ALU.mult, ALU.add))
        dstep(dve.tensor_tensor_scan(ROW_M[:, 0:SEQ], ROW_F[:, 0:SEQ], ROW_I[:, 0:SEQ], 0.0, ALU.add, ALU.max))

        def steps_of(r):
            return r[:, SEQ:T].rearrange("p (b s) -> p b s", b=NB)

        def chunks_of(r):
            return r[:, 0:SEQ].rearrange("p (c s) -> p c s", c=SEQ // L)

        fs, is_, ms = steps_of(ROW_F), steps_of(ROW_I), steps_of(ROW_M)
        for s in range(DS):
            dstep(tt(ms[:, :, s], m0 if s == 0 else ms[:, :, s - 1], fs[:, :, s], ALU.add))
            dstep(tt(ms[:, :, s], ms[:, :, s], is_[:, :, s], ALU.max))
        dstep(tt(ROW_RS, ROW_I, ROW_BC, ALU.subtract))
        dstep(tt(ROW_RL, ROW_BC, ROW_M, ALU.subtract))
        nch = SEQ // L
        for part, c, n in ((chunks_of, nch, L), (steps_of, NB, DS)):
            rl, rs, g, m = part(ROW_RL), part(ROW_RS), part(ROW_G), part(ROW_M)
            tt(part(ROW_W), rs, bc(rl[:, :, n - 1:n], H, c, n), ALU.add)
            tt(part(ROW_KD), bc(g[:, :, n - 1:n], H, c, n), g, ALU.subtract)
            if c == nch:
                tt(part(ROW_IW)[:, 1:, :], rl[:, 1:, :], bc(m[:, 0:c - 1, n - 1:n], H, c - 1, n), ALU.add)
                cp(part(ROW_IW)[:, 0, :], rl[:, 0, :])
            else:
                ins = tt(part(ROW_IW), rl, bc(m0.unsqueeze(2), H, c, n), ALU.add)
        ins.then_inc(sg("rowX"), 1)
        dve.wait_ge(sg("x_norm"), 5)
        for t, (t0, n) in enumerate(TILES):
            va = v_a[0:n, t, :].rearrange("p (h v) -> p h v", h=H)
            dve.wait_ge(*filled(("v", t)))
            dve.memset(va[:, :, DH:DA], 1.0)
            if t < 2:
                ins = cp(va[:, :, 0:DH], bank_of(("v", t)).rearrange("p (h v) -> p h v", h=H))
            else:
                for h in range(H):
                    ins = cp(va[:, h, 0:DH], bank_of(("v", t))[NS * h:NS * h + NS, 0:DH])
            ins.then_inc(freed(("v", t)), 1)
        for t, (t0, n) in enumerate(TILES):
            dve.wait_ge(*taken(("mo", t)))
            dstep(ts(mo[0:n, t, :], mo[0:n, t, :], 0.5, 0.5, ALU.mult, ALU.add))
        dve.memset(cin[:, :, 0:HIST], 0.0)
        cp(cis.rearrange("p c (b s) -> p c b s", b=NB)[:, :, :, 0:HIST],
           cwT[:, :, 0:NB * HIST].rearrange("p c (b s) -> p c b s", b=NB))
        dve.wait_ge(sg("memk_out"), 32)
        dve.memset(Cp, 0.0).then_inc(sg("C0"), 1)
        dve.wait_ge(*filled("cols"))
        for t, (t0, n) in enumerate(TILES):
            src = bank_of("cols")[0:n, 32 * t:32 * t + 32].rearrange("p (q h) -> p q h", h=H)
            ins = cp(cols[0:n, t, :, :], src)
            steps["dve"] += 1
            ins.then_inc(dve_step, 1)
        dve.wait_ge(dve_step, steps["dve"])
        for t, (t0, n) in enumerate(TILES):
            ins = ts(cols[0:n, t, COL_G, :], cols[0:n, t, COL_G, :], -1.0, None, ALU.mult)
        ins.then_inc(freed("cols"), 1)
        dve.wait_ge(*taken("cols"))
        dve.wait_ge(*filled("dec"))
        dstep(cp(dec, bank_of("dec")[:, 0:H * NCH].rearrange("p (h c) -> p h c", h=H)))
        cp(gl, bank_of("dec")[:, H * NCH:2 * H * NCH].rearrange("p (h c) -> p h c", h=H)) \
            .then_inc(freed("dec"), 1)
        dve.wait_ge(*taken("dec"))

        def spread(c, t, n, width=DH):
            return bc(cols[0:n, t, c, :].unsqueeze(2), n, H, width)

        def heads(x):
            return x.rearrange("p (h v) -> p h v", h=H)

        for t, (t0, n) in enumerate(TILES):
            qx, kx, qwx, dx, sx = forms(t)
            dve.wait_ge(*filled(("qT", t)))
            tt(heads(q_t[0:n, t, :]), heads(q_t[0:n, t, :]), spread(COL_IW, t, n), ALU.mult).then_inc(sg("qw"), 1)
            dve.wait_ge(*filled(("kT", t)))
            tt(heads(k_t[0:n, t, :]), heads(k_t[0:n, t, :]), spread(COL_W, t, n), ALU.mult).then_inc(sg("kw"), 1)
            dve.wait_ge(*filled(("qwT", t)))
            if t == 1:
                dve.wait_ge(*filled(("num", 0, 1)))
            cp(qwx[:, 0:H * n], bank_of(("qwT", t))[:, 0:H * n]).then_inc(freed(("qwT", t)), 1)
            dve.wait_ge(*taken(("dl", t)))
            dve.wait_ge(*filled(("sc", t)))
            dstep(tt(sx[0:n, 0:H * n], bank_of(("sc", t))[0:n, 0:H * n], dx[0:n, 0:H * n], ALU.mult))
            mark(freed(("sc", t)), 1)
            mark(sg("sT"), 1)

            def update(t, c):
                ch = 2 * t + c
                for g in range(2):
                    dve.wait_ge(*filled(("Cu", t, c, g)))
                    for h in (2 * g, 2 * g + 1):
                        u = bank_of(("Cu", t, c, g))[:, (h % 2) * DA:(h % 2 + 1) * DA]
                        ins = stt(Cp[:, h, :], Cp[:, h, :], dec[:, h, ch:ch + 1], u, ALU.mult, ALU.add)
                    ins.then_inc(freed(("Cu", t, c, g)), 1)
                dve.wait_ge(*taken(("Cu", t, c, 1)))

            if t < 2:
                update(t, 0)
                update(t, 1)
                if t == 1:
                    cp(nst[:, NB * H:], Cp[:, :, DH]).then_inc(sg("Cp"), 1)
            else:
                for h in range(H):
                    C = Cs[h % 2]
                    dve.wait_ge(sg(f"Cs_in{h % 2}"), 16 * (h // 2 + 1))
                    cp(C[:, :, DH], vecT[:, V_N0 + h:V_N0 + NB * H:H])
                    if h:
                        dve.wait_ge(*filled(("Cs", h - 1, 2)))
                    if h == 0:
                        dve.wait_ge(*taken(("qwT", t)))
                    tt(qwm, bc(qwx[:, h * n:(h + 1) * n].unsqueeze(1), 128, NB, n),
                       cst[:, C_BROW:C_BROW + NB * n].rearrange("p (b l) -> p b l", b=NB), ALU.mult) \
                        .then_inc(sg("qwm"), 1)
                    tt(vblk, bc(v_a[0:n, t, h * DA:(h + 1) * DA].unsqueeze(1), n, NB, DA),
                       bc(cst[0:n, C_BCOL:C_BCOL + NB].unsqueeze(2), n, NB, DA), ALU.mult) \
                        .then_inc(sg("vblk"), 1)
                    for g, (b0, b1) in enumerate(((0, 3), (3, 6), (6, 8))):
                        dve.wait_ge(*filled(("Cs", h, g)))
                        for b in range(b0, b1):
                            u = bank_of(("Cs", h, g))[:, (b - b0) * DA:(b - b0 + 1) * DA]
                            ins = stt(C[:, b, :], C[:, b, :], dec[:, h, 4 + b:5 + b], u, ALU.mult, ALU.add)
                        ins.then_inc(freed(("Cs", h, g)), 1)
                    dve.wait_ge(*taken(("Cs", h, 2)))
                    cp(nst[:, h:NB * H:H], C[:, :, DH]).then_inc(sg("Cs"), 1)
            dve.wait_ge(sg("num_in"), t + 1)
            for g in range(2):
                ins = cp(hs4[0:n, 0, 2 * g:2 * g + 2],
                         bank_of(("num", t, g))[0:n, 0:2 * DA].rearrange("p (h v) -> p h v", h=2)[:, :, DH])
                ins.then_inc(freed(("num", t, g)), 1)
            dve.wait_ge(*taken(("num", t, 1)))
            dve.wait_ge(*taken(("num", t, 0)))
            dstep(stt(hs4[0:n, 1, :], hs4[0:n, 0, :], -1.0, hs4[0:n, 0, :], ALU.mult, ALU.max))
            dstep(tt(hs4[0:n, 1, :], hs4[0:n, 1, :], cols[0:n, t, COL_EN, :], ALU.max))
            dstep(dve.reciprocal(hs4[0:n, 1, :], hs4[0:n, 1, :]))
            dstep(tt(dx[0:n, 0:128 * H] if t < 2 else dT[0:n, :], num[0:n, :], num[0:n, :], ALU.mult))
            dstep(dve.tensor_reduce(hs4[0:n, 2, :], heads(dT[0:n, :]), AX.X, ALU.add))
            if t == 0:
                mark(sg("dT_free"), 1)
            dstep(tt(hs4[0:n, 2, :], hs4[0:n, 2, :], hs4[0:n, 1, :], ALU.mult))
            tt(hs4[0:n, 3, :], hs4[0:n, 2, :], hs4[0:n, 1, :], ALU.mult).then_inc(sg("ms"), 1)
            dve.wait_ge(sg("ms_r"), t + 1)
            dstep(tt(hs4[0:n, 5, :], hs4[0:n, 4, :], hs4[0:n, 1, :], ALU.mult))
            dstep(tt(heads(num[0:n, :]), heads(num[0:n, :]), bc(hs4[0:n, 5, :].unsqueeze(2), n, H, DH), ALU.mult))
            tt(num[0:n, :], num[0:n, :], mo[0:n, t, :], ALU.mult).then_inc(sg("ha"), 1)
            dve.wait_ge(*filled(("haT", t)))
            tt(brT[0][:, :, t0:t0 + n], bank_of(("haT", t))[:, 0:H * n].rearrange("p (h l) -> p h l", h=H),
               bc(vecT[:, V_ML:V_ML + H].unsqueeze(2), 128, H, n), ALU.mult).then_inc(freed(("haT", t)), 1)
        dve.wait_ge(*taken(("haT", 2)))
        dve.wait_ge(sg("Cs"), 4)
        mark(sg("nst"), 1)

        tl = tailT.rearrange("p c (b s) -> p c b s", s=HIST)
        dve.wait_ge(*taken(("cv", NCT - 1)))
        cp(tl[:, :, 0, :], cin[:, :, SEQ:SEQ + HIST])
        cp(tl[:, :, 1:, :], cis.rearrange("p c (b s) -> p c b s", b=NB)[:, :, :, DS:DS + HIST]) \
            .then_inc(sg("tailT"), 1)
        dve.wait_ge(*filled(("Cs", H - 1, 2)))
        for g in range(3):
            for j in range(CW):
                for c in range(4 * g, 4 * g + 4):
                    w = cwT[:, c, NB * HIST + j:NB * HIST + j + 1]
                    xp = cin[:, c, j:j + SEQ]
                    xs = cis[:, c, :].rearrange("p (b s) -> p b s", b=NB)[:, :, j:j + DS]
                    op_, os_ = cvT[:, c, 0:SEQ], cvT[:, c, SEQ:T].rearrange("p (b s) -> p b s", b=NB)
                    if j == 0:
                        ts(op_, xp, w, None, ALU.mult)
                        ins = ts(os_, xs, w, None, ALU.mult)
                    else:
                        stt(op_, xp, w, op_, ALU.mult, ALU.add)
                        ins = stt(os_, xs, w, os_, ALU.mult, ALU.add)
                if j < CW - 1:
                    dstep(ins)
            ins.then_inc(sg("conv"), 1)
        dve.wait_ge(sg("gout_e"), 1)
        for t, (t0, n) in enumerate(TILES):
            stt(gout[0:n, t, :], mo[0:n, t, :], 1.0, gout[0:n, t, :], ALU.add, ALU.mult)
        mark(sg("gout"))

        def silu(g):
            e = stmp[:, g % 2, :]
            v = cvT[:, 4 * g:4 * g + 4, :].rearrange("p c t -> p (c t)")
            dve.wait_ge(sg("silu_e"), g + 1)
            dstep(ts(e, e, 0.5, 0.5, ALU.mult, ALU.add))
            tt(v, v, e, ALU.mult).then_inc(sg("cvT"), 1)
            dve.wait_ge(sg("cvT"), g + 1)

        dve.wait_ge(sg("gout"), 1)
        dve.wait_ge(*taken(("xqT", 2)))
        tt(qm.rearrange("p h (b l) -> p h b l", b=NB), bc(xqT[:, :, SEQ:T].unsqueeze(2), 128, H, NB, NS),
           bc(cst[:, C_BROW:C_BROW + NB * NS].rearrange("p (b l) -> p b l", b=NB).unsqueeze(1),
              128, H, NB, NS), ALU.mult).then_inc(sg("qm"), 1)
        for i in range(2):
            for g in range(2):
                dve.wait_ge(*filled(("xs", i, g)))
                ins = dve.tensor_reduce(negmax[:, 2 * g:2 * g + 2],
                                        bank_of(("xs", i, g)).rearrange("p (h m) -> p h m", h=2),
                                        AX.X, ALU.max, negate=True)
            ins.then_inc(sg("negmax"), 1)
            silu(i)
            dve.wait_ge(*taken(("xs", i, 1)))
            dstep(dve.reciprocal(psumx, psumx))
            tt(pr, pr, bc(psumx.unsqueeze(2), 128, H, MEM), ALU.mult).then_inc(sg("pr"), 1)
            if i:
                dve.wait_ge(*filled(("hcT", 0)))
            dve.wait_ge(*filled(("prT", i, 1)))
            cp(prT[:, 1, :], bank_of(("prT", i, 1))).then_inc(freed(("prT", i, 1)), 1)
        for b in range(NB):
            dve.wait_ge(*filled(("KbT", b, 0)))
            if b >= 2:
                dve.wait_ge(sg("K_read"), b - 1)
            cp(KTb[b % 2][:, 0:2, :].rearrange("p h m -> p (h m)"), bank_of(("KbT", b, 0))) \
                .then_inc(freed(("KbT", b, 0)), 1)
            if b == 1:
                silu(2)
        dve.wait_ge(*filled("ss"))
        dve.tensor_reduce(negmax[:, 0:1], bank_of("ss")[:, 0:MEM], AX.X, ALU.max, negate=True) \
            .then_inc(sg("negmax"), 1)
        dve.wait_ge(*taken("ss"))
        dstep(dve.reciprocal(psumx[:, 0:1], psumx[:, 0:1]))
        ts(pr[:, 0, :], pr[:, 0, :], psumx[:, 0:1], None, ALU.mult).then_inc(sg("pr"), 1)
        dve.wait_ge(*filled("spT"))
        for m in range(2):
            ins = tt(spT[:, m, :].rearrange("p (b h l) -> p b h l", b=NB, h=H),
                     bc(bank_of("spT")[:, 128 * m:128 * m + 128].rearrange("p (h l) -> p h l", h=H).unsqueeze(1),
                        128, NB, H, NS),
                     bc(cst[:, C_BROW:C_BROW + NB * NS].rearrange("p (b l) -> p b l", b=NB).unsqueeze(2),
                        128, NB, H, NS), ALU.mult)
        ins.then_inc(freed("spT"), 1)
        dve.wait_ge(*filled("hcsT"))
        cp(brT[2][:, :, SEQ:T], bank_of("hcsT")[:, 0:128].rearrange("p (h l) -> p h l", h=H)) \
            .then_inc(freed("hcsT"), 1)
        dve.wait_ge(*taken("hcsT"))

        parts_done = [0]

        def merge_out(j, nn, t):
            wd = 512 if t < 2 else 128
            s = sig[:, steps_m[0] % 2, 0:wd]
            mx = mixed[:, t, 512 * nn:512 * nn + 512] if t < 2 else mixs[:, nn, :]
            dve.wait_ge(*taken(("mg", j, nn, t)))
            dve.wait_ge(*filled(("mb", j, nn, t)))
            o = bank_of(("mb", j, nn, t))[:, 0:wd]
            dst = mx if j == 0 else s
            stt(dst, s, 1.0, o, ALU.add, ALU.mult).then_inc(freed(("mb", j, nn, t)), 1)
            dve.wait_ge(*taken(("mb", j, nn, t)))
            if j:
                tt(mx, mx, s, ALU.add).then_inc(sg("sig_read"), 1)
            else:
                mark(sg("sig_read"))
            steps_m[0] += 1

        steps_m = [0]

        def part():
            j, nn, t, x = PARTS[parts_done[0]]
            parts_done[0] += 1
            if x >= 2:
                merge_out(j, nn, t)

        def part_at(t, point):
            for _ in range(PART_AT[t][point]):
                if parts_done[0] < len(PARTS):
                    part()

        dve.memset(Sp, 0.0).then_inc(sg("S0"), 1)
        for t, (t0, n) in enumerate(TILES):
            dve.wait_ge(*taken(("raw", t, 2)))
            q, k, v = (heads(raw[0:n, j, :]) for j in range(3))
            dstep(tt(kd[0:n, :], raw[0:n, 0, :], raw[0:n, 0, :], ALU.mult))
            dstep(tt(kbg[0:n, :], raw[0:n, 1, :], raw[0:n, 1, :], ALU.mult))
            dstep(dve.tensor_reduce(hs4[0:n, 0, :], heads(kd[0:n, :]), AX.X, ALU.add))
            dve.tensor_reduce(hs4[0:n, 1, :], heads(kbg[0:n, :]), AX.X, ALU.add).then_inc(sg("gss"), 1)
            dve.wait_ge(sg("gss_r"), t + 1)
            s4 = lambda j: hs4[0:n, j, :]
            wide = lambda x: bc(x.unsqueeze(2), n, H, DH)
            dstep(tt(s4(4), s4(3), cols[0:n, t, COL_B, :], ALU.mult))
            dstep(tt(s4(8), s4(4), cols[0:n, t, COL_EG, :], ALU.mult))
            dstep(tt(s4(9), s4(3), cols[0:n, t, COL_KD, :], ALU.mult))
            dstep(ts(s4(2), s4(2), QSCALE, None, ALU.mult))
            dstep(tt(s4(10), s4(2), cols[0:n, t, COL_EG, :], ALU.mult))
            tt(heads(kbg[0:n, :]), k, wide(s4(8)), ALU.mult)
            tt(heads(kd[0:n, :]), k, wide(s4(9)), ALU.mult)
            tt(heads(kb[0:n, :]), k, wide(s4(4)), ALU.mult)
            tt(heads(qd[0:n, :]), q, wide(s4(10)), ALU.mult)
            tt(v, v, spread(COL_B, t, n), ALU.mult).then_inc(sg("gv"), 1)
            dve.wait_ge(sg("gv"), t + 1)
            tt(k, k, wide(s4(3)), ALU.mult).then_inc(sg("gq"), 1)
            tt(q, q, wide(s4(2)), ALU.mult).then_inc(sg("gq"), 1)
            mark(sg("gq"), 1)
            mark(sg("gq"), 1)
            part_at(t, "raw")
            dve.wait_ge(*filled(("kbT", t)))
            cp(kbT[:, 0:H * n], bank_of(("kbT", t))[:, 0:H * n]).then_inc(freed(("kbT", t)), 1)
            dve.wait_ge(*filled(("qdT", t)))
            cp(qdT[:, 0:H * n], bank_of(("qdT", t))[:, 0:H * n]).then_inc(freed(("qdT", t)), 1)
            dve.wait_ge(*taken(("dG", t)))
            dve.wait_ge(*filled(("KK", t)))
            tt(AT[0:n, 0:H * n], bank_of(("KK", t))[0:n, 0:H * n], dG[0:n, 0:H * n], ALU.mult) \
                .then_inc(freed(("KK", t)), 1)
            dve.wait_ge(*filled(("QK", t)))
            tt(QKT[0:n, 0:H * n], bank_of(("QK", t))[0:n, 0:H * n], dG[0:n, 0:H * n], ALU.mult) \
                .then_inc(freed(("QK", t)), 1)
            dve.wait_ge(*taken(("QK", t)))
            part_at(t, "forms")
            part_at(t, "KK")
            blocks = lambda x: x[0:n, 0:H * n].rearrange("p (h l) -> p h l", h=H)
            idb = bc(ident[0:n, 0:n].unsqueeze(1), n, H, n)
            nl = 2 if t == 2 else LEVELS
            for lev in range(nl):
                mk_ = cst[0:n, C_LVL + 128 * lev:C_LVL + 128 * lev + n]
                tt(blocks(dG), blocks(AT), bc(mk_.unsqueeze(1), n, H, n), ALU.mult).then_inc(sg("ATk"), 1)
                dve.wait_ge(sg("ATk"), lv(t, lev) + 1)
                if lev == 0:
                    dstep(tt(blocks(Um), idb, blocks(dG), ALU.subtract))
                    dve.wait_ge(*filled(("X", t, 0)))
                    tt(blocks(Tm), idb, bank_of(("X", t, 0))[0:n, 0:H * n].rearrange("p (h l) -> p h l", h=H),
                       ALU.subtract).then_inc(freed(("X", t, 0)), 1)
                    dve.wait_ge(*taken(("X", t, 0)))
                    continue
                if lev < nl - 1:
                    dve.wait_ge(*filled(("Y", t, lev)))
                    tt(Tm[0:n, 0:H * n], Tm[0:n, 0:H * n], bank_of(("Y", t, lev))[0:n, 0:H * n], ALU.subtract) \
                        .then_inc(freed(("Y", t, lev)), 1)
                    dve.wait_ge(*taken(("Y", t, lev)))
                dve.wait_ge(*filled(("YT", t, lev)))
                tt(Um[0:n, 0:H * n], Um[0:n, 0:H * n], bank_of(("YT", t, lev))[0:n, 0:H * n], ALU.subtract) \
                    .then_inc(freed(("YT", t, lev)), 1)
                dve.wait_ge(*taken(("YT", t, lev)))
                part_at(t, "level")
            if t < 2:
                for c in range(2):
                    ch = 2 * t + c
                    part_at(t, "vn")
                    dve.wait_ge(*filled(("go", t, c)))
                    dve.wait_ge(*filled(("So", t, c)))
                    for h in range(H):
                        hv = slice(128 * h, 128 * h + 128)
                        ins = stt(Sp[:, hv], Sp[:, hv], gl[:, h, ch:ch + 1], bank_of(("So", t, c))[:, hv],
                                  ALU.mult, ALU.add)
                    ins.then_inc(freed(("So", t, c)), 1)
                    dve.wait_ge(*taken(("So", t, c)))
                if t == 1:
                    mark(sg("Spout"), 1)
            else:
                dve.wait_ge(*taken(("wT", t)))
                for h in range(H):
                    if h:
                        dve.wait_ge(*filled(("So2", h - 1, 1)))
                    dve.wait_ge(sg(f"Ss_in{h % 2}"), 16 * (h // 2 + 1))
                    brow = cst[:, C_BROW:C_BROW + NB * n].rearrange("p (b l) -> p b l", b=NB)
                    tt(qdm, bc(qdT[:, h * n:(h + 1) * n].unsqueeze(1), 128, NB, n), brow, ALU.mult)
                    tt(nwm, bc(kbT[:, h * n:(h + 1) * n].unsqueeze(1), 128, NB, n), brow, ALU.mult) \
                        .then_inc(sg("nwm"), 1)
                    dve.wait_ge(*taken(("vn2", h)))
                    tt(vnb, bc(vn[0:n, 128 * h:128 * h + 128].unsqueeze(1), n, NB, DH),
                       bc(cst[0:n, C_BCOL:C_BCOL + NB].unsqueeze(2), n, NB, DH), ALU.mult).then_inc(sg("vnb"), 1)
                    part_at(t, "vn")
                    for g in range(2):
                        dve.wait_ge(*filled(("So2", h, g)))
                        for b in range(4 * g, 4 * g + 4):
                            ins = stt(Ss[h % 2][:, b, :], Ss[h % 2][:, b, :], gl[:, h, 4 + b:5 + b],
                                      bank_of(("So2", h, g))[:, 128 * (b - 4 * g):128 * (b - 4 * g) + 128],
                                      ALU.mult, ALU.add)
                        ins.then_inc(freed(("So2", h, g)), 1)
                    mark(sg("Ssd"), 1)
                    dve.wait_ge(sg("Ssd"), h + 1)
            part_at(t, "hb")
            dve.wait_ge(*taken(("go", t, 1) if t < 2 else ("go2", H - 1)))
            dstep(tt(AT[0:n, :], Xm[0:n, :], Xm[0:n, :], ALU.mult))
            dve.tensor_reduce(hs4[0:n, 5, :], heads(AT[0:n, :]), AX.X, ALU.add).then_inc(sg("gs"), 1)
            dve.wait_ge(sg("gs_r"), t + 1)
            dstep(tt(heads(kb[0:n, :]), heads(Xm[0:n, :]), wide(s4(7)), ALU.mult))
            tt(kb[0:n, :], kb[0:n, :], gout[0:n, t, :], ALU.mult).then_inc(sg("hb"), 1)
            dve.wait_ge(*filled(("hbT", t)))
            ts(brT[1][:, :, t0:t0 + n], bank_of(("hbT", t))[:, 0:H * n].rearrange("p (h l) -> p h l", h=H),
               vecT[:, V_GD:V_GD + 1], 0.5, ALU.mult, ALU.mult).then_inc(freed(("hbT", t)), 1)

        while parts_done[0] < len(PARTS):
            part()
        for nn in range(2):
            for t in range(3):
                merge_out(1, nn, t)
        dve.wait_ge(sg("sig_read"), 18)
        for t in range(3):
            mark(sg("mixed"), 1)
        for t, (t0, n) in enumerate(TILES):
            dve.wait_ge(*filled(("mixT", t, 1)))
            ts(mixT[:, 4:8, t0:t0 + n], bank_of(("mixT", t, 1))[:, 0:4 * n].rearrange("p (c l) -> p c l", c=4),
               0.5, None, ALU.mult) \
                .then_inc(freed(("mixT", t, 1)), 1)
        dve.wait_ge(sg("x2_in"), 48)
        for nn in range(2):
            for t, (t0, n) in enumerate(TILES):
                name = (("out", nn), t)
                dve.wait_ge(*filled(name))
                if t < 2:
                    xx = x2[:, t, 512 * nn:512 * nn + 512]
                    ins = tt(xx, xx, bank_of(name), ALU.add)
                else:
                    for c in range(4):
                        xx = x2[0:NS, t, 512 * nn + 128 * c:512 * nn + 128 * c + 128]
                        ins = tt(xx, xx, bank_of(name)[NS * c:NS * c + NS, 0:128], ALU.add)
                ins.then_inc(freed(name), 1)
        for t, (t0, n) in enumerate(TILES):
            dve.wait_ge(*taken((("out", 1), t)))
            mark(sg("x2"), 1)

        for t, (t0, n) in enumerate(TILES):
            dve.wait_ge(sg("rst"), t + 1)
            ts(h2p[0:n, t, :].rearrange("p (c f) -> p f c", c=KD), x2[0:n, t, :].rearrange("p (f c) -> p f c", c=KD),
               rst[0:n, t:t + 1], None, ALU.mult).then_inc(sg("h2p"), 1)
        for t, (t0, n) in enumerate(TILES):
            for hf in range(2):
                dve.wait_ge(*filled(("h2T", t, hf)))
                tt(h2T[:, 4 * hf:4 * hf + 4, t0:t0 + n],
                   bank_of(("h2T", t, hf))[:, 0:4 * n].rearrange("p (c l) -> p c l", c=4),
                   bc(gffn[:, 4 * hf:4 * hf + 4].unsqueeze(2), 128, 4, n), ALU.mult) \
                    .then_inc(freed(("h2T", t, hf)), 1)
        dve.wait_ge(*filled("lgT"))
        ts(lgT[0:20, :], bank_of("lgT")[0:20, 0:T], brt, None, ALU.add).then_inc(freed("lgT"), 1)
        dstep(dve.memset(LG, 0.0))
        dve.wait_ge(*filled("lg"))
        for t, (t0, n) in enumerate(TILES):
            ins = cp(LG[0:n, t, :], bank_of("lg")[0:n, 20 * t:20 * t + 20])
        ins.then_inc(freed("lg"), 1)
        dve.wait_ge(*taken("lg"))
        first = cst[:, C_FIRST:C_FIRST + 3 * EG]
        flat = lambda x: x.rearrange("p t e -> p (t e)")
        w4 = lambda x: bc(x.unsqueeze(2), 128, 3, 4)

        def best(o, x, m):
            dstep(dve.tensor_reduce(m, x, AX.X, ALU.max))
            dstep(tt(le4[:, :, 0:4], x, w4(m), ALU.is_equal))
            dstep(cp(le4[:, :, 4:8], le4[:, :, 0:4]))
            dstep(cp(flat(oh2), le4[:, :, 4:8]))
            dstep(dve.tensor_tensor_scan(le12, first, flat(oh2), 0.0, ALU.mult, ALU.add))
            dstep(stt(flat(o), le12, 1.0, flat(oh2), ALU.is_equal, ALU.mult))

        best(oh, LG[:, :, 0:G], rt1[:, 0, :])
        tt(rtmp, LG[:, :, 0:G], w4(rt1[:, 0, :]), ALU.subtract).then_inc(sg("lge"), 1)
        le = LG[:, :, G:20]
        lesel = rkm[:, :, 0:4]
        for g in range(G):
            dstep(tt(le4[:, :, 4 * g:4 * g + 4], le[:, :, 4 * g:4 * g + 4], bc(oh[:, :, g:g + 1], 128, 3, 4), ALU.mult))
        dstep(tt(le4[:, :, 0:8], le4[:, :, 0:8], le4[:, :, 8:16], ALU.add))
        dstep(tt(lesel, le4[:, :, 0:4], le4[:, :, 4:8], ALU.add))
        best(oh1, lesel, rt1[:, 1, :])
        dstep(stt(lesel, oh1, NEG, lesel, ALU.mult, ALU.add))
        best(oh3, lesel, rt1[:, 2, :])
        tt(rt1[:, 4, :], rt1[:, 2, :], rt1[:, 1, :], ALU.subtract).then_inc(sg("top"), 1)
        dve.wait_ge(sg("lge_r"), 1)
        dstep(dve.tensor_reduce(rt1[:, 3, :], rtmp, AX.X, ALU.add))
        dstep(dve.reciprocal(rt1[:, 3, :], rt1[:, 3, :]))
        dve.wait_ge(sg("top_r"), 1)
        dstep(ts(rt1[:, 6, :], rt1[:, 5, :], 1.0, None, ALU.add))
        dstep(dve.reciprocal(rt1[:, 6, :], rt1[:, 6, :]))
        dstep(tt(rt1[:, 6, :], rt1[:, 6, :], rt1[:, 3, :], ALU.mult))
        dstep(tt(rt1[:, 7, :], rt1[:, 6, :], rt1[:, 5, :], ALU.mult))
        dstep(tt(rtmp, oh1, w4(rt1[:, 6, :]), ALU.mult))
        dstep(tt(le4[:, :, 0:4], oh3, w4(rt1[:, 7, :]), ALU.mult))
        dstep(tt(rtmp, rtmp, le4[:, :, 0:4], ALU.add))
        dstep(tt(oh1, oh1, oh3, ALU.add))
        for g in range(G):
            tt(cmb[:, :, 4 * g:4 * g + 4], rtmp, bc(oh[:, :, g:g + 1], 128, 3, 4), ALU.mult)
            ins = tt(msk[:, :, 4 * g:4 * g + 4], oh1, bc(oh[:, :, g:g + 1], 128, 3, 4), ALU.mult)
        ins.then_inc(sg("msk"), 1)
        dve.wait_ge(sg("msk"), 1)
        dve.wait_ge(*filled("rank"))
        dstep(dve.memset(rkm, 0.0))
        for t, (t0, n) in enumerate(TILES):
            dstep(stt(rkm[0:n, t, :], bank_of("rank")[0:n, E * t:E * t + E], 1.0, msk[0:n, t, :], ALU.add, ALU.mult))
        dstep(dve.tensor_reduce(rt1[0:1, 11, 0:1], bank_of("rank")[0:1, 3 * E:4 * E], AX.X, ALU.max))
        cp(flag[0:1, 0:1], rt1[0:1, 11, 0:1]).then_inc(sg("flag"), 1)
        mark(freed("rank"), 1)

        def choices(p):
            k = 0

            def then(ins):
                nonlocal k
                k += 1
                ins.then_inc(sg("choice"), 1)
                dve.wait_ge(sg("choice"), 7 * p + k)

            then(ts(le4, rkm, -1.0, None, ALU.add))
            for t, (t0, n) in enumerate(TILES):
                P4 = Pm[0:n, t, :].rearrange("p (e j) -> p e j", e=E)
                W4 = Pw[0:n, t, :].rearrange("p (e j) -> p e j", e=E)
                then(tt(P4, bc(cst[0:n, C_IOTA:C_IOTA + SLOTS].unsqueeze(1), n, E, SLOTS),
                        bc(le4[0:n, t, :].unsqueeze(2), n, E, SLOTS), ALU.is_equal))
                then(tt(W4, P4, bc(cmb[0:n, t, :].unsqueeze(2), n, E, SLOTS), ALU.mult))
            mark(sg("Pm"))

        choices(0)
        mark(sg("pws_free"), 2)
        mark(sg("ea_free"), 2)
        mark(sg("act_free"), 2)
        mark(sg("outp_free"), 1)

        def group(p, g):
            it = 4 * p + g
            for j in range(4):
                dve.wait_ge(*gfilled("hg", j, p, g))
                tt(hg[:, 2 * j:2 * j + 2, :], gbank("hg", j).rearrange("p (c l) -> p c l", c=2),
                   bc(gffn[:, 2 * j:2 * j + 2].unsqueeze(2), 128, 2, 256), ALU.mult).then_inc(gfree("hg", j), 1)
            for pr_ in range(2):
                for e in (2 * pr_, 2 * pr_ + 1):
                    ee, ab = ea[:, e % 2, :], actb[:, e % 2, :]
                    dve.wait_ge(sg("ea"), it * 4 + (e + 1))
                    stt(ee, ee, 1.0, gbank("gu", e)[:, 0:256], ALU.add, ALU.mult).then_inc(sg("silu"), 1)
                    dve.wait_ge(sg("silu"), it * 4 + (e + 1))
                    stt(ab, ee, 0.5, gbank("gu", e)[:, 256:512], ALU.mult, ALU.mult).then_inc(sg("act"), 1)
                    dve.wait_ge(sg("act"), it * 4 + (e + 1))
                    mark(gfree("gu", e), 1)
                    mark(sg("ea_free"), 1)
                if pr_ == 1:
                    add_y(0, p, g)
                dve.wait_ge(*gfilled("dn", 2 * pr_ + 1, p, g))
                if pr_ == 1:
                    pass
                dve.wait_ge(sg("outp_free"), it * 2 + (pr_ + 1))
                cp(outp[:, 512:1024], gbank("dn", 2 * pr_ + 1)).then_inc(gfree("dn", 2 * pr_ + 1), 1)
            add_y(1, p, g)
            mark(sg("act_free"), 4)
            mark(sg("pws_free"), 2)

        def add_y(pr_, p, g):
            it = 4 * p + g
            for t, (t0, n) in enumerate(TILES):
                for nn in range(2):
                    j = 6 * pr_ + 2 * t + nn
                    dve.wait_ge(*gfilled("y", j, p, g))
                    xx = x2[0:n, t, 512 * nn:512 * nn + 512]
                    ins = tt(xx, xx, gbank("y", j)[0:n, :], ALU.add)
                    ins.then_inc(gfree("y", j), 1)
            mark(sg("outp_free"), 1)

        with dve.Fori(0, G) as g:
            group(0, g)
        dve.wait_ge(sg("flag"), 1)
        most = dve.value_load(flag[0:1, 0:1], min_val=0, max_val=T)
        with dve.If(most > SLOTS):
            with dve.Fori(1, PASSES) as p:
                for e in (2, 3):
                    dve.wait_ge(*moved("dn", e, p - 1, G - 1))
                dve.wait_ge(*moved("y", 11, p - 1, G - 1))
                ts(rkm, rkm, -float(SLOTS), None, ALU.add).then_inc(sg("shift"), 1)
                dve.wait_ge(sg("shift"), p)
                choices(p)
                with dve.Fori(0, G) as g:
                    group(p, g)
        mark(sg("x3"), 1)
        dve.wait_ge(sg("gfin_in"), 16)
        for t, (t0, n) in enumerate(TILES):
            dve.wait_ge(sg("rst"), 4 + t)
            stt(x2[0:n, t, :], x2[0:n, t, :], rst[0:n, t:t + 1], gfin[0:n, :], ALU.mult, ALU.mult) \
                .then_inc(sg("y"), 1)

    ctx.close()


_OUTS = [("y_prompt", (1, SEQ, D)), ("y_sample", (NB, DS, D)),
         ("mem_k", (1, 1, MEM, H, DH)), ("mem_v", (1, 1, MEM, H, DH)),
         ("C_p", (1, 1, H, DH, DH)), ("n_p", (1, 1, H, DH)), ("m_p", (1, 1, H)), ("S_p", (1, 1, H, DH, DH)),
         ("conv_p", (1, 1, HIST, CCH)),
         ("C_s", (1, NB, H, DH, DH)), ("n_s", (1, NB, H, DH)), ("m_s", (1, NB, H)), ("S_s", (1, NB, H, DH, DH)),
         ("conv_s", (1, NB, HIST, CCH))]


def kernel(**inputs):
    import concourse.bacc as bacc
    from concourse.bass_utils import run_bass_kernel_spmd

    nc = bacc.Bacc("TRN2", target_bir_lowering=False, num_devices=1)
    arrays, a, out = {}, {}, {}
    for name in inputs:
        x = np.ascontiguousarray(inputs[name])
        arrays[f"in_{name}"] = x
        a[name] = nc.dram_tensor(f"in_{name}", x.shape, mybir.dt.from_np(x.dtype), kind="ExternalInput").ap()
    arrays["in_table"] = constants()
    a["table"] = nc.dram_tensor("in_table", (128, C_ALL), F32, kind="ExternalInput").ap()
    for name, shape in _OUTS:
        out[name] = nc.dram_tensor(f"out_{name}", shape, F32, kind="ExternalOutput").ap()
    build(nc, a, out)
    r = run_bass_kernel_spmd(nc, [arrays], core_ids=[0])
    return tuple(r.results[0][f"out_{name}"] for name, _ in _OUTS)
```

```python
from contextlib import ExitStack

import numpy as np
import concourse.bass as bass
from concourse import mybir

F32 = mybir.dt.float32
I32 = mybir.dt.int32
ALU = mybir.AluOpType
ACT = mybir.ActivationFunctionType
AX = mybir.AxisListType

D = 1024
KD = D // 128
SEQ, NB, DS = 256, 8, 4
NS = NB * DS
T = SEQ + NS
TILES = [(0, 128), (128, 128), (SEQ, NS)]
H, DH = 4, 128
W = H * DH
DA = DH + 1
L = 64
NCH = SEQ // L + NB
CW = 4
CCH = 3 * W
NCT = CCH // 128
HIST = CW - 1
MEM = 256
G, EG = 4, 4
E = G * EG
SLOTS = 64
EPS = 1e-6
NEG = -1e30
RING, UNIT = 6, 4096
RING0 = 4
NSCRAP = 40
ARENA, SMALL = 19056, 1620
QSCALE = DH ** -0.5
PASSES = -(-T // SLOTS)
LEVELS = 6

O_Q, O_K, O_V = 0, W, 2 * W
O_IF = 3 * W
O_MO = O_IF + 2 * H
O_GQKV = O_MO + W
O_GAB = O_GQKV + CCH
O_GOUT = O_GAB + 2 * H
O_XQ = O_GOUT + W
O_GATE = O_XQ + W

C_ID, C_NEGP, C_NEGS, C_LVL = 0, 128, 256, 288
C_SEL = C_LVL + LEVELS * 128
C_BROW = C_SEL + H * 128
C_BCOL = C_BROW + NB * NS
C_IOTA = C_BCOL + NB
C_TRI = C_IOTA + SLOTS
C_FIRST = C_TRI + 128
C_N = C_FIRST + 3 * EG
C_RST = C_N
C_ALL = C_RST + T


def constants():
    t = np.zeros((128, C_ALL), np.float32)
    s, l = np.arange(128)[:, None], np.arange(128)[None, :]
    t[:, C_ID:C_ID + 128] = s == l
    t[:, C_NEGP:C_NEGP + 128] = np.where((s // L == l // L) & (s <= l), 0, NEG)
    t[:NS, C_NEGS:C_NEGS + NS] = np.where((s // DS == l // DS) & (s <= l), 0, NEG)[:NS, :NS]
    for k in range(LEVELS):
        n = 1 << k
        t[:, C_LVL + 128 * k:C_LVL + 128 * (k + 1)] = (s // n + 1 == l // n) & (l // n % 2 == 1)
    for h in range(H):
        t[h, C_SEL + 128 * h:C_SEL + 128 * (h + 1)] = 1
    for b in range(NB):
        t[:, C_BROW + NS * b:C_BROW + NS * (b + 1)] = np.arange(NS) // DS == b
        t[:NS, C_BCOL + b] = np.arange(NS) // DS == b
    t[:, C_IOTA:C_IOTA + SLOTS] = np.arange(SLOTS)
    t[:, C_TRI:C_TRI + 128] = s < l
    n = np.arange(T)
    t[:, C_RST:C_RST + T] = np.where(n < SEQ, n % L != 0, n % DS != 0)
    t[:, C_FIRST:C_FIRST + 3 * EG] = np.arange(3 * EG) % EG != 0
    return t


def bc(ap, *shape):
    return ap.to_broadcast(list(shape))


def build(nc, a, out):
    ctx = ExitStack()

    def sb(name, *shape):
        return ctx.enter_context(nc.sbuf_tensor(name, list(shape), F32))

    def sem(name):
        return ctx.enter_context(nc.semaphore(name))

    ring = sb("ring", 128, RING, UNIT)
    cst = sb("cst", 128, C_N)
    ones = sb("ones", 128, 128)
    hT = sb("hT", 128, KD, T)
    brT = [sb(f"brT{j}", 128, H, T) for j in range(3)]
    small = sb("small", 128, SMALL)
    arena = sb("arena", 128, ARENA)
    flag = ctx.enter_context(nc.sbuf_tensor("flag", [1, 1], I32))
    PS = ctx.enter_context(nc.psum_tensor("PS", [128, 8, 512], F32))

    ident = cst[:, C_ID:C_ID + 128]
    at = [0]

    def tiny(*shape):
        n = int(np.prod(shape[1:]))
        v = small[0:shape[0], at[0]:at[0] + n]
        at[0] += n
        assert at[0] <= SMALL
        if len(shape) == 3:
            v = v.rearrange("p (a b) -> p a b", b=shape[2])
        if len(shape) == 4:
            v = v.rearrange("p (a b c) -> p a b c", b=shape[2], c=shape[3])
        return v

    def place(start, *shape):
        n = int(np.prod(shape[1:]))
        assert start + n <= ARENA, (start, shape)
        v = arena[0:shape[0], start:start + n]
        if len(shape) == 3:
            v = v.rearrange("p (a b) -> p a b", b=shape[2])
        if len(shape) == 4:
            v = v.rearrange("p (a b c) -> p a b c", b=shape[2], c=shape[3])
        return v, start + n

    NV = 2 * KD + H + 1 + NB * H
    vecT = tiny(128, NV)
    tailT = tiny(128, NCT, HIST * (NB + 1))
    V_MIX, V_MEM, V_ML, V_GD, V_N0 = 0, KD, 2 * KD, 2 * KD + H, 2 * KD + H + 1
    cwT = tiny(128, NCT, NB * HIST + CW)
    ss = tiny(128, 5)
    rstd = tiny(128, 5)
    gffn = tiny(128, KD)
    bias4 = tiny(H, 5)
    brb = tiny(128, 20)
    m0 = tiny(H, NB)
    dec = tiny(128, H, NCH)
    gl = tiny(128, H, NCH)
    cols = tiny(128, 3, 8, H)
    hs4 = tiny(128, 12, H)
    nst = tiny(128, NB * H + H)
    rst = tiny(128, 3)
    negmax = tiny(128, H)
    psumx = tiny(128, H)
    COL_RS, COL_W, COL_IW, COL_EN, COL_G, COL_B, COL_EG, COL_KD = range(8)

    full = [sem(f"full{b}") for b in range(8)]
    free = [sem(f"free{b}") for b in range(8)]
    ring_full = [sem(f"ring_full{s}") for s in range(RING)]
    uses, count = {}, [0] * 8

    def filled(name):
        b, n = uses[name]
        return full[b], n + 1

    def bank_of(name):
        return PS[:, uses[name][0], :]

    def freed(name):
        return free[uses[name][0]]

    dve_step, act_step = sem("dve_step"), sem("act_step")
    steps = {"dve": 0, "act": 0}

    def dstep(ins):
        steps["dve"] += 1
        ins.then_inc(dve_step, 1)
        nc.vector.wait_ge(dve_step, steps["dve"])

    def astep(ins):
        steps["act"] += 1
        ins.then_inc(act_step, 1)
        nc.scalar.wait_ge(act_step, steps["act"])


    S = {}

    def sg(name):
        if name not in S:
            S[name] = sem(name)
        return S[name]

    def taken(name):
        b, n = uses[name]
        return free[b], n + 1

    def lv(t, k):
        return LEVELS * t + k

    def spare(start, *shape):
        n = int(np.prod(shape[1:]))
        assert start + n <= (RING - RING0) * UNIT
        v = ring[0:shape[0], RING0:RING, :].rearrange("p a b -> p (a b)")[:, start:start + n]
        if len(shape) == 3:
            v = v.rearrange("p (a b) -> p a b", b=shape[2])
        if len(shape) == 4:
            v = v.rearrange("p (a b c) -> p a b c", b=shape[2], c=shape[3])
        return v, start + n

    KT, p = place(0, 128, H, MEM)
    memv, p = place(p, 128, 2, W)
    A0 = p
    xin, p = place(5828, 128, 5, D)
    memT, p = place(p, 128, KD, MEM)
    junk, p = place(p, 128, D)
    wg, p = place(p, 128, KD, 16)
    vrow, p = place(p, NV, 128)
    crow, p = place(p, NB * HIST + CW, CCH)
    memk, p = place(p, 128, 2, W)
    cin, p = place(A0, 128, NCT, HIST + SEQ)
    cis, p = place(p, 128, NCT, NB * (HIST + DS))
    B0 = p
    q_t, p = place(p, 128, 3, W)
    k_t, p = place(p, 128, 3, W)
    v_a, p = place(p, 128, 3, H * DA)
    mo, p = place(p, 128, 3, W)
    gout, p = place(p, 128, 3, W)
    M0 = p
    qTt, p = place(p, 128, W)
    kTt, p = place(p, 128, W)
    qwTt, p = place(p, 128, W)
    dT, p = place(p, 128, W)
    sT, p = place(p, 128, W)
    num, p = place(p, 128, W)
    Cp, p = place(p, 128, H, DA)
    vblk1, _ = place(p, NS, NB, DA)
    vblk0, _ = place(M0, NS, NB, DA)
    vblk = [vblk0, vblk1]
    sform, p = place(p + NB * DA + NB * NS, 128, 5, H * NS)
    rowG, _ = place(M0 + 5120, H, T)
    nrow, _ = place(M0 + 5408, NB * H + H, 128)
    gtmp, _ = place(M0 + 4608, 128, W)
    rset, _ = place(p - 640, H, T)
    cvT, p = spare(0, 128, NCT, T)
    stmp, _ = spare(p, 128, 2, 4 * T)
    kT, p = spare(p, 128, W)
    qT, p = spare(p, 128, W)
    qdT, p = spare(p, 128, W)
    kbT, p = spare(p, 128, W)
    QKT, p = spare(p, 128, W)
    S0_ = p
    Cs, _ = spare((RING - RING0) * UNIT - H * NB * DA, 128, H, NB, DA)
    qwm, _ = place(M0 + NB * DA, 128, H, NB, NS)
    tails, _ = place(M0, HIST * (NB + 1), CCH)
    mixed, p = place(B0, 128, 2, D)
    mixs, p = place(p, 128, 2, 4 * NS)
    sig, p = place(p, 128, 2, W)
    B1 = p
    mixT, p = place(p, 128, KD, T)
    xq, p = place(A0, 128, 3, W)
    xqT, p = place(p, 128, H, T)
    pr, p = place(p, 128, H, MEM)
    assert p <= B0
    spT, _ = place(A0, 128, 2, NB * 4 * NS)
    hcs, _ = place(A0 + 2 * NB * 4 * NS, 128, 128)
    prT, p = place(B1, 128, 2, W)
    qm, p = place(p, 128, H, NB * NS)
    assert p <= M0 - 3 * W
    Kb, Vb, KTb = [None, None], [None] * 4, [None, None]
    Kb[0], p = place(M0 + 3 * W, 128, 2, W)
    Vb[0], p = place(p, 128, 2, W)
    Kb[1], p = place(p, 128, 2, W)
    KTb[1], p = place(B0, 128, H, MEM)
    Vb[1], p = place(p, 128, 2, W)
    KTb[0], p = place(p, 128, H, MEM)
    assert p <= B1
    Vb[2], p = spare(S0_, 128, 2, W)
    Vb[3], p = spare(p, 128, 2, W)
    raw, p = place(A0, 128, 3, W)
    kb, p = place(p, 128, W)
    kbg, p = place(p, 128, W)
    kd, p = place(p, 128, W)
    qd, p = place(p, 128, W)
    dG, p = place(M0, 128, W)
    Ak = [dG, gtmp]
    AT, p = place(p, 128, W)
    Tm, p = place(p, 128, W)
    Um, p = place(p, 128, W)
    Xm, p = place(p, 128, W)
    vn, p = place(p, 128, W)
    Sp, p = place(p, 128, W)
    nwm, p = place(p, 128, H, NB, NS)
    qdm, q = place(B1, 128, H, NB, NS)
    Ss, vnb = [None] * 4, [None] * 2
    vnb[0], _ = place(q, NS, NB, DH)
    Ss[0], q = spare(S0_, 128, NB, DH)
    Ss[1], q = spare(q, 128, NB, DH)
    Ss[2], q = spare(0, 128, NB, DH)
    Ss[3], q = spare(q, 128, NB, DH)
    vnb[1], q = spare(q, NS, NB, DH)
    x2, p = place(ARENA - 3 * D, 128, 3, D)
    h2p, p = place(0, 128, 3, D)
    h2T, p = place(p, 128, KD, T)
    Pm, p = place(p, 128, 3, E * SLOTS)
    Pw, p = place(p, 128, 3, E * SLOTS)
    PwT, p = place(p, 128, E // 2, T)
    hg, p = place(p, 128, KD, 4 * SLOTS)
    assert p <= ARENA - 3 * D
    gfin = hT[:, :, :].rearrange("p a b -> p (a b)")[:, 0:D]
    ysum = hT[:, :, :].rearrange("p a b -> p (a b)")[:, D:D + 256]
    outp, p = place(3 * D, 128, D)
    ea, p = place(p, 128, 2, 256)
    actb, p = place(p, 128, 2, 256)
    actT = [brT[0][:, :, :].rearrange("p a b -> p (a b)")[:, 256 * j:256 * j + 256] for j in range(2)]
    pws = [brT[1][:, :, :].rearrange("p a b -> p (a b)")[:, T * j:T * j + T] for j in range(2)]
    LG = tiny(128, 3, 20)
    oh = tiny(128, 3, 4)
    oh1 = tiny(128, 3, 4)
    oh2 = tiny(128, 3, 4)
    rtmp = tiny(128, 3, 4)
    rt1 = tiny(128, 12, 3)
    msk = tiny(128, 3, E)
    cmb = tiny(128, 3, E)
    rkm = tiny(128, 3, E)
    le4 = tiny(128, 3, E)
    wr = tiny(128, KD, 20)
    scrap = tiny(1, NSCRAP)
    oh3 = tiny(128, 3, 4)
    le12 = tiny(128, 12)
    R0, R1, R2 = (brT[j][0:H] for j in range(3))
    ROW_I, ROW_F, ROW_A, ROW_B = (R0[:, j, :] for j in range(4))
    ROW_Z, ROW_E = R1[:, 0:2, :], R1[:, 2:4, :]
    ROW_RS, ROW_W, ROW_IW, ROW_EN = (R1[:, j, :] for j in range(4))
    ROW_M, ROW_BC, ROW_G, ROW_KD = (R2[:, j, :] for j in range(4))
    ROW_RL, ROW_EG = ROW_BC, ROW_A

    def forms(t):
        if t < 2:
            return qTt, kTt, qwTt, dT, sT
        return [sform[:, j, :] for j in range(5)]

    w_in = a["w_in"][0]

    def cols_of(w, c):
        return w[:, c:c + 512].rearrange("(c p) n -> p c n", p=128)

    units = []
    units.append(("kvK", cols_of(a["w_mem_kv"][0], 0)))
    units.append(("kvV", cols_of(a["w_mem_kv"][0], W)))
    for name, o in (("q", O_Q), ("k", O_K), ("v", O_V), ("mo", O_MO), ("g0", O_GQKV), ("g1", O_GQKV + W),
                    ("g2", O_GQKV + 2 * W), ("xq", O_XQ), ("gout", O_GOUT)):
        units.append((name, cols_of(w_in, o)))
    for kind, j, n in (("br", 0, 0), ("gate", 0, 0), ("gate", 0, 1), ("gate", 2, 0), ("br", 2, 0), ("gate", 2, 1),
                       ("gate", 1, 0), ("gate", 1, 1), ("br", 1, 0)):
        if kind == "br":
            w = a[("w_br_mlstm", "w_br_gdn", "w_br_xattn")[j]][0]
            units.append((("br", j), w.rearrange("(c p) n -> p c n", p=128)))
        else:
            units.append((("gate", j, n), cols_of(w_in, O_GATE + j * D + n * 512)))
    for n in range(2):
        units.append((("out", n), cols_of(a["w_out"][0], n * 512)))
    NU = len(units)
    unit_no = {name: n for n, (name, _) in enumerate(units)}
    unit_last = {}

    def unit_ready(name):
        n = unit_no[name]
        return ring_full[n % RING0], 16 * (n // RING0 + 1)

    def unit(name):
        return ring[:, unit_no[name] % RING0, :]

    GROUP = [("hg", j, 4 + j) for j in range(4)]
    for pr_ in range(2):
        e0, e1 = 2 * pr_, 2 * pr_ + 1
        GROUP += [("gu", e0, 0), ("gu", e1, 1), ("aT", e0, 2), ("aT", e1, 2)]
        GROUP += [("dn", 2 * pr_, 3), ("dn", 2 * pr_ + 1, 4)]
        GROUP += [("y", 5 * pr_ + j, 5 + (5 * pr_ + j) % 3) for j in range(5)]
    g_uses, g_count = {}, [0] * 8
    for kind, j, b in GROUP:
        g_uses[(kind, j)] = (b, g_count[b])
        g_count[b] += 1
    SLOT_T = [3, 3, 2, 0, 0, 0, 0, 0]
    g_base = [0] * 8
    UPG = 12
    G_UNITS = [("g", 0), ("u", 0), ("g", 1), ("u", 1), ("d", 0), ("d", 1),
               ("g", 2), ("u", 2), ("g", 3), ("u", 3), ("d", 2), ("d", 3)]
    g_unit = {x: n for n, x in enumerate(G_UNITS)}
    G_LAST = [("gu", 0), ("gu", 0), ("gu", 1), ("gu", 1), ("dn", 1), ("dn", 1),
              ("gu", 2), ("gu", 2), ("gu", 3), ("gu", 3), ("dn", 3), ("dn", 3)]

    G_SLOTS = [4, 5, 2, 3, 0, 1]
    slot_before = [max((n for n in range(NU) if n % RING0 == s_), default=-1) if s_ < RING0 else -1
                   for s_ in range(RING)]

    def gslot(x):
        return G_SLOTS[g_unit[x] % RING]

    def gready(x, p, g):
        s_ = gslot(x)
        before = slot_before[s_] // RING0 + 1
        return ring_full[s_], (4 * p + g) * (16 * UPG // RING) + 16 * (before + g_unit[x] // RING + 1)

    def g_order(kind, j, p, g):
        b, n = g_uses[(kind, j)]
        return b, (4 * p + g) * g_count[b] + (p * SLOT_T[b]) + (g_base[b] + n)

    def gfilled(kind, j, p, g):
        b, n = g_order(kind, j, p, g)
        return full[b], n + 1

    def gtaken(kind, j, p, g):
        b, n = g_order(kind, j, p, g)
        return free[b], n

    def moved(kind, j, p, g):
        b, n = g_order(kind, j, p, g)
        return free[b], n + 1

    def t_order(e, p):
        b = e % 3
        return b, p * (4 * g_count[b] + SLOT_T[b]) + (g_base[b] - SLOT_T[b] + e // 3)

    def gbank(kind, j):
        return PS[:, g_uses[(kind, j)][0], :]

    def gfull(kind, j):
        return full[g_uses[(kind, j)][0]]

    def gfree(kind, j):
        return free[g_uses[(kind, j)][0]]

    FILL = [[[0], [1], [2], [3], [4]], [[5], [6], [7], [], [8]], [[9], [], [10], [11], [], []]]
    PARTS = [(j, nn, t, x) for j in (0, 2) for nn in range(2) for t in range(3) for x in ((0, 1, 2) if t < 2 else (3,))]
    PART_AT = [{"raw": 2, "forms": 2, "KK": 1, "level": 1, "vn": 1, "hb": 1}] * 2 + \
        [{"raw": 2, "forms": 0, "KK": 1, "level": 1, "vn": 0, "hb": 1}]
    block = ctx.enter_context(nc.Block())

    @block.tensor
    def _(pe):
        def use(name, b):
            uses[name] = (b, count[b])
            if count[b]:
                pe.wait_ge(free[b], count[b])
            count[b] += 1
            return PS[:, b, :]

        pe.wait_ge(sg("cst_in"), 16)
        pe.wait_ge(sg("vrow_in"), 16 * 5)
        o = use("vec", 6)
        pe.transpose(o[:, 0:NV], vrow, ident[0:NV, 0:NV]).then_inc(full[6], 1)
        for j in (3, 4, 0, 1, 2):
            n = NS if j == 2 else 128
            pe.wait_ge(sg("x_norm"), (3, 4, 0, 1, 2).index(j) + 1)
            for hf in range(2):
                o = use(("xT", j, hf), (2 * j + hf) % 6)
                for c in range(4):
                    ins = pe.transpose(o[:, c * n:(c + 1) * n],
                                       xin[0:n, j, 512 * hf + 128 * c:512 * hf + 128 * c + 128],
                                       ident[0:n, 0:n])
                ins.then_inc(full[(2 * j + hf) % 6], 1)

        def samples(o, src, chunks, w, done):
            for k in range(chunks):
                for c in range(4):
                    ins = pe.matmul(o[NS * c:NS * c + NS, 0:128], src[:, k, SEQ:T], w(k)[:, 128 * c:128 * c + 128],
                                    start=(k == 0), stop=(k == chunks - 1))
            ins.then_inc(done, 1)

        def project(name, src, tiles, banks):
            pe.wait_ge(*unit_ready(name))
            for t, b in zip(tiles, banks):
                t0, n = TILES[t]
                o = use((name, t), b)
                if t == 2:
                    samples(o, src, KD, lambda k: unit(name)[:, 512 * k:512 * k + 512], full[b])
                    continue
                for k in range(KD):
                    ins = pe.matmul(o[0:n, :], src[:, k, t0:t0 + n], unit(name)[:, 512 * k:512 * k + 512],
                                    start=(k == 0), stop=(k == KD - 1))
                ins.then_inc(full[b], 1)
            unit_last[name] = (name, tiles[-1])

        pe.wait_ge(*taken(("xT", 4, 1)))
        project("kvK", memT, (0, 1), (0, 1))
        project("kvV", memT, (0, 1), (2, 3))
        pe.wait_ge(*taken(("kvK", 1)))
        for hf in range(2):
            o = use(("KT", hf), 4 + hf)
            for h in range(2):
                for m in range(2):
                    ins = pe.transpose(o[:, 256 * h + 128 * m:256 * h + 128 * m + 128],
                                       memk[:, m, 128 * (2 * hf + h):128 * (2 * hf + h) + 128], ident)
            ins.then_inc(full[4 + hf], 1)

        pe.wait_ge(sg("crow_in"), 32)
        o = use("crow", 7)
        nr = NB * HIST + CW
        for c in range(NCT):
            ins = pe.transpose(o[:, c * nr:(c + 1) * nr], crow[:, 128 * c:128 * c + 128], ident[0:nr, 0:nr])
        ins.then_inc(full[7], 1)

        pe.wait_ge(*taken(("xT", 2, 1)))
        pe.wait_ge(sg("wg_in"), 32)
        o = use("gates", 6)
        for j in range(4):
            for k in range(KD):
                ins = pe.matmul(o[32 * j:32 * j + 4, 0:T], wg[:, k, 4 * j:4 * j + 4], hT[:, k, :],
                                start=(k == 0), stop=(k == KD - 1))
        ins.then_inc(full[6], 1)

        for u, name in enumerate(("q", "k", "v", "mo")):
            b0 = 3 * (u % 2)
            project(name, hT, (0, 1, 2), (b0, b0 + 1, b0 + 2))
        pe.wait_ge(sg("rows"), 1)
        o = use("cols", 7)
        rows8 = (ROW_RS, ROW_W, ROW_IW, ROW_EN, ROW_G, ROW_B, ROW_EG, ROW_KD)
        for t, (t0, n) in enumerate(TILES):
            for j, r in enumerate(rows8):
                c = (t * 8 + j) * H
                ins = pe.transpose(o[0:n, c:c + H], r[:, t0:t0 + n], ident[0:H, 0:H])
        ins.then_inc(full[7], 1)
        o = use("dec", 6)
        for j, r in enumerate((ROW_IW, ROW_EG)):
            for h in range(H):
                c = (j * H + h) * NCH
                sel = cst[0:H, C_SEL + 128 * h:C_SEL + 128 * h + 128]
                pe.matmul(o[:, c:c + 4], sel, r[:, L - 1:SEQ:L], start=(j == 0 and h == 0), stop=False,
                          skip_group_check=True)
                ins = pe.matmul(o[:, c + 4:c + NCH], sel, r[:, SEQ + DS - 1:T:DS], start=False,
                                stop=(j == 1 and h == H - 1), skip_group_check=True)
        ins.then_inc(full[6], 1)

        def masked_rows(name, b, row, t):
            t0, n = TILES[t]
            neg = cst[0:n, C_NEGS:C_NEGS + n] if t == 2 else cst[0:n, C_NEGP:C_NEGP + n]
            o = use(name, b)
            pe.matmul(o[0:n, 0:H * n].rearrange("p (h l) -> p h l", h=H), ident[0:n, 0:n],
                      bc(neg.unsqueeze(1), n, H, n), start=True, stop=False)
            for h in range(H):
                ins = pe.matmul(o[0:n, h * n:(h + 1) * n], cst[0:H, C_SEL + 128 * h:C_SEL + 128 * h + n],
                                row[:, t0:t0 + n], start=False, stop=(h == H - 1))
            ins.then_inc(full[b], 1)

        def turn(name, b, src, n):
            o = use(name, b)
            for h in range(H):
                ins = pe.transpose(o[:, h * n:(h + 1) * n], src[:, 128 * h:128 * h + 128], ident[0:n, 0:n])
            ins.then_inc(full[b], 1)

        def fill(k):
            b = 6 + k % 2
            u, c = f"g{k // 4}", k % 4
            if c == 0:
                pe.wait_ge(*unit_ready(u))
            o = use(("cv", k), b)
            for kk in range(KD):
                ins = pe.matmul(o[:, 0:T], unit(u)[:, 512 * kk + 128 * c:512 * kk + 128 * c + 128],
                                hT[:, kk, :], start=(kk == 0), stop=(kk == KD - 1))
            ins.then_inc(full[b], 1)
            unit_last[u] = ("cv", k)

        def fill_at(t, point):
            for k in FILL[t][point]:
                fill(k)

        def first_forms(t):
            n = TILES[t][1]
            pe.wait_ge(*taken(("q", t)))
            turn(("qT", t), 0, q_t[0:n, t, :], n)
            pe.wait_ge(*taken(("k", t)))
            turn(("kT", t), 1, k_t[0:n, t, :], n)
            masked_rows(("dl", t), 3, ROW_RL, t)

        first_forms(0)
        for t, (t0, n) in enumerate(TILES):
            qx, kx, qwx, dx, sx = forms(t)
            pe.wait_ge(sg("qw"), t + 1)
            turn(("qwT", t), 2, q_t[0:n, t, :], n)
            fill_at(t, 0)
            pe.wait_ge(*taken(("kT", t)))
            o = use(("sc", t), 0)
            for h in range(H):
                ins = pe.matmul(o[0:n, h * n:(h + 1) * n], kx[:, h * n:(h + 1) * n], qx[:, h * n:(h + 1) * n],
                                start=True, stop=True)
            ins.then_inc(full[0], 1)
            fill_at(t, 1)
            pe.wait_ge(sg("sT"), t + 1)
            pe.wait_ge(*taken(("v", t)))
            oo = [use(("num", t, 0), 4), use(("num", t, 1), 5)] if t < 2 else None
            for h in range(H) if t < 2 else ():
                pe.matmul(oo[h // 2][0:n, (h % 2) * DA:(h % 2 + 1) * DA], sx[0:n, h * n:(h + 1) * n],
                          v_a[0:n, t, h * DA:(h + 1) * DA], start=(h % 2 == 0), stop=False,
                          skip_group_check=True)
            pe.wait_ge(*taken(("qwT", t)))
            pe.wait_ge(sg("kw"), t + 1)
            if t < 2:
                for c in range(2):
                    r = slice(L * c, L * c + L)
                    if t or c:
                        before = (t, c - 1) if c else (t - 1, 1)
                        pe.wait_ge(*taken(("Cu", *before, 0)))
                        pe.wait_ge(*taken(("Cu", *before, 1)))
                    else:
                        pe.wait_ge(sg("C0"), 1)
                    for h in range(H):
                        ins = pe.matmul(oo[h // 2][r, (h % 2) * DA:(h % 2 + 1) * DA],
                                        qwx[:, h * n + L * c:h * n + L * c + L], Cp[:, h, :],
                                        start=False, stop=(c == 1), skip_group_check=True)
                        if c == 1 and h % 2:
                            ins.then_inc(full[4 + h // 2], 1)
                    uu = [use(("Cu", t, c, 0), 1), use(("Cu", t, c, 1), 2)]
                    for h in range(H):
                        ins = pe.matmul(uu[h // 2][:, (h % 2) * DA:(h % 2 + 1) * DA],
                                        k_t[r, t, 128 * h:128 * h + 128], v_a[r, t, h * DA:(h + 1) * DA],
                                        start=(h % 2 == 0), stop=(h % 2 == 1), skip_group_check=True)
                        if h % 2:
                            ins.then_inc(full[uses[("Cu", t, c, h // 2)][0]], 1)
                    fill_at(t, 2 + c)
            else:
                o = use(("num", t, 0), 4)
                pe.wait_ge(sg("qwm"), 1)
                for h in range(H):
                    pe.matmul(o[NS * h:NS * h + NS, 0:DA], sx[0:n, h * n:(h + 1) * n],
                              v_a[0:n, t, h * DA:(h + 1) * DA], start=True, stop=False, skip_group_check=True)
                for b in range(NB):
                    for h in range(H):
                        ins = pe.matmul(o[NS * h:NS * h + NS, 0:DA], qwm[:, h, b, :], Cs[:, h, b, :], start=False,
                                        stop=(b == NB - 1), skip_group_check=True)
                ins.then_inc(full[4], 1)
                for h in range(H):
                    pe.wait_ge(sg("vblk"), h + 1)
                    for g, (b0, b1) in enumerate(((0, 3), (3, 6), (6, 8))):
                        bk = (1, 2, 3)[g]
                        o = use(("Cs", h, g), bk)
                        pe.matmul(o[:, 0:(b1 - b0) * DA], k_t[0:n, t, 128 * h:128 * h + 128],
                                  vblk[h % 2][:, b0:b1, :].rearrange("p b v -> p (b v)"),
                                  start=True, stop=True).then_inc(full[bk], 1)
                    fill_at(t, 2 + h)
            if t < 2:
                fill_at(t, 4)
                first_forms(t + 1)
            else:
                project("xq", hT, (0,), (6,))
            pe.wait_ge(sg("ha"), t + 1)
            turn(("haT", t), 5, num[0:n, :], n)
        pe.wait_ge(sg("nst"), 1)
        o = use("nT", 3)
        pe.transpose(o[0:NB * H + H, 0:128], nst, ident).then_inc(full[3], 1)

        def scores(so, b):
            pe.wait_ge(*taken(("KbT", b, 0)))
            pe.wait_ge(*taken(("KbT", b, 1)))
            for h in range(H):
                ins = pe.matmul(so[NS * h:NS * h + NS, 0:MEM], qm[:, h, NS * b:NS * b + NS], KTb[b % 2][:, h, :],
                                start=(b == 0), stop=(b == NB - 1))
            if b == NB - 1:
                ins.then_inc(full[6], 1)
            else:
                ins.then_inc(sg("K_read"), 1)

        def turn_keys(b):
            pe.wait_ge(sg(f"Kb{b % 2}"), 16 * (b // 2 + 1))
            for g in range(2):
                bk = 2 + g + 2 * (b % 2)
                o = use(("KbT", b, g), bk)
                for h in (2 * g, 2 * g + 1):
                    for m in range(2):
                        ins = pe.transpose(o[:, MEM * (h % 2) + 128 * m:MEM * (h % 2) + 128 * m + 128],
                                           Kb[b % 2][:, m, 128 * h:128 * h + 128], ident)
                ins.then_inc(full[bk], 1)

        pe.wait_ge(sg("tailT"), 1)
        for g in range(3):
            o = use(("tail", g), g)
            for c in range(4):
                ins = pe.transpose(o[0:HIST * (NB + 1), 128 * c:128 * c + 128], tailT[:, 4 * g + c, :], ident)
            ins.then_inc(full[g], 1)
        project("xq", hT, (1, 2), (3, 4))
        for t, (t0, n) in enumerate(TILES):
            pe.wait_ge(*taken(("xq", t)))
            turn(("xqT", t), t % 2, xq[0:n, t, :], n)
        turn_keys(0)
        turn_keys(1)
        for t in range(2):
            t0 = 128 * t
            pe.wait_ge(*taken(("xqT", t)))
            if t == 0:
                pe.wait_ge(*taken(("KT", 1)))
            for g in range(2):
                bk = 2 + g - 2 * t
                o = use(("xs", t, g), bk)
                for h in (2 * g, 2 * g + 1):
                    ins = pe.matmul(o[:, MEM * (h % 2):MEM * (h % 2) + MEM], xqT[:, h, t0:t0 + 128], KT[:, h, :],
                                    start=True, stop=True)
                ins.then_inc(full[bk], 1)
        pe.wait_ge(sg("qm"), 1)
        so = use("ss", 6)
        scores(so, 0)
        scores(so, 1)
        for t in range(2):
            project("gout", hT, (t,), (7,))
            if t:
                scores(so, 2)
            pe.wait_ge(sg("pr"), t + 1)
            for m in range(2):
                o = use(("prT", t, m), 4 + m)
                for h in range(H):
                    ins = pe.transpose(o[:, 128 * h:128 * h + 128], pr[:, h, 128 * m:128 * m + 128], ident)
                ins.then_inc(full[4 + m], 1)
            pe.wait_ge(*taken(("prT", t, 0)))
            pe.wait_ge(*taken(("prT", t, 1)))
            o = use(("hcT", t), 7)
            for h in range(H):
                for m in range(2):
                    ins = pe.matmul(o[:, 128 * h:128 * h + 128], memv[:, m, 128 * h:128 * h + 128],
                                    prT[:, m, 128 * h:128 * h + 128], start=(m == 0), stop=(m == 1))
            ins.then_inc(full[7], 1)
            turn_keys(2 + t)
        project("gout", hT, (2,), (7,))
        for b in range(4, NB):
            turn_keys(b)
            scores(so, b - 1)
        scores(so, NB - 1)
        pe.wait_ge(sg("pr"), 3)
        o = use("spT", 1)
        for m in range(2):
            ins = pe.transpose(o[:, 128 * m:128 * m + 128], pr[:, 0, 128 * m:128 * m + 128], ident)
        ins.then_inc(full[1], 1)
        pe.wait_ge(*taken("spT"))
        o = use("hcs", 6)
        for b in range(NB):
            pe.wait_ge(sg(f"Vb{b % 4}"), 16 * (b // 4 + 1))
            for m in range(2):
                for h in range(H):
                    ins = pe.matmul(o[NS * h:NS * h + NS, 0:128],
                                    spT[:, m, 128 * b + NS * h:128 * b + NS * h + NS],
                                    Vb[b % 4][:, m, 128 * h:128 * h + 128],
                                    start=(b == 0 and m == 0), stop=(b == NB - 1 and m == 1))
            if b < NB - 1:
                ins.then_inc(sg("V_read"), 1)
        ins.then_inc(full[6], 1)
        pe.wait_ge(*taken("hcs"))
        o = use("hcsT", 7)
        pe.transpose(o[:, 0:128], hcs, ident).then_inc(full[7], 1)

        def merge_part(j, nn, t, x):
            t0, n = TILES[t]
            if x in (0, 3):
                merges[0] += 1
                use(("mg", j, nn, t), 5 + merges[0] % 2)
            bg = 5 + merges[0] % 2
            wg_ = lambda k: unit(("gate", j, nn))[:, 512 * k:512 * k + 512]
            wb_ = lambda k: unit(("br", j))[:, D * k + 512 * nn:D * k + 512 * nn + 512]
            if t == 0 and x == 0:
                pe.wait_ge(*unit_ready(("gate", j, nn)))
            if x < 2:
                for k in range(4 * x, 4 * x + 4):
                    ins = pe.matmul(PS[:, bg, :], hT[:, k, t0:t0 + n], wg_(k), start=(k == 0), stop=(k == KD - 1))
                if x == 1:
                    ins.then_inc(full[bg], 1)
            if x == 2:
                if t == 0 and nn == 0:
                    pe.wait_ge(*unit_ready(("br", j)))
                o = use(("mb", j, nn, t), 7)
                for k in range(H):
                    ins = pe.matmul(o, brT[j][:, k, t0:t0 + n], wb_(k), start=(k == 0), stop=(k == H - 1))
                ins.then_inc(full[7], 1)
            if x == 3:
                samples(PS[:, bg, :], hT, KD, wg_, full[bg])
                samples(use(("mb", j, nn, t), 7), brT[j], H, wb_, full[7])
                unit_last[("gate", j, nn)] = ("mb", j, nn, 2)
                unit_last[("br", j)] = ("mb", j, nn, 2)

        def part_at(t, point):
            for _ in range(PART_AT[t][point]):
                if parts_done[0] < len(PARTS):
                    merge_part(*PARTS[parts_done[0]])
                    parts_done[0] += 1

        parts_done, merges = [0], [0]
        pe.wait_ge(*taken("hcsT"))
        pe.wait_ge(sg("rowG"), 1)
        pe.wait_ge(sg("cvT"), 3)

        def turn_raw(t):
            t0, n = TILES[t]
            for g in range(3):
                o = use(("raw", t, g), g)
                for c in range(4):
                    ins = pe.transpose(o[0:n, 128 * c:128 * c + 128], cvT[:, 4 * g + c, t0:t0 + n], ident)
                ins.then_inc(full[g], 1)
            masked_rows(("dG", t), 3, rowG, t)

        turn_raw(0)
        for t, (t0, n) in enumerate(TILES):
            part_at(t, "raw")
            pe.wait_ge(sg("gq"), 4 * t + 1)
            turn(("kT2", t), 4, raw[0:n, 1, :], n)
            pe.wait_ge(sg("gq"), 4 * t + 2)
            turn(("kbT", t), 0, kb[0:n, :], n)
            pe.wait_ge(sg("gq"), 4 * t + 3)
            turn(("qT2", t), 1, raw[0:n, 0, :], n)
            pe.wait_ge(sg("gq"), 4 * t + 4)
            turn(("qdT", t), 2, qd[0:n, :], n)
            part_at(t, "forms")
            pe.wait_ge(*taken(("qT2", t)))
            pe.wait_ge(*taken(("qdT", t)))
            for name, b, x in ((("KK", t), 3, kbT), (("QK", t), 4, qT)):
                o = use(name, b)
                for h in range(H):
                    ins = pe.matmul(o[0:n, h * n:(h + 1) * n], kT[:, h * n:(h + 1) * n], x[:, h * n:(h + 1) * n],
                                    start=True, stop=True)
                ins.then_inc(full[b], 1)
            part_at(t, "KK")
            if t == 2:
                merge_part(1, 0, 0, 0)
            nl = 2 if t == 2 else LEVELS
            for k in range(nl):
                pe.wait_ge(sg("ATk"), lv(t, k) + 1)
                if k:
                    pe.wait_ge(*taken(("X", t, 0) if k == 1 else ("Y", t, k - 1)))
                o = use(("X", t, k), 0)
                for h in range(H):
                    ins = pe.matmul(o[0:n, h * n:(h + 1) * n], Ak[k % 2][0:n, h * n:(h + 1) * n],
                                    ident[0:n, 0:n] if k == 0 else Tm[0:n, h * n:(h + 1) * n],
                                    start=True, stop=True)
                ins.then_inc(full[0], 1)
                if k == 0:
                    continue
                pe.wait_ge(*taken(("X", t, k)))
                if k > 1:
                    pe.wait_ge(*taken(("YT", t, k - 1)))
                if k < nl - 1:
                    o = use(("Y", t, k), 2)
                    for h in range(H):
                        ins = pe.matmul(o[0:n, h * n:(h + 1) * n], Um[0:n, h * n:(h + 1) * n],
                                        Xm[0:n, h * n:(h + 1) * n], start=True, stop=True)
                    ins.then_inc(full[2], 1)
                o = use(("YT", t, k), 1)
                for h in range(H):
                    ins = pe.matmul(o[0:n, h * n:(h + 1) * n], Xm[0:n, h * n:(h + 1) * n],
                                    Um[0:n, h * n:(h + 1) * n], start=True, stop=True)
                ins.then_inc(full[1], 1)
                part_at(t, "level")
            pe.wait_ge(*taken(("YT", t, nl - 1)))
            pe.wait_ge(sg("gv"), t + 1)
            o = use(("wT", t), 3)
            for h in range(H):
                ins = pe.matmul(o[:, h * n:(h + 1) * n], kbg[0:n, 128 * h:128 * h + 128],
                                Um[0:n, h * n:(h + 1) * n], start=True, stop=True)
            ins.then_inc(full[3], 1)
            pe.wait_ge(*taken(("wT", t)))
            pe.wait_ge(*taken(("QK", t)))
            if t < 2:
                for c in range(2):
                    r = slice(L * c, L * c + L)
                    if t or c:
                        pe.wait_ge(*taken(("So", t, c - 1) if c else ("So", t - 1, 1)))
                    else:
                        pe.wait_ge(sg("S0"), 1)
                    o = use(("vn", t, c), 4)
                    for h in range(H):
                        hc = slice(h * n + L * c, h * n + L * c + L)
                        hv = slice(128 * h, 128 * h + 128)
                        pe.matmul(o[r, hv], Um[0:n, hc], raw[0:n, 2, hv], start=(h == 0), stop=False,
                                  skip_group_check=True)
                        ins = pe.matmul(o[r, hv], kbT[:, hc], Sp[:, hv], start=False, stop=(h == H - 1),
                                        skip_group_check=True)
                    ins.then_inc(full[4], 1)
                    part_at(t, "vn")
                    pe.wait_ge(*taken(("vn", t, c)))
                    o = use(("So", t, c), 0)
                    for h in range(H):
                        hv = slice(128 * h, 128 * h + 128)
                        ins = pe.matmul(o[:, hv], kd[r, hv], vn[r, hv], start=True, stop=True)
                    ins.then_inc(full[0], 1)
                    o = use(("go", t, c), 1)
                    for h in range(H):
                        hc = slice(h * n + L * c, h * n + L * c + L)
                        hv = slice(128 * h, 128 * h + 128)
                        pe.matmul(o[r, hv], qdT[:, hc], Sp[:, hv], start=(h == 0), stop=False,
                                  skip_group_check=True)
                        ins = pe.matmul(o[r, hv], QKT[r, hc], vn[r, hv], start=False, stop=(h == H - 1),
                                        skip_group_check=True)
                    ins.then_inc(full[1], 1)
            else:
                hc = [slice(h * n, (h + 1) * n) for h in range(H)]
                hv = [slice(128 * h, 128 * h + 128) for h in range(H)]
                hp = [slice(NS * h, NS * h + NS) for h in range(H)]
                merge_part(1, 0, 0, 1)
                pe.wait_ge(sg("nwm"), 1)
                for h in range(H):
                    pe.wait_ge(sg(f"Ss_in{h}"), 16)
                o = use("vn2", 4)
                for h in range(H):
                    pe.matmul(o[hp[h], 0:DH], Um[0:n, hc[h]], raw[0:n, 2, hv[h]], start=True, stop=False,
                              skip_group_check=True)
                for b in range(NB):
                    for h in range(H):
                        ins = pe.matmul(o[hp[h], 0:DH], nwm[:, h, b, :], Ss[h][:, b, :], start=False,
                                        stop=(b == NB - 1), skip_group_check=True)
                ins.then_inc(full[4], 1)
                o = use("go2", 1)
                for b in range(NB):
                    for h in range(H):
                        pe.matmul(o[hp[h], 0:DH], qdm[:, h, b, :], Ss[h][:, b, :], start=(b == 0), stop=False,
                                  skip_group_check=True)
                pe.wait_ge(*taken("vn2"))
                for h in range(H):
                    ins = pe.matmul(o[hp[h], 0:DH], QKT[0:n, hc[h]], vn[0:n, hv[h]], start=False, stop=True,
                                    skip_group_check=True)
                ins.then_inc(full[1], 1)
                for h in range(H):
                    pe.wait_ge(sg("vnb"), h + 1)
                    for g in range(2):
                        bk = (0, 3)[g]
                        o = use(("So2", h, g), bk)
                        pe.matmul(o, kd[0:n, hv[h]], vnb[h % 2][:, 4 * g:4 * g + 4, :].rearrange("p b v -> p (b v)"),
                                  start=True, stop=True).then_inc(full[bk], 1)
                    part_at(t, "vn")
            part_at(t, "hb")
            if t < 2:
                turn_raw(t + 1)
            else:
                merge_part(1, 0, 1, 0)
                merge_part(1, 0, 1, 1)
            pe.wait_ge(sg("hb"), t + 1)
            turn(("hbT", t), 4, kb[0:n, :], n)

        while parts_done[0] < len(PARTS):
            merge_part(*PARTS[parts_done[0]])
            parts_done[0] += 1
        pe.wait_ge(*taken(("hbT", 2)))

        def turn_mixed(t, hf):
            pe.wait_ge(sg("mixed"), 3 * hf + t + 1)
            t0, n = TILES[t]
            o = use(("mixT", t, hf), hf)
            if t == 2:
                pe.transpose(o[:, 0:128], mixs[:, hf, :], ident).then_inc(full[hf], 1)
                return
            for c in range(4):
                ins = pe.transpose(o[:, c * n:(c + 1) * n],
                                   mixed[0:n, t, 512 * hf + 128 * c:512 * hf + 128 * c + 128],
                                   ident[0:n, 0:n])
            ins.then_inc(full[hf], 1)

        for nn in range(2):
            for t in range(3):
                for x in ((0, 1, 2) if nn else (2,)) if t < 2 else (3,):
                    merge_part(1, nn, t, x)
                if nn == 1:
                    turn_mixed(t, 0)
        for t in range(3):
            turn_mixed(t, 1)
        for t in range(3):
            pe.wait_ge(*taken(("mixT", t, 0)))
            pe.wait_ge(*taken(("mixT", t, 1)))
            for nn in range(2):
                project(("out", nn), mixT, (t,), (2 + (2 * t + nn) % 4,))

        def turn_h2(t):
            t0, n = TILES[t]
            pe.wait_ge(sg("h2p"), t + 1)
            for hf in range(2):
                o = use(("h2T", t, hf), 6 + hf)
                for c in range(4):
                    ins = pe.transpose(o[:, c * n:(c + 1) * n],
                                       h2p[0:n, t, 512 * hf + 128 * c:512 * hf + 128 * c + 128],
                                       ident[0:n, 0:n])
                ins.then_inc(full[6 + hf], 1)

        pe.wait_ge(sg("wr_in"), 32)
        lg = use("lg", 1)
        turn_h2(0)
        for t, (t0, n) in enumerate(TILES):
            if t < 2:
                turn_h2(t + 1)
            pe.wait_ge(*taken(("h2T", t, 0)))
            pe.wait_ge(*taken(("h2T", t, 1)))
            for k in range(KD):
                ins = pe.matmul(lg[0:n, 20 * t:20 * t + 20], h2T[:, k, t0:t0 + n], wr[:, k, :],
                                start=(k == 0), stop=(k == KD - 1))
        ins.then_inc(full[1], 1)
        pe.wait_ge(sg("msk"), 1)
        pe.wait_ge(sg("ones"), 1)
        o = use("rank", 2)
        for t, (t0, n) in enumerate(TILES):
            for u in range(t + 1):
                ins = pe.matmul(o[0:n, E * t:E * t + E],
                                cst[0:n, C_TRI:C_TRI + n] if u == t else ones[:, 0:n],
                                msk[0:TILES[u][1], u, :], start=(u == 0), stop=(u == t))
        for u, (t0, n) in enumerate(TILES):
            ins = pe.matmul(o[0:1, 3 * E:4 * E], ones[0:n, 0:1], msk[0:n, u, :], start=(u == 0), stop=(u == 2))
        ins.then_inc(full[2], 1)

        def slots_T(p=None):
            for e in range(E // 2):
                if e % (EG // 2) == 0:
                    pe.wait_ge(sg("Pm"), (0 if p is None else p * G) + (2 * e // EG + 1))
                if p is None:
                    o = use(("PwT", e), e % 3)
                else:
                    b, n = t_order(e, p)
                    pe.wait_ge(free[b], n)
                    o = PS[:, b, :]
                for t, (t0, n) in enumerate(TILES):
                    ins = pe.transpose(o[:, t0:t0 + n], Pw[0:n, t, 128 * e:128 * e + 128], ident[0:n, 0:n])
                ins.then_inc(full[e % 3], 1)

        slots_T()
        for b in range(8):
            g_base[b] = count[b]

        def group(p, g):
            for j in range(4):
                pe.wait_ge(*gtaken("hg", j, p, g))
                o = gbank("hg", j)
                for c in (2 * j, 2 * j + 1):
                    for t, (t0, n) in enumerate(TILES):
                        ins = pe.matmul(o[:, 256 * (c % 2):256 * (c % 2) + 256], h2p[0:n, t, 128 * c:128 * c + 128],
                                        Pm[0:n, t, bass.ds(g * 256, 256)], start=(t == 0), stop=(t == 2))
                ins.then_inc(gfull("hg", j), 1)
            for pr_ in range(2):
                for e in (2 * pr_, 2 * pr_ + 1):
                    pe.wait_ge(*gready(("g", e), p, g))
                    pe.wait_ge(*gready(("u", e), p, g))
                    pe.wait_ge(*gtaken("gu", e, p, g))
                    o = gbank("gu", e)
                    s0 = gslot(("g", e))
                    for k in range(KD):
                        if e == 0 and k % 2 == 0:
                            pe.wait_ge(*moved("hg", k // 2, p, g))
                        for hf in range(2):
                            ins = pe.matmul(o[64 * hf:64 * hf + 64, :], hg[:, k, 64 * e:64 * e + 64],
                                            ring[:, s0:s0 + 2, 512 * k + 256 * hf:512 * k + 256 * hf + 256],
                                            start=(k == 0), stop=(k == KD - 1))
                    ins.then_inc(gfull("gu", e), 1)
                if pr_ == 1:
                    scatter(0, p, g)
                for e in (2 * pr_, 2 * pr_ + 1):
                    pe.wait_ge(sg("act"), (4 * p + g) * 4 + (e + 1))
                    pe.wait_ge(*gtaken("aT", e, p, g))
                    o = gbank("aT", e)
                    for c in range(2):
                        ins = pe.transpose(o[:, 128 * c:128 * c + 128], actb[:, e % 2, 128 * c:128 * c + 128], ident)
                    ins.then_inc(gfull("aT", e), 1)
                for e in (2 * pr_, 2 * pr_ + 1):
                    pe.wait_ge(*moved("aT", e, p, g))
                for x in range(2):
                    pe.wait_ge(*gready(("d", 2 * pr_ + x), p, g))
                for nn in range(2):
                    pe.wait_ge(*gtaken("dn", 2 * pr_ + nn, p, g))
                for nn in range(2):
                    o = gbank("dn", 2 * pr_ + nn)
                    for c in range(4):
                        hf, cc = c // 2, c % 2
                        for x in range(2):
                            w = ring[:, gslot(("d", 2 * pr_ + x)), D * c + 512 * nn:D * c + 512 * nn + 512]
                            ins = pe.matmul(o[64 * x:64 * x + 64, :],
                                            actT[x][:, 128 * cc + 64 * hf:128 * cc + 64 * hf + 64], w,
                                            start=(c == 0), stop=(c == 3))
                    ins.then_inc(gfull("dn", 2 * pr_ + nn), 1)
            scatter(1, p, g)

        def scatter(pr_, p, g):
            pe.wait_ge(sg("pws"), (4 * p + g) * 2 + (pr_ + 1))
            for nn in range(2):
                pe.wait_ge(*moved("dn", 2 * pr_ + nn, p, g))
                for t, (t0, n) in enumerate(TILES[0:2]):
                    j = 5 * pr_ + 2 * nn + t
                    pe.wait_ge(*gtaken("y", j, p, g))
                    pe.matmul(gbank("y", j), pws[pr_][:, t0:t0 + n], outp[:, 512 * nn:512 * nn + 512],
                              start=True, stop=True).then_inc(gfull("y", j), 1)
            j = 5 * pr_ + 4
            pe.wait_ge(*gtaken("y", j, p, g))
            for nn in range(2):
                for c in range(4):
                    ins = pe.matmul(gbank("y", j)[NS * c:NS * c + NS, 128 * nn:128 * nn + 128], pws[pr_][:, SEQ:T],
                                    outp[:, 512 * nn + 128 * c:512 * nn + 128 * c + 128], start=True, stop=True,
                                    skip_group_check=True)
            ins.then_inc(gfull("y", j), 1)

        with pe.Fori(0, G) as g:
            group(0, g)
        pe.wait_ge(sg("flag"), 1)
        most = pe.value_load(flag[0:1, 0:1], min_val=0, max_val=T)
        with pe.If(most > SLOTS):
            with pe.Fori(1, PASSES) as p:
                slots_T(p)
                with pe.Fori(0, G) as g:
                    group(p, g)

    @block.sync
    def _(sp):
        for j in (3, 4):
            sp.dma_start(xin[:, j, :], a["mem_prompt"][0, 128 * (j - 3):128 * (j - 2), :]).then_inc(sg(f"xin{j}"), 16)
        r = 0
        for x, n in ((a["norm_mix"][0], KD), (a["mem_norm"][0], KD), (a["mlstm_norm"][0], H),
                     (a["gdn_norm"][0], 1)):
            sp.dma_start(vrow[r:r + n, :], x.rearrange("(r c) -> r c", c=128)).then_inc(sg("vrow_in"), 16)
            r += n
        sp.dma_start(vrow[r:r + NB * H, :],
                     a["state_mlstm_n"][0].rearrange("b h k -> (b h) k")).then_inc(sg("vrow_in"), 16)
        sp.dma_start(cst[:, :], a["table"][:, 0:C_N]).then_inc(sg("cst_in"), 16)
        for j, (t0, n) in enumerate(TILES):
            x = a["x_prompt"][0, t0:t0 + n, :] if j < 2 else a["x_sample"].rearrange("b s d -> (b s) d")
            sp.dma_start(xin[0:n, j, :], x).then_inc(sg(f"xin{j}"), 16)
        sp.dma_start(wg[:, :, 0:8], w_in[:, O_IF:O_IF + 8].rearrange("(c p) n -> p c n", p=128)) \
            .then_inc(sg("wg_in"), 16)
        sp.dma_start(wg[:, :, 8:16], w_in[:, O_GAB:O_GAB + 8].rearrange("(c p) n -> p c n", p=128)) \
            .then_inc(sg("wg_in"), 16)
        for n, (name, src) in enumerate(units):
            if n >= RING0:
                sp.wait_ge(*filled(unit_last[units[n - RING0][0]]))
            sp.dma_start(unit(name).rearrange("p (c n) -> p c n", c=src.shape[1]), src) \
                .then_inc(ring_full[n % RING0], 16)

        def load_group(p, g, first):
            for u, (kind, e) in enumerate(G_UNITS):
                if first and G_SLOTS[u % RING] >= RING0 and u < RING:
                    if u == 0:
                        sp.wait_ge(*filled(("hbT", 2)))
                        sp.wait_ge(sg("Ss_out"), 16 * H)
                elif first and u < RING:
                    sp.wait_ge(*filled(unit_last[units[slot_before[G_SLOTS[u]]][0]]))
                elif u < RING:
                    kd_, j = G_LAST[u + UPG - RING]
                    b, n = g_uses[(kd_, j)]
                    sp.wait_ge(full[b], prev_order(kd_, j, p, g))
                else:
                    sp.wait_ge(*gfilled(*G_LAST[u - RING], p, g))
                w = {"g": "w_exp_gate", "u": "w_exp_up", "d": "w_exp_down"}[kind]
                if kind == "d":
                    src = a[w][0, bass.ds(g * EG + e, 1)].rearrange("e (c p) n -> p (e c) n", p=128)
                else:
                    src = a[w][0, bass.ds(g * EG + e, 1)].rearrange("e (p c) n -> p (e c) n", p=128)
                sp.dma_start(ring[:, gslot((kind, e)), :].rearrange("p (c n) -> p c n", c=4 if kind == "d" else 8),
                             src).then_inc(ring_full[gslot((kind, e))], 16)

        def prev_order(kind, j, p, g):
            b, n = g_uses[(kind, j)]
            if isinstance(g, int):
                if g:
                    return (4 * p + (g - 1)) * g_count[b] + p * SLOT_T[b] + (g_base[b] + n + 1)
                return (4 * p - 1) * g_count[b] + (p - 1) * SLOT_T[b] + (g_base[b] + n + 1)
            return (4 * p + g) * g_count[b] + p * SLOT_T[b] + (g_base[b] + n + 1 - g_count[b])

        load_group(0, 0, True)
        with sp.Fori(1, G) as g:
            load_group(0, g, False)
        sp.wait_ge(sg("flag"), 1)
        most = sp.value_load(flag[0:1, 0:1], min_val=0, max_val=T)
        with sp.If(most > SLOTS):
            with sp.Fori(1, PASSES) as p:
                load_group(p, 0, False)
                with sp.Fori(1, G) as g:
                    load_group(p, g, False)
        for t, (t0, n) in enumerate(TILES):
            y = out["y_prompt"][0, t0:t0 + n, :] if t < 2 else out["y_sample"].rearrange("b s d -> (b s) d")
            sp.wait_ge(sg("y"), t + 1)
            sp.dma_start(y, x2[0:n, t, :]).then_inc(sg("y_out"), 16)
        sp.wait_ge(sg("y_out"), 48)

    @block.gpsimd
    def _(pool):
        small_in = sg("small_in")
        for dst, src in ((bias4[:, 0:1], a["b_igate"][0]), (bias4[:, 1:2], a["b_fgate"][0]),
                         (bias4[:, 2:3], a["dt_bias"][0]), (bias4[:, 3:4], a["a_log"][0])):
            pool.dma_start(dst, src.rearrange("(n a) -> n a", a=1)).then_inc(small_in, 16)
        pool.dma_start(brb[:, 0:G], a["b_router_group"][0].partition_broadcast(128)).then_inc(small_in, 16)
        pool.dma_start(brb[:, G:20], a["b_router_expert"][0].partition_broadcast(128)).then_inc(small_in, 16)
        pool.dma_start(rset, a["table"][0:H, C_RST:C_ALL]).then_inc(small_in, 16)
        pool.dma_start(m0, a["state_mlstm_m"][0].rearrange("b h -> h b"), allow_slow_non_contiguous=True) \
            .then_inc(small_in, 16)
        pool.dma_start(gffn, a["norm_ffn"][0].rearrange("(p c) -> p c", c=KD)).then_inc(small_in, 16)
        pool.dma_start(crow[0:NB * HIST, :], a["state_gdn_conv"][0].rearrange("b s c -> (b s) c")) \
            .then_inc(sg("crow_in"), 16)
        pool.dma_start(crow[NB * HIST:, :], a["conv_w"][0]).then_inc(sg("crow_in"), 16)
        pool.dma_start(wr[:, :, 0:G], a["w_router_group"][0].rearrange("(p c) n -> p c n", c=KD)) \
            .then_inc(sg("wr_in"), 16)
        pool.dma_start(wr[:, :, G:20], a["w_router_expert"][0].rearrange("(p c) n -> p c n", c=KD)) \
            .then_inc(sg("wr_in"), 16)
        pool.memset(ones[:, :], 1.0).then_inc(sg("ones"), 1)
        for m in range(2):
            pool.wait_ge(*taken(("kvK", m)))
            pool.dma_start(out["mem_k"][0, 0, 128 * m:128 * m + 128].rearrange("m h d -> m (h d)"),
                           memk[:, m, :]).then_inc(sg("memk_out"), 16)
            pool.wait_ge(*taken(("kvV", m)))
            pool.dma_start(out["mem_v"][0, 0, 128 * m:128 * m + 128].rearrange("m h d -> m (h d)"),
                           memv[:, m, :]).then_inc(sg("kv_out"), 16)
        pool.wait_ge(sg("rows"), 1)
        pool.dma_start(out["m_p"][0].rearrange("b h -> h b"), ROW_M[:, SEQ - 1:SEQ],
                        allow_slow_non_contiguous=True) \
            .then_inc(sg("m_out"), 16)
        pool.dma_start(out["m_s"][0].rearrange("b h -> h b"), ROW_M[:, SEQ + DS - 1:T:DS],
                        allow_slow_non_contiguous=True) \
            .then_inc(sg("m_out"), 16)
        for h in range(H):
            pool.dma_start(Cs[:, h, :, 0:DH], a["state_mlstm_C"][0, :, h].rearrange("b k v -> k b v")) \
                .then_inc(sg("Cs_in"), 16)
        pool.wait_ge(sg("Cp"), 1)
        pool.dma_start(out["C_p"][0, 0].rearrange("h k v -> k h v"), Cp[:, :, 0:DH]).then_inc(sg("Cp_out"), 16)
        for h in range(H):
            pool.wait_ge(sg("Cs"), h + 1)
            pool.dma_start(out["C_s"][0, :, h].rearrange("b k v -> k b v"), Cs[:, h, :, 0:DH]) \
                .then_inc(sg("Cs_out"), 16)
        pool.wait_ge(*taken("nT"))
        pool.dma_start(out["n_s"][0].rearrange("b h k -> (b h) k"), nrow[0:NB * H, :]).then_inc(sg("n_out"), 16)
        pool.dma_start(out["n_p"][0, 0], nrow[NB * H:NB * H + H, :]).then_inc(sg("n_out"), 16)
        pool.wait_ge(*taken(("tail", 2)))
        pool.dma_start(out["conv_p"][0, 0], tails[0:HIST, :]).then_inc(sg("tail_out"), 16)
        pool.dma_start(out["conv_s"][0].rearrange("b s c -> (b s) c"), tails[HIST:, :]).then_inc(sg("tail_out"), 16)
        pool.wait_ge(sg("Cs_out"), 16 * H)
        pool.wait_ge(sg("Cp_out"), 16)
        pool.wait_ge(*filled(("haT", 2)))
        for b in range(NB):
            if b >= 2:
                pool.wait_ge(*filled(("KbT", b - 2, 1)))
            pool.dma_start(Kb[b % 2], a["cache_mem_k"][0, b].rearrange("(c p) h d -> p c (h d)", p=128)) \
                .then_inc(sg(f"Kb{b % 2}"), 16)
            for v in range(4) if b == 1 else ():
                pool.dma_start(Vb[v], a["cache_mem_v"][0, v].rearrange("(c p) h d -> p c (h d)", p=128)) \
                    .then_inc(sg(f"Vb{v}"), 16)
        for b in range(4, NB):
            pool.wait_ge(sg("V_read"), b - 3)
            pool.dma_start(Vb[b % 4], a["cache_mem_v"][0, b].rearrange("(c p) h d -> p c (h d)", p=128)) \
                .then_inc(sg(f"Vb{b % 4}"), 16)
        pool.wait_ge(*filled("hcs"))
        for h in range(H):
            if h == 2:
                pool.wait_ge(*filled(("raw", 2, 2)))
            pool.dma_start(Ss[h], a["state_gdn_S"][0, :, h].rearrange("b k v -> k b v")) \
                .then_inc(sg(f"Ss_in{h}"), 16)
        pool.wait_ge(sg("Spout"), 1)
        pool.dma_start(out["S_p"][0, 0].rearrange("h k v -> k h v"),
                       Sp.rearrange("p (h v) -> p h v", h=H)).then_inc(sg("Sp_out"), 16)
        for h in range(H):
            pool.wait_ge(sg("Ssd"), h + 1)
            pool.dma_start(out["S_s"][0, :, h].rearrange("b k v -> k b v"), Ss[h]).then_inc(sg("Ss_out"), 16)
        pool.wait_ge(sg("Ss_out"), 16 * H)
        pool.wait_ge(sg("Sp_out"), 16)
        pool.wait_ge(*filled(("hbT", 2)))
        for t, (t0, n) in enumerate(TILES):
            x = a["x_prompt"][0, t0:t0 + n, :] if t < 2 else a["x_sample"].rearrange("b s d -> (b s) d")
            pool.dma_start(x2[0:n, t, :], x).then_inc(sg("x2_in"), 16)
        pool.wait_ge(*filled((("out", 1), 2)))
        pool.dma_start(gfin, a["final_norm"].partition_broadcast(128)).then_inc(sg("gfin_in"), 16)
        for s, n in (("kv_out", 32), ("memk_out", 32), ("m_out", 32), ("n_out", 32), ("tail_out", 32),
                     ("gfin_in", 16), ("wr_in", 32)):
            pool.wait_ge(sg(s), n)

    @block.scalar
    def _(act):
        def run(o, i, f, **kw):
            return act.activation(o, i, f, **kw)

        act.preload_act_table_set("natural_log_exp_and_others")
        for i, j in enumerate((3, 4, 0, 1, 2)):
            n = NS if j == 2 else 128
            act.wait_ge(sg(f"xin{j}"), 16)
            astep(run(junk[0:n, :], xin[0:n, j, :], ACT.Square, accum_out=ss[0:n, j:j + 1]))
            astep(run(rstd[0:n, j:j + 1], ss[0:n, j:j + 1], ACT.Ln, scale=1.0 / D, bias=EPS))
            run(rstd[0:n, j:j + 1], rstd[0:n, j:j + 1], ACT.Exp, scale=-0.5).then_inc(sg("rstd"), 1)

        def copy_out(name, o, i, scale=1.0, wait=True):
            if wait:
                act.wait_ge(*filled(name))
            run(o, i, ACT.Copy, scale=scale).then_inc(freed(name), 1)

        def rows_out(name, t, o, scale, f=ACT.Copy, done=None):
            act.wait_ge(*filled((name, t)))
            if t < 2:
                ins = run(o[:, t, :], bank_of((name, t)), f, scale=scale)
            else:
                for c in range(4):
                    ins = run(o[0:NS, t, 128 * c:128 * c + 128], bank_of((name, t))[NS * c:NS * c + NS, 0:128], f,
                              scale=scale)
            ins.then_inc(done or freed((name, t)), 1)

        for name, o in (("kvK", memk), ("kvV", memv)):
            for m in range(2):
                copy_out((name, m), o[:, m, :], bank_of((name, m)))
        for hf in range(2):
            copy_out(("KT", hf), KT[:, 2 * hf:2 * hf + 2, :].rearrange("p h m -> p (h m)"), bank_of(("KT", hf)))
        act.wait_ge(sg("small_in"), 16 * 9)
        astep(run(bias4[:, 4:5], bias4[:, 3:4], ACT.Exp))
        act.wait_ge(*filled("gates"))
        run(ROW_B, bank_of("gates")[96:100, 0:T], ACT.Exp, scale=-1.0).then_inc(sg("rowB"), 1)
        act.wait_ge(sg("rowZ"), 1)
        astep(run(ROW_E, ROW_E, ACT.Exp))
        run(ROW_E, ROW_E, ACT.Ln, bias=1.0).then_inc(sg("rowL"), 1)
        for t, (t0, n) in enumerate(TILES):
            rows_out("q", t, q_t, 1.0)
        for t, (t0, n) in enumerate(TILES):
            rows_out("k", t, k_t, QSCALE)
        act.wait_ge(sg("rowX"), 1)
        astep(run(ROW_EN, ROW_M, ACT.Exp, scale=-1.0))
        astep(run(ROW_EG, ROW_G, ACT.Exp))
        astep(run(ROW_W, ROW_W, ACT.Exp))
        astep(run(ROW_IW, ROW_IW, ACT.Exp))
        run(ROW_KD, ROW_KD, ACT.Exp).then_inc(sg("rows"), 1)
        act.preload_act_table_set("exp_and_others")
        for t, (t0, n) in enumerate(TILES):
            rows_out("mo", t, mo, 0.5, ACT.Tanh)
        def fill_at(t, point):
            for k in FILL[t][point]:
                act.wait_ge(*filled(("cv", k)))
                run(cvT[:, k, :], bank_of(("cv", k))[:, 0:T], ACT.Copy, scale=cwT[:, k, NB * HIST + HIST:NB * HIST + CW])
                run(cin[:, k, HIST:], bank_of(("cv", k))[:, 0:SEQ], ACT.Copy)
                run(cis[:, k, :].rearrange("p (b s) -> p b s", b=NB)[:, :, HIST:],
                    bank_of(("cv", k))[:, SEQ:T].rearrange("p (b s) -> p b s", b=NB), ACT.Copy) \
                    .then_inc(freed(("cv", k)), 1)

        act.preload_act_table_set("natural_log_exp_and_others")
        for t, (t0, n) in enumerate(TILES):
            qx, kx, qwx, dx, sx = forms(t)
            if t == 1:
                act.wait_ge(*filled(("sc", 0)))
            copy_out(("qT", t), qx[:, 0:H * n], bank_of(("qT", t))[:, 0:H * n])
            copy_out(("kT", t), kx[:, 0:H * n], bank_of(("kT", t))[:, 0:H * n])
            act.wait_ge(*filled(("dl", t)))
            act.wait_ge(*taken("cols"))
            if t == 1:
                act.wait_ge(sg("dT_free"), 1)
            for h in range(H):
                ins = run(dx[0:n, h * n:(h + 1) * n], bank_of(("dl", t))[0:n, h * n:(h + 1) * n], ACT.Exp,
                          bias=cols[0:n, t, COL_RS, h:h + 1])
            ins.then_inc(freed(("dl", t)), 1)
            fill_at(t, 0)
            fill_at(t, 1)
            for point in (2, 3) if t < 2 else (2, 3, 4, 5):
                fill_at(t, point)
            if t:
                act.wait_ge(*filled(("haT", t - 1)))
            if t == 2:
                act.wait_ge(*filled(("num", t, 0)))
                for h in range(H):
                    ins = run(num[0:n, DH * h:DH * h + DH], bank_of(("num", t, 0))[n * h:n * h + n, 0:DH], ACT.Copy)
            for g in range(2) if t < 2 else ():
                act.wait_ge(*filled(("num", t, g)))
                ins = run(num[0:n, 256 * g:256 * g + 256].rearrange("p (h v) -> p h v", h=2),
                          bank_of(("num", t, g))[0:n, 0:2 * DA].rearrange("p (h v) -> p h v", h=2)[:, :, 0:DH],
                          ACT.Copy)
            ins.then_inc(sg("num_in"), 1)
            if t < 2:
                fill_at(t, 4)
            act.wait_ge(sg("ms"), t + 1)
            astep(run(hs4[0:n, 3, :], hs4[0:n, 3, :], ACT.Ln, scale=1.0 / DH, bias=EPS))
            run(hs4[0:n, 4, :], hs4[0:n, 3, :], ACT.Exp, scale=-0.5).then_inc(sg("ms_r"), 1)
        act.wait_ge(*filled(("haT", 2)))
        run(rowG, ROW_G, ACT.Copy).then_inc(sg("rowG"), 1)
        copy_out("nT", nrow, bank_of("nT")[0:NB * H + H, 0:128])

        act.preload_act_table_set("exp_and_others")

        def gate_out(t):
            wd = 512 if t < 2 else 128
            act.wait_ge(*filled(("gout", t)))
            if t:
                act.wait_ge(*taken(("gout", t - 1)))
            run(gtmp[:, 0:wd], bank_of(("gout", t))[:, 0:wd], ACT.Tanh, scale=0.5).then_inc(sg("gout_e"), 1)

        for g in range(3):
            if g == 0:
                act.wait_ge(*filled(("haT", 2)))
            copy_out(("tail", g), tails[:, 512 * g:512 * g + 512], bank_of(("tail", g))[0:HIST * (NB + 1), :])
        act.wait_ge(sg("conv"), 2)
        act.wait_ge(sg("tailT"), 1)
        for t, (t0, n) in enumerate(TILES):
            rows_out("xq", t, xq, QSCALE)
        act.wait_ge(sg("conv"), 3)
        act.wait_ge(sg("Cs_out"), 16 * H)
        for g in range(2):
            run(stmp[:, g % 2, :], cvT[:, 4 * g:4 * g + 4, :].rearrange("p c t -> p (c t)"), ACT.Tanh, scale=0.5) \
                .then_inc(sg("silu_e"), 1)
        for t, (t0, n) in enumerate(TILES):
            copy_out(("xqT", t), xqT[:, :, t0:t0 + n],
                     bank_of(("xqT", t))[:, 0:H * n].rearrange("p (h l) -> p h l", h=H))
        def keys_out(b):
            if b >= 2:
                act.wait_ge(sg("K_read"), b - 1)
            copy_out(("KbT", b, 1), KTb[b % 2][:, 2:4, :].rearrange("p h m -> p (h m)"),
                     bank_of(("KbT", b, 1)))

        keys_out(0)
        keys_out(1)
        for i in range(2):
            act.wait_ge(sg("negmax"), i + 1)
            if i:
                act.wait_ge(*filled(("prT", i - 1, 1)))
            for h in range(H):
                name = ("xs", i, h // 2)
                ins = run(pr[:, h, :], bank_of(name)[:, MEM * (h % 2):MEM * (h % 2) + MEM], ACT.Exp,
                          bias=negmax[:, h:h + 1], accum_out=psumx[:, h:h + 1])
                if h % 2:
                    ins.then_inc(freed(name), 1)
            gate_out(i)
            copy_out(("prT", i, 0), prT[:, 0, :], bank_of(("prT", i, 0)))
            copy_out(("hcT", i), brT[2][:, :, 128 * i:128 * i + 128],
                     bank_of(("hcT", i)).rearrange("p (h l) -> p h l", h=H))
            keys_out(2 + i)
        gate_out(2)
        act.wait_ge(sg("cvT"), 1)
        run(stmp[:, 0, :], cvT[:, 8:12, :].rearrange("p c t -> p (c t)"), ACT.Tanh, scale=0.5) \
            .then_inc(sg("silu_e"), 1)
        for b in range(4, NB):
            keys_out(b)
        act.wait_ge(sg("negmax"), 3)
        act.wait_ge(*filled(("prT", 1, 1)))
        run(pr[:, 0, :], bank_of("ss")[:, 0:MEM], ACT.Exp, bias=negmax[:, 0:1], accum_out=psumx[:, 0:1]) \
            .then_inc(freed("ss"), 1)
        copy_out("hcs", hcs, bank_of("hcs")[:, 0:128])

        steps_m, parts_done = [0], [0]

        def merge_out(j, nn, t):
            wd = 512 if t < 2 else 128
            act.wait_ge(*filled(("mg", j, nn, t)))
            if steps_m[0] >= 2:
                act.wait_ge(sg("sig_read"), steps_m[0] - 1)
            run(sig[:, steps_m[0] % 2, 0:wd], bank_of(("mg", j, nn, t))[:, 0:wd], ACT.Tanh, scale=0.5) \
                .then_inc(freed(("mg", j, nn, t)), 1)
            steps_m[0] += 1

        def part():
            j, nn, t, x = PARTS[parts_done[0]]
            parts_done[0] += 1
            if x >= 2:
                merge_out(j, nn, t)

        def part_at(t, point):
            for _ in range(PART_AT[t][point]):
                if parts_done[0] < len(PARTS):
                    part()

        for t, (t0, n) in enumerate(TILES):
            if t == 0:
                act.wait_ge(*filled("hcsT"))
            for g in range(3):
                act.wait_ge(*filled(("raw", t, g)))
                copy_out(("raw", t, g), raw[0:n, g, :], bank_of(("raw", t, g))[0:n, :], wait=False)
            act.preload_act_table_set("natural_log_exp_and_others")
            act.wait_ge(sg("gss"), t + 1)
            astep(run(hs4[0:n, 0:2, :], hs4[0:n, 0:2, :], ACT.Ln, bias=EPS))
            run(hs4[0:n, 2:4, :], hs4[0:n, 0:2, :], ACT.Exp, scale=-0.5).then_inc(sg("gss_r"), 1)
            act.preload_act_table_set("exp_and_others")
            part_at(t, "raw")
            copy_out(("kT2", t), kT[:, 0:H * n], bank_of(("kT2", t))[:, 0:H * n])
            act.wait_ge(*filled(("dG", t)))
            if t == 0:
                act.wait_ge(sg("tail_out"), 32)
            for h in range(H):
                ins = run(dG[0:n, h * n:(h + 1) * n], bank_of(("dG", t))[0:n, h * n:(h + 1) * n], ACT.Exp,
                          bias=cols[0:n, t, COL_G, h:h + 1])
            ins.then_inc(freed(("dG", t)), 1)
            copy_out(("qT2", t), qT[:, 0:H * n], bank_of(("qT2", t))[:, 0:H * n])
            part_at(t, "forms")
            part_at(t, "KK")
            for k in range(1, 2 if t == 2 else LEVELS):
                copy_out(("X", t, k), Xm[0:n, 0:H * n], bank_of(("X", t, k))[0:n, 0:H * n])
                part_at(t, "level")
            copy_out(("wT", t), kbT[:, 0:H * n], bank_of(("wT", t))[:, 0:H * n], scale=-1.0)
            if t < 2:
                for c in range(2):
                    r = slice(L * c, L * c + L)
                    copy_out(("vn", t, c), vn[r, :], bank_of(("vn", t, c))[r, :])
                    part_at(t, "vn")
                    act.wait_ge(*filled(("go", t, c)))
                    copy_out(("go", t, c), Xm[r, :], bank_of(("go", t, c))[r, :], wait=False)
            else:
                act.wait_ge(*filled("vn2"))
                for h in range(H):
                    ins = run(vn[0:n, DH * h:DH * h + DH], bank_of("vn2")[n * h:n * h + n, 0:DH], ACT.Copy)
                ins.then_inc(freed("vn2"), 1)
                act.wait_ge(*filled("go2"))
                for h in range(H):
                    ins = run(Xm[0:n, DH * h:DH * h + DH], bank_of("go2")[n * h:n * h + n, 0:DH], ACT.Copy)
                ins.then_inc(freed("go2"), 1)
                for h in range(H):
                    part_at(t, "vn")
            part_at(t, "hb")
            act.preload_act_table_set("natural_log_exp_and_others")
            act.wait_ge(sg("gs"), t + 1)
            astep(run(hs4[0:n, 6, :], hs4[0:n, 5, :], ACT.Ln, scale=1.0 / DH, bias=EPS))
            run(hs4[0:n, 7, :], hs4[0:n, 6, :], ACT.Exp, scale=-0.5).then_inc(sg("gs_r"), 1)
            act.preload_act_table_set("exp_and_others")

        while parts_done[0] < len(PARTS):
            part()
        for nn in range(2):
            for t, (t0, n) in enumerate(TILES):
                merge_out(1, nn, t)
                if nn == 1:
                    copy_out(("mixT", t, 0), mixT[:, 0:4, t0:t0 + n],
                             bank_of(("mixT", t, 0))[:, 0:4 * n].rearrange("p (c l) -> p c l", c=4), scale=0.5)

        def rms_x2(t, n, where):
            astep(run(where[0:n, :], x2[0:n, t, :], ACT.Square, accum_out=rst[0:n, t:t + 1]))
            astep(run(rst[0:n, t:t + 1], rst[0:n, t:t + 1], ACT.Ln, scale=1.0 / D, bias=EPS))
            run(rst[0:n, t:t + 1], rst[0:n, t:t + 1], ACT.Exp, scale=-0.5).then_inc(sg("rst"), 1)

        act.preload_act_table_set("natural_log_exp_and_others")
        for t, (t0, n) in enumerate(TILES):
            act.wait_ge(sg("x2"), t + 1)
            rms_x2(t, n, Pm[:, 0, :])
        act.wait_ge(sg("lge"), 1)
        run(rtmp, rtmp, ACT.Exp).then_inc(sg("lge_r"), 1)
        act.wait_ge(sg("top"), 1)
        run(rt1[:, 5, :], rt1[:, 4, :], ACT.Exp).then_inc(sg("top_r"), 1)

        def slots_out(p=None):
            for e in range(E // 2):
                b, k = uses[("PwT", e)] if p is None else t_order(e, p)
                act.wait_ge(full[b], k + 1)
                run(PwT[:, e, :], PS[:, b, 0:T], ACT.Copy).then_inc(free[b], 1)

        slots_out()
        act.preload_act_table_set("exp_and_others")

        def group(p, g):
            it = 4 * p + g
            for pr_ in range(2):
                act.wait_ge(sg("pws_free"), it * 2 + (pr_ + 1))
                run(pws[pr_], PwT[:, bass.ds(g * 2 + pr_, 1), :].rearrange("p a t -> p (a t)"), ACT.Copy) \
                    .then_inc(sg("pws"), 1)
            for pr_ in range(2):
                for e in (2 * pr_, 2 * pr_ + 1):
                    act.wait_ge(*gfilled("gu", e, p, g))
                    act.wait_ge(sg("ea_free"), it * 4 + (e + 1))
                    run(ea[:, e % 2, :], gbank("gu", e)[:, 0:256], ACT.Tanh, scale=0.5).then_inc(sg("ea"), 1)
                for e in (2 * pr_, 2 * pr_ + 1):
                    act.wait_ge(*gfilled("aT", e, p, g))
                    if e < 2:
                        act.wait_ge(sg("act_free"), it * 4 + (e + 1))
                    else:
                        act.wait_ge(*gfilled("dn", 1, p, g))
                    run(actT[e % 2], gbank("aT", e)[:, 0:256], ACT.Copy).then_inc(gfree("aT", e), 1)
                act.wait_ge(*gfilled("dn", 2 * pr_, p, g))
                act.wait_ge(sg("outp_free"), it * 2 + (pr_ + 1))
                run(outp[:, 0:512], gbank("dn", 2 * pr_), ACT.Copy).then_inc(gfree("dn", 2 * pr_), 1)

        with act.Fori(0, G) as g:
            group(0, g)
        act.wait_ge(sg("flag"), 1)
        most = act.value_load(flag[0:1, 0:1], min_val=0, max_val=T)
        with act.If(most > SLOTS):
            with act.Fori(1, PASSES) as p:
                slots_out(p)
                with act.Fori(0, G) as g:
                    group(p, g)
        act.preload_act_table_set("natural_log_exp_and_others")
        for t, (t0, n) in enumerate(TILES):
            act.wait_ge(sg("x3"), 1 + t // 2)
            rms_x2(t, n, Pw[:, 0, :])

    @block.vector
    def _(dve):
        tt, ts, stt = dve.tensor_tensor, dve.tensor_scalar, dve.scalar_tensor_tensor
        cp = dve.tensor_copy

        marks = [0]

        def mark(sem_, n=1):
            marks[0] = (marks[0] + 1) % NSCRAP
            dve.memset(scrap[:, marks[0]:marks[0] + 1], 0.0).then_inc(sem_, n)

        dve.wait_ge(*filled("vec"))
        cp(vecT, bank_of("vec")[:, 0:NV]).then_inc(freed("vec"), 1)
        for i, j in enumerate((3, 4, 0, 1, 2)):
            n = NS if j == 2 else 128
            dve.wait_ge(sg("rstd"), i + 1)
            ts(xin[0:n, j, :], xin[0:n, j, :], rstd[0:n, j:j + 1], None, ALU.mult).then_inc(sg("x_norm"), 1)
        dve.wait_ge(*taken("vec"))
        for j in (3, 4, 0, 1, 2):
            n = NS if j == 2 else 128
            for hf in range(2):
                g0 = (V_MEM if j > 2 else V_MIX) + 4 * hf
                dst = memT[:, 4 * hf:4 * hf + 4, 128 * (j - 3):128 * (j - 2)] if j > 2 else \
                    hT[:, 4 * hf:4 * hf + 4, TILES[j][0]:TILES[j][0] + n]
                dve.wait_ge(*filled(("xT", j, hf)))
                tt(dst, bank_of(("xT", j, hf))[:, 0:4 * n].rearrange("p (c l) -> p c l", c=4),
                   bc(vecT[:, g0:g0 + 4].unsqueeze(2), 128, 4, n), ALU.mult).then_inc(freed(("xT", j, hf)), 1)

        dve.wait_ge(*filled("crow"))
        cp(cwT, bank_of("crow")[:, 0:NCT * (NB * HIST + CW)].rearrange("p (c r) -> p c r", c=NCT)) \
            .then_inc(freed("crow"), 1)

        dve.wait_ge(sg("small_in"), 16 * 9)
        dve.wait_ge(*filled("gates"))
        gt = bank_of("gates")
        ts(ROW_Z[:, 0, :], gt[32:32 + H, 0:T], bias4[:, 1:2], None, ALU.add)
        dstep(ts(ROW_Z[:, 1, :], gt[64:64 + H, 0:T], bias4[:, 2:3], None, ALU.add))
        stt(ROW_E, ROW_Z, -1.0, ROW_Z, ALU.mult, ALU.min).then_inc(sg("rowZ"), 1)
        dstep(ts(ROW_I, gt[0:H, 0:T], bias4[:, 0:1], None, ALU.add))
        dve.wait_ge(sg("rowB"), 1)
        dstep(ts(ROW_B, ROW_B, 1.0, None, ALU.add))
        dve.reciprocal(ROW_B, ROW_B).then_inc(freed("gates"), 1)
        dve.wait_ge(sg("rowL"), 1)
        dstep(stt(ROW_F, ROW_Z[:, 0, :], 0.0, ROW_E[:, 0, :], ALU.min, ALU.subtract))
        dstep(stt(ROW_A, ROW_Z[:, 1, :], 0.0, ROW_E[:, 1, :], ALU.max, ALU.add))
        dstep(ts(ROW_A, ROW_A, bias4[:, 4:5], -1.0, ALU.mult, ALU.mult))
        dve.wait_ge(sg("cst_in"), 16)
        dstep(dve.tensor_tensor_scan(ROW_BC, rset, ROW_F, 0.0, ALU.mult, ALU.add))
        dstep(dve.tensor_tensor_scan(ROW_G, rset, ROW_A, 0.0, ALU.mult, ALU.add))
        dstep(dve.tensor_tensor_scan(ROW_M[:, 0:SEQ], ROW_F[:, 0:SEQ], ROW_I[:, 0:SEQ], 0.0, ALU.add, ALU.max))

        def steps_of(r):
            return r[:, SEQ:T].rearrange("p (b s) -> p b s", b=NB)

        def chunks_of(r):
            return r[:, 0:SEQ].rearrange("p (c s) -> p c s", c=SEQ // L)

        fs, is_, ms = steps_of(ROW_F), steps_of(ROW_I), steps_of(ROW_M)
        for s in range(DS):
            dstep(tt(ms[:, :, s], m0 if s == 0 else ms[:, :, s - 1], fs[:, :, s], ALU.add))
            dstep(tt(ms[:, :, s], ms[:, :, s], is_[:, :, s], ALU.max))
        dstep(tt(ROW_RS, ROW_I, ROW_BC, ALU.subtract))
        dstep(tt(ROW_RL, ROW_BC, ROW_M, ALU.subtract))
        nch = SEQ // L
        for part, c, n in ((chunks_of, nch, L), (steps_of, NB, DS)):
            rl, rs, g, m = part(ROW_RL), part(ROW_RS), part(ROW_G), part(ROW_M)
            tt(part(ROW_W), rs, bc(rl[:, :, n - 1:n], H, c, n), ALU.add)
            tt(part(ROW_KD), bc(g[:, :, n - 1:n], H, c, n), g, ALU.subtract)
            if c == nch:
                tt(part(ROW_IW)[:, 1:, :], rl[:, 1:, :], bc(m[:, 0:c - 1, n - 1:n], H, c - 1, n), ALU.add)
                cp(part(ROW_IW)[:, 0, :], rl[:, 0, :])
            else:
                ins = tt(part(ROW_IW), rl, bc(m0.unsqueeze(2), H, c, n), ALU.add)
        ins.then_inc(sg("rowX"), 1)
        dve.wait_ge(sg("x_norm"), 5)
        for t, (t0, n) in enumerate(TILES):
            va = v_a[0:n, t, :].rearrange("p (h v) -> p h v", h=H)
            dve.wait_ge(*filled(("v", t)))
            dve.memset(va[:, :, DH:DA], 1.0)
            if t < 2:
                ins = cp(va[:, :, 0:DH], bank_of(("v", t)).rearrange("p (h v) -> p h v", h=H))
            else:
                for h in range(H):
                    ins = cp(va[:, h, 0:DH], bank_of(("v", t))[NS * h:NS * h + NS, 0:DH])
            ins.then_inc(freed(("v", t)), 1)
        for t, (t0, n) in enumerate(TILES):
            dve.wait_ge(*taken(("mo", t)))
            dstep(ts(mo[0:n, t, :], mo[0:n, t, :], 0.5, 0.5, ALU.mult, ALU.add))
        dve.memset(cin[:, :, 0:HIST], 0.0)
        cp(cis.rearrange("p c (b s) -> p c b s", b=NB)[:, :, :, 0:HIST],
           cwT[:, :, 0:NB * HIST].rearrange("p c (b s) -> p c b s", b=NB))
        dve.wait_ge(sg("memk_out"), 32)
        dve.memset(Cp, 0.0).then_inc(sg("C0"), 1)
        dve.wait_ge(*filled("cols"))
        for t, (t0, n) in enumerate(TILES):
            src = bank_of("cols")[0:n, 32 * t:32 * t + 32].rearrange("p (q h) -> p q h", h=H)
            ins = cp(cols[0:n, t, :, :], src)
            steps["dve"] += 1
            ins.then_inc(dve_step, 1)
        dve.wait_ge(dve_step, steps["dve"])
        for t, (t0, n) in enumerate(TILES):
            ins = ts(cols[0:n, t, COL_G, :], cols[0:n, t, COL_G, :], -1.0, None, ALU.mult)
        ins.then_inc(freed("cols"), 1)
        dve.wait_ge(*taken("cols"))
        dve.wait_ge(*filled("dec"))
        dstep(cp(dec, bank_of("dec")[:, 0:H * NCH].rearrange("p (h c) -> p h c", h=H)))
        cp(gl, bank_of("dec")[:, H * NCH:2 * H * NCH].rearrange("p (h c) -> p h c", h=H)) \
            .then_inc(freed("dec"), 1)
        dve.wait_ge(*taken("dec"))

        def spread(c, t, n, width=DH):
            return bc(cols[0:n, t, c, :].unsqueeze(2), n, H, width)

        def heads(x):
            return x.rearrange("p (h v) -> p h v", h=H)

        def conv_tap(g, j):
            if j == 0:
                dve.wait_ge(*taken(("cv", 4 * g + 3)))
            for c in range(4 * g, 4 * g + 4):
                w = cwT[:, c, NB * HIST + j:NB * HIST + j + 1]
                xp = cin[:, c, j:j + SEQ]
                xs = cis[:, c, :].rearrange("p (b s) -> p b s", b=NB)[:, :, j:j + DS]
                op_, os_ = cvT[:, c, 0:SEQ], cvT[:, c, SEQ:T].rearrange("p (b s) -> p b s", b=NB)
                stt(op_, xp, w, op_, ALU.mult, ALU.add)
                ins = stt(os_, xs, w, os_, ALU.mult, ALU.add)
            if j < CW - 2:
                dstep(ins)
            else:
                ins.then_inc(sg("conv"), 1)

        for t, (t0, n) in enumerate(TILES):
            qx, kx, qwx, dx, sx = forms(t)
            dve.wait_ge(*filled(("qT", t)))
            tt(heads(q_t[0:n, t, :]), heads(q_t[0:n, t, :]), spread(COL_IW, t, n), ALU.mult).then_inc(sg("qw"), 1)
            dve.wait_ge(*filled(("kT", t)))
            tt(heads(k_t[0:n, t, :]), heads(k_t[0:n, t, :]), spread(COL_W, t, n), ALU.mult).then_inc(sg("kw"), 1)
            dve.wait_ge(*filled(("qwT", t)))
            if t == 1:
                dve.wait_ge(*filled(("num", 0, 1)))
            cp(qwx[:, 0:H * n], bank_of(("qwT", t))[:, 0:H * n]).then_inc(freed(("qwT", t)), 1)
            dve.wait_ge(*taken(("dl", t)))
            dve.wait_ge(*filled(("sc", t)))
            dstep(tt(sx[0:n, 0:H * n], bank_of(("sc", t))[0:n, 0:H * n], dx[0:n, 0:H * n], ALU.mult))
            mark(freed(("sc", t)), 1)
            mark(sg("sT"), 1)
            if t:
                conv_tap(t - 1, 0)

            def update(t, c):
                ch = 2 * t + c
                for g in range(2):
                    dve.wait_ge(*filled(("Cu", t, c, g)))
                    for h in (2 * g, 2 * g + 1):
                        u = bank_of(("Cu", t, c, g))[:, (h % 2) * DA:(h % 2 + 1) * DA]
                        ins = stt(Cp[:, h, :], Cp[:, h, :], dec[:, h, ch:ch + 1], u, ALU.mult, ALU.add)
                    ins.then_inc(freed(("Cu", t, c, g)), 1)
                dve.wait_ge(*taken(("Cu", t, c, 1)))

            if t < 2:
                update(t, 0)
                if t:
                    conv_tap(t - 1, 1)
                update(t, 1)
                if t:
                    conv_tap(t - 1, 2)
                if t == 1:
                    cp(nst[:, NB * H:], Cp[:, :, DH]).then_inc(sg("Cp"), 1)
            else:
                dve.wait_ge(sg("Cs_in"), 16 * H)
                dstep(cp(Cs[:, :, :, DH], vecT[:, V_N0:V_N0 + NB * H].rearrange("p (b h) -> p h b", h=H)))
                dve.wait_ge(*filled(("num", 1, 1)))
                dve.wait_ge(*taken(("qwT", t)))
                tt(qwm, bc(qwx.rearrange("p (h l) -> p h l", h=H).unsqueeze(2), 128, H, NB, n),
                   bc(cst[:, C_BROW:C_BROW + NB * n].rearrange("p (b l) -> p b l", b=NB).unsqueeze(1),
                      128, H, NB, n), ALU.mult).then_inc(sg("qwm"), 1)

                def masked_values(h):
                    if h >= 2:
                        dve.wait_ge(*filled(("Cs", h - 2, 2)))
                    tt(vblk[h % 2], bc(v_a[0:n, t, h * DA:(h + 1) * DA].unsqueeze(1), n, NB, DA),
                       bc(cst[0:n, C_BCOL:C_BCOL + NB].unsqueeze(2), n, NB, DA), ALU.mult) \
                        .then_inc(sg("vblk"), 1)

                masked_values(0)
                for h in range(H):
                    if h < H - 1:
                        masked_values(h + 1)
                    for g, (b0, b1) in enumerate(((0, 3), (3, 6), (6, 8))):
                        dve.wait_ge(*filled(("Cs", h, g)))
                        for b in range(b0, b1):
                            u = bank_of(("Cs", h, g))[:, (b - b0) * DA:(b - b0 + 1) * DA]
                            ins = stt(Cs[:, h, b, :], Cs[:, h, b, :], dec[:, h, 4 + b:5 + b], u, ALU.mult, ALU.add)
                        ins.then_inc(freed(("Cs", h, g)), 1)
                    dve.wait_ge(*taken(("Cs", h, 2)))
                    cp(nst[:, h:NB * H:H], Cs[:, h, :, DH]).then_inc(sg("Cs"), 1)
                    if h < 2:
                        conv_tap(t - 1, 1 + h)
            dve.wait_ge(sg("num_in"), t + 1)
            if t < 2:
                for g in range(2):
                    cp(hs4[0:n, 0, 2 * g:2 * g + 2],
                       bank_of(("num", t, g))[0:n, 0:2 * DA].rearrange("p (h v) -> p h v", h=2)[:, :, DH]) \
                        .then_inc(freed(("num", t, g)), 1)
                dve.wait_ge(*taken(("num", t, 1)))
            else:
                for h in range(H):
                    ins = cp(hs4[0:n, 0, h:h + 1], bank_of(("num", t, 0))[n * h:n * h + n, DH:DA])
                ins.then_inc(freed(("num", t, 0)), 1)
            dve.wait_ge(*taken(("num", t, 0)))
            dstep(stt(hs4[0:n, 1, :], hs4[0:n, 0, :], -1.0, hs4[0:n, 0, :], ALU.mult, ALU.max))
            dstep(tt(hs4[0:n, 1, :], hs4[0:n, 1, :], cols[0:n, t, COL_EN, :], ALU.max))
            dstep(dve.reciprocal(hs4[0:n, 1, :], hs4[0:n, 1, :]))
            dstep(tt(dx[0:n, 0:128 * H] if t < 2 else dT[0:n, :], num[0:n, :], num[0:n, :], ALU.mult))
            dstep(dve.tensor_reduce(hs4[0:n, 2, :], heads(dT[0:n, :]), AX.X, ALU.add))
            if t == 0:
                mark(sg("dT_free"), 1)
            dstep(tt(hs4[0:n, 2, :], hs4[0:n, 2, :], hs4[0:n, 1, :], ALU.mult))
            tt(hs4[0:n, 3, :], hs4[0:n, 2, :], hs4[0:n, 1, :], ALU.mult).then_inc(sg("ms"), 1)
            dve.wait_ge(sg("ms_r"), t + 1)
            dstep(tt(hs4[0:n, 5, :], hs4[0:n, 4, :], hs4[0:n, 1, :], ALU.mult))
            dstep(tt(heads(num[0:n, :]), heads(num[0:n, :]), bc(hs4[0:n, 5, :].unsqueeze(2), n, H, DH), ALU.mult))
            tt(num[0:n, :], num[0:n, :], mo[0:n, t, :], ALU.mult).then_inc(sg("ha"), 1)
            dve.wait_ge(*filled(("haT", t)))
            tt(brT[0][:, :, t0:t0 + n], bank_of(("haT", t))[:, 0:H * n].rearrange("p (h l) -> p h l", h=H),
               bc(vecT[:, V_ML:V_ML + H].unsqueeze(2), 128, H, n), ALU.mult).then_inc(freed(("haT", t)), 1)
        dve.wait_ge(*taken(("haT", 2)))
        dve.wait_ge(sg("Cs"), 4)
        mark(sg("nst"), 1)

        tl = tailT.rearrange("p c (b s) -> p c b s", s=HIST)
        dve.wait_ge(*taken(("cv", NCT - 1)))
        cp(tl[:, :, 0, :], cin[:, :, SEQ:SEQ + HIST])
        cp(tl[:, :, 1:, :], cis.rearrange("p c (b s) -> p c b s", b=NB)[:, :, :, DS:DS + HIST]) \
            .then_inc(sg("tailT"), 1)
        for j in range(CW - 1):
            conv_tap(2, j)

        def gate_out(t):
            n = TILES[t][1]
            dve.wait_ge(sg("gout_e"), t + 1)
            if t < 2:
                ins = stt(gout[:, t, :], gtmp, 1.0, bank_of(("gout", t)), ALU.add, ALU.mult)
            else:
                for c in range(4):
                    r = slice(n * c, n * c + n)
                    ins = stt(gout[0:n, t, 128 * c:128 * c + 128], gtmp[r, 0:128], 1.0,
                              bank_of(("gout", t))[r, 0:128], ALU.add, ALU.mult)
            ins.then_inc(freed(("gout", t)), 1)

        def silu(g):
            e = stmp[:, g % 2, :]
            v = cvT[:, 4 * g:4 * g + 4, :].rearrange("p c t -> p (c t)")
            dve.wait_ge(sg("silu_e"), g + 1)
            dstep(ts(e, e, 0.5, 0.5, ALU.mult, ALU.add))
            tt(v, v, e, ALU.mult).then_inc(sg("cvT"), 1)
            dve.wait_ge(sg("cvT"), g + 1)

        dve.wait_ge(*taken(("xqT", 2)))
        tt(qm.rearrange("p h (b l) -> p h b l", b=NB), bc(xqT[:, :, SEQ:T].unsqueeze(2), 128, H, NB, NS),
           bc(cst[:, C_BROW:C_BROW + NB * NS].rearrange("p (b l) -> p b l", b=NB).unsqueeze(1),
              128, H, NB, NS), ALU.mult).then_inc(sg("qm"), 1)
        def keys_out(b):
            dve.wait_ge(*filled(("KbT", b, 0)))
            if b >= 2:
                dve.wait_ge(sg("K_read"), b - 1)
            cp(KTb[b % 2][:, 0:2, :].rearrange("p h m -> p (h m)"), bank_of(("KbT", b, 0))) \
                .then_inc(freed(("KbT", b, 0)), 1)

        keys_out(0)
        keys_out(1)
        for i in range(2):
            for g in range(2):
                dve.wait_ge(*filled(("xs", i, g)))
                ins = dve.tensor_reduce(negmax[:, 2 * g:2 * g + 2],
                                        bank_of(("xs", i, g)).rearrange("p (h m) -> p h m", h=2),
                                        AX.X, ALU.max, negate=True)
            ins.then_inc(sg("negmax"), 1)
            dve.wait_ge(*taken(("xs", i, 1)))
            dstep(dve.reciprocal(psumx, psumx))
            tt(pr, pr, bc(psumx.unsqueeze(2), 128, H, MEM), ALU.mult).then_inc(sg("pr"), 1)
            gate_out(i)
            if i:
                dve.wait_ge(*filled(("hcT", 0)))
            dve.wait_ge(*filled(("prT", i, 1)))
            cp(prT[:, 1, :], bank_of(("prT", i, 1))).then_inc(freed(("prT", i, 1)), 1)
            keys_out(2 + i)
            silu(i)
        gate_out(2)
        silu(2)
        for b in range(4, NB):
            keys_out(b)
        dve.wait_ge(*filled("ss"))
        dve.tensor_reduce(negmax[:, 0:1], bank_of("ss")[:, 0:MEM], AX.X, ALU.max, negate=True) \
            .then_inc(sg("negmax"), 1)
        dve.wait_ge(*taken("ss"))
        dstep(dve.reciprocal(psumx[:, 0:1], psumx[:, 0:1]))
        ts(pr[:, 0, :], pr[:, 0, :], psumx[:, 0:1], None, ALU.mult).then_inc(sg("pr"), 1)
        dve.wait_ge(*filled("spT"))
        for m in range(2):
            ins = tt(spT[:, m, :].rearrange("p (b h l) -> p b h l", b=NB, h=H),
                     bc(bank_of("spT")[:, 128 * m:128 * m + 128].rearrange("p (h l) -> p h l", h=H).unsqueeze(1),
                        128, NB, H, NS),
                     bc(cst[:, C_BROW:C_BROW + NB * NS].rearrange("p (b l) -> p b l", b=NB).unsqueeze(2),
                        128, NB, H, NS), ALU.mult)
        ins.then_inc(freed("spT"), 1)
        dve.wait_ge(*filled("hcsT"))
        cp(brT[2][:, :, SEQ:T], bank_of("hcsT")[:, 0:128].rearrange("p (h l) -> p h l", h=H)) \
            .then_inc(freed("hcsT"), 1)
        dve.wait_ge(*taken("hcsT"))

        parts_done = [0]

        def merge_out(j, nn, t):
            wd = 512 if t < 2 else 128
            s = sig[:, steps_m[0] % 2, 0:wd]
            mx = mixed[:, t, 512 * nn:512 * nn + 512] if t < 2 else mixs[:, nn, :]
            dve.wait_ge(*taken(("mg", j, nn, t)))
            dve.wait_ge(*filled(("mb", j, nn, t)))
            o = bank_of(("mb", j, nn, t))[:, 0:wd]
            dst = mx if j == 0 else s
            stt(dst, s, 1.0, o, ALU.add, ALU.mult).then_inc(freed(("mb", j, nn, t)), 1)
            dve.wait_ge(*taken(("mb", j, nn, t)))
            if j:
                tt(mx, mx, s, ALU.add).then_inc(sg("sig_read"), 1)
            else:
                mark(sg("sig_read"))
            steps_m[0] += 1

        steps_m = [0]

        def part():
            j, nn, t, x = PARTS[parts_done[0]]
            parts_done[0] += 1
            if x >= 2:
                merge_out(j, nn, t)

        def part_at(t, point):
            for _ in range(PART_AT[t][point]):
                if parts_done[0] < len(PARTS):
                    part()

        dve.memset(Sp, 0.0).then_inc(sg("S0"), 1)
        for t, (t0, n) in enumerate(TILES):
            dve.wait_ge(*taken(("raw", t, 2)))
            q, k, v = (heads(raw[0:n, j, :]) for j in range(3))
            dstep(tt(kd[0:n, :], raw[0:n, 0, :], raw[0:n, 0, :], ALU.mult))
            dstep(tt(kbg[0:n, :], raw[0:n, 1, :], raw[0:n, 1, :], ALU.mult))
            dstep(dve.tensor_reduce(hs4[0:n, 0, :], heads(kd[0:n, :]), AX.X, ALU.add))
            dve.tensor_reduce(hs4[0:n, 1, :], heads(kbg[0:n, :]), AX.X, ALU.add).then_inc(sg("gss"), 1)
            dve.wait_ge(sg("gss_r"), t + 1)
            s4 = lambda j: hs4[0:n, j, :]
            wide = lambda x: bc(x.unsqueeze(2), n, H, DH)
            dstep(tt(s4(4), s4(3), cols[0:n, t, COL_B, :], ALU.mult))
            dstep(tt(s4(8), s4(4), cols[0:n, t, COL_EG, :], ALU.mult))
            dstep(tt(s4(9), s4(3), cols[0:n, t, COL_KD, :], ALU.mult))
            dstep(ts(s4(2), s4(2), QSCALE, None, ALU.mult))
            dstep(tt(s4(10), s4(2), cols[0:n, t, COL_EG, :], ALU.mult))
            tt(heads(kbg[0:n, :]), k, wide(s4(8)), ALU.mult)
            tt(heads(kd[0:n, :]), k, wide(s4(9)), ALU.mult)
            tt(heads(kb[0:n, :]), k, wide(s4(4)), ALU.mult)
            tt(heads(qd[0:n, :]), q, wide(s4(10)), ALU.mult)
            tt(v, v, spread(COL_B, t, n), ALU.mult).then_inc(sg("gv"), 1)
            dve.wait_ge(sg("gv"), t + 1)
            tt(k, k, wide(s4(3)), ALU.mult).then_inc(sg("gq"), 1)
            tt(q, q, wide(s4(2)), ALU.mult).then_inc(sg("gq"), 1)
            mark(sg("gq"), 1)
            mark(sg("gq"), 1)
            part_at(t, "raw")
            dve.wait_ge(*filled(("kbT", t)))
            cp(kbT[:, 0:H * n], bank_of(("kbT", t))[:, 0:H * n]).then_inc(freed(("kbT", t)), 1)
            dve.wait_ge(*filled(("qdT", t)))
            cp(qdT[:, 0:H * n], bank_of(("qdT", t))[:, 0:H * n]).then_inc(freed(("qdT", t)), 1)
            dve.wait_ge(*taken(("dG", t)))
            dve.wait_ge(*filled(("KK", t)))
            tt(AT[0:n, 0:H * n], bank_of(("KK", t))[0:n, 0:H * n], dG[0:n, 0:H * n], ALU.mult) \
                .then_inc(freed(("KK", t)), 1)
            dve.wait_ge(*filled(("QK", t)))
            tt(QKT[0:n, 0:H * n], bank_of(("QK", t))[0:n, 0:H * n], dG[0:n, 0:H * n], ALU.mult) \
                .then_inc(freed(("QK", t)), 1)
            dve.wait_ge(*taken(("QK", t)))
            part_at(t, "forms")
            part_at(t, "KK")
            blocks = lambda x: x[0:n, 0:H * n].rearrange("p (h l) -> p h l", h=H)
            idb = bc(ident[0:n, 0:n].unsqueeze(1), n, H, n)
            nl = 2 if t == 2 else LEVELS

            def between(lev):
                mk_ = cst[0:n, C_LVL + 128 * lev:C_LVL + 128 * lev + n]
                tt(blocks(Ak[lev % 2]), blocks(AT), bc(mk_.unsqueeze(1), n, H, n), ALU.mult) \
                    .then_inc(sg("ATk"), 1)

            between(0)
            between(1)
            for lev in range(nl):
                if lev == 0:
                    dve.wait_ge(sg("ATk"), lv(t, 0) + 1)
                    dstep(tt(blocks(Um), idb, blocks(dG), ALU.subtract))
                    dve.wait_ge(*filled(("X", t, 0)))
                    tt(blocks(Tm), idb, bank_of(("X", t, 0))[0:n, 0:H * n].rearrange("p (h l) -> p h l", h=H),
                       ALU.subtract).then_inc(freed(("X", t, 0)), 1)
                    dve.wait_ge(*taken(("X", t, 0)))
                    if nl > 2:
                        between(2)
                    continue
                if lev < nl - 1:
                    dve.wait_ge(*filled(("Y", t, lev)))
                    tt(Tm[0:n, 0:H * n], Tm[0:n, 0:H * n], bank_of(("Y", t, lev))[0:n, 0:H * n], ALU.subtract) \
                        .then_inc(freed(("Y", t, lev)), 1)
                    dve.wait_ge(*taken(("Y", t, lev)))
                dve.wait_ge(*filled(("YT", t, lev)))
                tt(Um[0:n, 0:H * n], Um[0:n, 0:H * n], bank_of(("YT", t, lev))[0:n, 0:H * n], ALU.subtract) \
                    .then_inc(freed(("YT", t, lev)), 1)
                dve.wait_ge(*taken(("YT", t, lev)))
                if lev + 2 < nl:
                    between(lev + 2)
                part_at(t, "level")
            if t < 2:
                for c in range(2):
                    ch = 2 * t + c
                    part_at(t, "vn")
                    dve.wait_ge(*filled(("go", t, c)))
                    dve.wait_ge(*filled(("So", t, c)))
                    for h in range(H):
                        hv = slice(128 * h, 128 * h + 128)
                        ins = stt(Sp[:, hv], Sp[:, hv], gl[:, h, ch:ch + 1], bank_of(("So", t, c))[:, hv],
                                  ALU.mult, ALU.add)
                    ins.then_inc(freed(("So", t, c)), 1)
                    dve.wait_ge(*taken(("So", t, c)))
                if t == 1:
                    mark(sg("Spout"), 1)
            else:
                dve.wait_ge(*taken(("wT", t)))
                brow = bc(cst[:, C_BROW:C_BROW + NB * n].rearrange("p (b l) -> p b l", b=NB).unsqueeze(1),
                          128, H, NB, n)
                for dst, src in ((qdm, qdT), (nwm, kbT)):
                    ins = tt(dst, bc(src[:, 0:H * n].rearrange("p (h l) -> p h l", h=H).unsqueeze(2), 128, H, NB, n),
                             brow, ALU.mult)
                ins.then_inc(sg("nwm"), 1)

                def masked_values(h):
                    if h >= 2:
                        dve.wait_ge(*filled(("So2", h - 2, 1)))
                    tt(vnb[h % 2], bc(vn[0:n, 128 * h:128 * h + 128].unsqueeze(1), n, NB, DH),
                       bc(cst[0:n, C_BCOL:C_BCOL + NB].unsqueeze(2), n, NB, DH), ALU.mult).then_inc(sg("vnb"), 1)

                dve.wait_ge(*taken("vn2"))
                masked_values(0)
                for h in range(H):
                    if h < H - 1:
                        masked_values(h + 1)
                    for g in range(2):
                        dve.wait_ge(*filled(("So2", h, g)))
                        for b in range(4 * g, 4 * g + 4):
                            ins = stt(Ss[h][:, b, :], Ss[h][:, b, :], gl[:, h, 4 + b:5 + b],
                                      bank_of(("So2", h, g))[:, 128 * (b - 4 * g):128 * (b - 4 * g) + 128],
                                      ALU.mult, ALU.add)
                        ins.then_inc(freed(("So2", h, g)), 1)
                    mark(sg("Ssd"), 1)
                    dve.wait_ge(sg("Ssd"), h + 1)
                    part_at(t, "vn")
            part_at(t, "hb")
            dve.wait_ge(*taken(("go", t, 1) if t < 2 else "go2"))
            dstep(tt(AT[0:n, :], Xm[0:n, :], Xm[0:n, :], ALU.mult))
            dve.tensor_reduce(hs4[0:n, 5, :], heads(AT[0:n, :]), AX.X, ALU.add).then_inc(sg("gs"), 1)
            dve.wait_ge(sg("gs_r"), t + 1)
            dstep(tt(heads(kb[0:n, :]), heads(Xm[0:n, :]), wide(s4(7)), ALU.mult))
            tt(kb[0:n, :], kb[0:n, :], gout[0:n, t, :], ALU.mult).then_inc(sg("hb"), 1)
            dve.wait_ge(*filled(("hbT", t)))
            ts(brT[1][:, :, t0:t0 + n], bank_of(("hbT", t))[:, 0:H * n].rearrange("p (h l) -> p h l", h=H),
               vecT[:, V_GD:V_GD + 1], 0.5, ALU.mult, ALU.mult).then_inc(freed(("hbT", t)), 1)

        while parts_done[0] < len(PARTS):
            part()
        def mixed_out(t, hf):
            t0, n = TILES[t]
            dve.wait_ge(*filled(("mixT", t, hf)))
            ts(mixT[:, 4 * hf:4 * hf + 4, t0:t0 + n],
               bank_of(("mixT", t, hf))[:, 0:4 * n].rearrange("p (c l) -> p c l", c=4),
               0.5, None, ALU.mult).then_inc(freed(("mixT", t, hf)), 1)

        for nn in range(2):
            for t in range(3):
                merge_out(1, nn, t)
                mark(sg("mixed"))
        for t in range(3):
            mixed_out(t, 1)
        dve.wait_ge(sg("x2_in"), 48)

        def scale_x2(t):
            n = TILES[t][1]
            dve.wait_ge(sg("rst"), t + 1)
            ts(h2p[0:n, t, :].rearrange("p (c f) -> p f c", c=KD), x2[0:n, t, :].rearrange("p (f c) -> p f c", c=KD),
               rst[0:n, t:t + 1], None, ALU.mult).then_inc(sg("h2p"), 1)

        for t, (t0, n) in enumerate(TILES):
            for nn in range(2):
                name = (("out", nn), t)
                dve.wait_ge(*filled(name))
                if t < 2:
                    xx = x2[:, t, 512 * nn:512 * nn + 512]
                    ins = tt(xx, xx, bank_of(name), ALU.add)
                else:
                    for c in range(4):
                        xx = x2[0:NS, t, 512 * nn + 128 * c:512 * nn + 128 * c + 128]
                        ins = tt(xx, xx, bank_of(name)[NS * c:NS * c + NS, 0:128], ALU.add)
                ins.then_inc(freed(name), 1)
            mark(sg("x2"))
            if t:
                scale_x2(t - 1)
        scale_x2(2)
        for t, (t0, n) in enumerate(TILES):
            for hf in range(2):
                dve.wait_ge(*filled(("h2T", t, hf)))
                tt(h2T[:, 4 * hf:4 * hf + 4, t0:t0 + n],
                   bank_of(("h2T", t, hf))[:, 0:4 * n].rearrange("p (c l) -> p c l", c=4),
                   bc(gffn[:, 4 * hf:4 * hf + 4].unsqueeze(2), 128, 4, n), ALU.mult) \
                    .then_inc(freed(("h2T", t, hf)), 1)
        dstep(dve.memset(LG, 0.0))
        dve.wait_ge(*filled("lg"))
        for t, (t0, n) in enumerate(TILES):
            ins = tt(LG[0:n, t, :], bank_of("lg")[0:n, 20 * t:20 * t + 20], brb[0:n, :], ALU.add)
        ins.then_inc(freed("lg"), 1)
        dve.wait_ge(*taken("lg"))
        first = cst[:, C_FIRST:C_FIRST + 3 * EG]
        flat = lambda x: x.rearrange("p t e -> p (t e)")
        w4 = lambda x: bc(x.unsqueeze(2), 128, 3, 4)

        def best(o, x, m):
            dstep(dve.tensor_reduce(m, x, AX.X, ALU.max))
            dstep(tt(oh2, x, w4(m), ALU.is_equal))
            dstep(dve.tensor_tensor_scan(le12, first, flat(oh2), 0.0, ALU.mult, ALU.add))
            dstep(stt(flat(o), le12, 1.0, flat(oh2), ALU.is_equal, ALU.mult))

        best(oh, LG[:, :, 0:G], rt1[:, 0, :])
        tt(rtmp, LG[:, :, 0:G], w4(rt1[:, 0, :]), ALU.subtract).then_inc(sg("lge"), 1)
        le = LG[:, :, G:20].rearrange("p t (g e) -> p t g e", g=G)
        lesel = rkm[:, :, 0:4]
        by_group = lambda x: x.rearrange("p t (g e) -> p t g e", g=G)
        chosen = bc(oh.unsqueeze(3), 128, 3, G, EG)
        dstep(tt(by_group(le4), le, chosen, ALU.mult))
        dstep(dve.tensor_reduce(lesel, le4.rearrange("p t (g e) -> p t e g", g=G), AX.X, ALU.add))
        best(oh1, lesel, rt1[:, 1, :])
        dstep(stt(lesel, oh1, NEG, lesel, ALU.mult, ALU.add))
        best(oh3, lesel, rt1[:, 2, :])
        tt(rt1[:, 4, :], rt1[:, 2, :], rt1[:, 1, :], ALU.subtract).then_inc(sg("top"), 1)
        dstep(tt(oh2, oh1, oh3, ALU.add))
        tt(by_group(msk), bc(oh2.unsqueeze(2), 128, 3, G, EG), chosen, ALU.mult).then_inc(sg("msk"), 1)
        dve.wait_ge(sg("lge_r"), 1)
        dstep(dve.tensor_reduce(rt1[:, 3, :], rtmp, AX.X, ALU.add))
        dstep(dve.reciprocal(rt1[:, 3, :], rt1[:, 3, :]))
        dve.wait_ge(sg("top_r"), 1)
        dstep(ts(rt1[:, 6, :], rt1[:, 5, :], 1.0, None, ALU.add))
        dstep(dve.reciprocal(rt1[:, 6, :], rt1[:, 6, :]))
        dstep(tt(rt1[:, 6, :], rt1[:, 6, :], rt1[:, 3, :], ALU.mult))
        dstep(tt(rt1[:, 7, :], rt1[:, 6, :], rt1[:, 5, :], ALU.mult))
        dstep(tt(rtmp, oh1, w4(rt1[:, 6, :]), ALU.mult))
        dstep(tt(le4[:, :, 0:4], oh3, w4(rt1[:, 7, :]), ALU.mult))
        dstep(tt(rtmp, rtmp, le4[:, :, 0:4], ALU.add))
        dstep(tt(by_group(cmb), bc(rtmp.unsqueeze(2), 128, 3, G, EG), chosen, ALU.mult))
        dstep(dve.memset(rkm, 0.0))
        dve.wait_ge(sg("msk"), 1)
        dve.wait_ge(*filled("rank"))
        for t, (t0, n) in enumerate(TILES):
            stt(rkm[0:n, t, :], bank_of("rank")[0:n, E * t:E * t + E], 1.0, msk[0:n, t, :], ALU.add, ALU.mult)
        dstep(dve.tensor_reduce(rt1[0:1, 11, 0:1], bank_of("rank")[0:1, 3 * E:4 * E], AX.X, ALU.max))
        cp(flag[0:1, 0:1], rt1[0:1, 11, 0:1]).then_inc(sg("flag"), 1)
        mark(freed("rank"), 1)

        def choices(p):
            k = 0

            def then(ins):
                nonlocal k
                k += 1
                ins.then_inc(sg("choice"), 1)
                dve.wait_ge(sg("choice"), (1 + 2 * G) * p + k)

            then(ts(le4, rkm, -1.0, None, ALU.add))
            for q in range(G):
                es = slice(EG * q, EG * q + EG)
                cols = slice(EG * SLOTS * q, EG * SLOTS * (q + 1))
                for src, by, dst, op in ((None, le4, Pm, ALU.is_equal), (Pm, cmb, Pw, ALU.mult)):
                    for t, (t0, n) in enumerate(TILES):
                        x = bc(cst[0:n, C_IOTA:C_IOTA + SLOTS].unsqueeze(1), n, EG, SLOTS) if src is None \
                            else src[0:n, t, cols].rearrange("p (e j) -> p e j", e=EG)
                        ins = tt(dst[0:n, t, cols].rearrange("p (e j) -> p e j", e=EG), x,
                                 bc(by[0:n, t, es].unsqueeze(2), n, EG, SLOTS), op)
                    then(ins)
                mark(sg("Pm"))

        choices(0)
        mark(sg("pws_free"), 2)
        dstep(dve.memset(ysum, 0.0))
        mark(sg("ea_free"), 2)
        mark(sg("act_free"), 2)
        mark(sg("outp_free"), 1)

        def group(p, g):
            it = 4 * p + g
            for j in range(4):
                dve.wait_ge(*gfilled("hg", j, p, g))
                tt(hg[:, 2 * j:2 * j + 2, :], gbank("hg", j).rearrange("p (c l) -> p c l", c=2),
                   bc(gffn[:, 2 * j:2 * j + 2].unsqueeze(2), 128, 2, 256), ALU.mult).then_inc(gfree("hg", j), 1)
            for pr_ in range(2):
                for e in (2 * pr_, 2 * pr_ + 1):
                    ee, ab = ea[:, e % 2, :], actb[:, e % 2, :]
                    dve.wait_ge(sg("ea"), it * 4 + (e + 1))
                    stt(ee, ee, 1.0, gbank("gu", e)[:, 0:256], ALU.add, ALU.mult).then_inc(sg("silu"), 1)
                    dve.wait_ge(sg("silu"), it * 4 + (e + 1))
                    stt(ab, ee, 0.5, gbank("gu", e)[:, 256:512], ALU.mult, ALU.mult).then_inc(sg("act"), 1)
                    dve.wait_ge(sg("act"), it * 4 + (e + 1))
                    mark(gfree("gu", e), 1)
                    mark(sg("ea_free"), 1)
                if pr_ == 1:
                    add_y(0, p, g)
                dve.wait_ge(*gfilled("dn", 2 * pr_ + 1, p, g))
                dve.wait_ge(sg("outp_free"), it * 2 + (pr_ + 1))
                cp(outp[:, 512:1024], gbank("dn", 2 * pr_ + 1)).then_inc(gfree("dn", 2 * pr_ + 1), 1)
            add_y(1, p, g)
            mark(sg("act_free"), 4)
            mark(sg("pws_free"), 2)

        def add_y(pr_, p, g):
            it = 4 * p + g
            for nn in range(2):
                for t in range(2):
                    j = 5 * pr_ + 2 * nn + t
                    dve.wait_ge(*gfilled("y", j, p, g))
                    xx = x2[:, t, 512 * nn:512 * nn + 512]
                    tt(xx, xx, gbank("y", j), ALU.add).then_inc(gfree("y", j), 1)
            j = 5 * pr_ + 4
            dve.wait_ge(*gfilled("y", j, p, g))
            tt(ysum, ysum, gbank("y", j)[:, 0:256], ALU.add).then_inc(gfree("y", j), 1)
            mark(sg("outp_free"), 1)

        with dve.Fori(0, G) as g:
            group(0, g)
        dve.wait_ge(sg("flag"), 1)
        most = dve.value_load(flag[0:1, 0:1], min_val=0, max_val=T)
        with dve.If(most > SLOTS):
            with dve.Fori(1, PASSES) as p:
                for e in (2, 3):
                    dve.wait_ge(*moved("dn", e, p - 1, G - 1))
                dve.wait_ge(*moved("y", 9, p - 1, G - 1))
                ts(rkm, rkm, -float(SLOTS), None, ALU.add).then_inc(sg("shift"), 1)
                dve.wait_ge(sg("shift"), p)
                choices(p)
                with dve.Fori(0, G) as g:
                    group(p, g)
        mark(sg("x3"), 1)
        dve.wait_ge(sg("x3"), 1)
        ytmp = Pw[0:NS, 2, :]
        for nn in range(2):
            for c in range(4):
                ins = cp(ytmp[:, 512 * nn + 128 * c:512 * nn + 128 * c + 128],
                         ysum[NS * c:NS * c + NS, 128 * nn:128 * nn + 128])
        dstep(ins)
        tt(x2[0:NS, 2, :], x2[0:NS, 2, :], ytmp, ALU.add).then_inc(sg("x3"), 1)
        dve.wait_ge(sg("gfin_in"), 16)
        for t, (t0, n) in enumerate(TILES):
            dve.wait_ge(sg("rst"), 4 + t)
            stt(x2[0:n, t, :], x2[0:n, t, :], rst[0:n, t:t + 1], gfin[0:n, :], ALU.mult, ALU.mult) \
                .then_inc(sg("y"), 1)

    ctx.close()


_OUTS = [("y_prompt", (1, SEQ, D)), ("y_sample", (NB, DS, D)),
         ("mem_k", (1, 1, MEM, H, DH)), ("mem_v", (1, 1, MEM, H, DH)),
         ("C_p", (1, 1, H, DH, DH)), ("n_p", (1, 1, H, DH)), ("m_p", (1, 1, H)), ("S_p", (1, 1, H, DH, DH)),
         ("conv_p", (1, 1, HIST, CCH)),
         ("C_s", (1, NB, H, DH, DH)), ("n_s", (1, NB, H, DH)), ("m_s", (1, NB, H)), ("S_s", (1, NB, H, DH, DH)),
         ("conv_s", (1, NB, HIST, CCH))]


def kernel(**inputs):
    import concourse.bacc as bacc
    from concourse.bass_utils import run_bass_kernel_spmd

    nc = bacc.Bacc("TRN2", target_bir_lowering=False, num_devices=1)
    arrays, a, out = {}, {}, {}
    for name in inputs:
        x = np.ascontiguousarray(inputs[name])
        arrays[f"in_{name}"] = x
        a[name] = nc.dram_tensor(f"in_{name}", x.shape, mybir.dt.from_np(x.dtype), kind="ExternalInput").ap()
    arrays["in_table"] = constants()
    a["table"] = nc.dram_tensor("in_table", (128, C_ALL), F32, kind="ExternalInput").ap()
    for name, shape in _OUTS:
        out[name] = nc.dram_tensor(f"out_{name}", shape, F32, kind="ExternalOutput").ap()
    build(nc, a, out)
    r = run_bass_kernel_spmd(nc, [arrays], core_ids=[0])
    return tuple(r.results[0][f"out_{name}"] for name, _ in _OUTS)
```
